# Optimizing a Trainium2 kernel written in Bass

```python
import jax, jax.numpy as jnp
from jax import lax
import numpy as np
import math
import jax
import jax.numpy as jnp

D_MODEL = 2048
BATCH = 1
SEQ = 256
DEPTH = 1

D_MIX = D_MODEL
D_A = D_MIX // 4
D_B = D_MIX // 4
D_C = D_MIX // 4
D_D = D_MIX // 4
GDN_HEAD_DIM = 128
GDN_HEADS = D_A // GDN_HEAD_DIM
GDN_CONV = 4
GDN_CHUNK = 64
GDN_CHUNK_LOG2 = 6
LRU_BLOCKS = 8
LRU_BLOCK_DIM = D_B // LRU_BLOCKS
LRU_CONV = 4
LRU_C = 8.0
SGU_GROUPS = 4
SGU_GROUP_DIM = D_C // SGU_GROUPS
SGU_CHUNK = 128
SCONV_WIDTH = 3
D_FF = (D_MODEL * 11) // 4
FFN_CONV = 3
IN_SIZES = (D_A, D_A, D_A, D_A, GDN_HEADS, GDN_HEADS, D_B, D_B, 2 * D_C, D_D, D_D, D_D)
N_IN = 4 * D_A + 2 * GDN_HEADS + 2 * D_B + 2 * D_C + 3 * D_D
EPS = 1e-6


def _split(t, sizes):
    idx, acc = [], 0
    for s in sizes[:-1]:
        acc += s
        idx.append(acc)
    return jnp.split(t, idx, axis=-1)

def rms_norm(x, w):
    xf = x.astype(jnp.float32)
    y = xf * lax.rsqrt(jnp.mean(xf * xf, axis=-1, keepdims=True) + EPS)
    return (y * w.astype(jnp.float32)).astype(x.dtype)

def layer_norm(x, w, b):
    xf = x.astype(jnp.float32)
    mu = jnp.mean(xf, axis=-1, keepdims=True)
    xc = xf - mu
    y = xc * lax.rsqrt(jnp.mean(xc * xc, axis=-1, keepdims=True) + EPS)
    return y * w.astype(jnp.float32) + b.astype(jnp.float32)

def causal_dwconv(x, w, b=None):
    K, C = w.shape
    y = lax.conv_general_dilated(x, w[:, None, :].astype(x.dtype), window_strides=(1,),
                                 padding=[(K - 1, 0)], dimension_numbers=('NWC', 'WIO', 'NWC'),
                                 feature_group_count=C)
    if b is not None:
        y = y + b.astype(x.dtype)
    return y

def l2norm(t):
    return t * lax.rsqrt(jnp.sum(t * t, axis=-1, keepdims=True) + EPS)

def chunk_gated_delta_rule(q, k, v, g, beta):
    Bn, S, H, Dk = q.shape
    Dv = v.shape[-1]
    nC = S // GDN_CHUNK
    C = GDN_CHUNK
    q = l2norm(q) * (Dk ** -0.5)
    k = l2norm(k)

    def chunks(t):
        return t.reshape(Bn, nC, C, H, -1).transpose(0, 3, 1, 2, 4)

    qc, kc, vc = chunks(q), chunks(k), chunks(v)
    gc = g.reshape(Bn, nC, C, H).transpose(0, 3, 1, 2)
    bc = beta.reshape(Bn, nC, C, H).transpose(0, 3, 1, 2)
    gcum = jnp.cumsum(gc, axis=-1)
    causal = jnp.tril(jnp.ones((C, C), dtype=bool))
    strict = jnp.tril(jnp.ones((C, C), dtype=bool), -1)
    diff = gcum[..., :, None] - gcum[..., None, :]
    decay = jnp.where(causal, jnp.exp(jnp.where(causal, diff, 0.0)), 0.0)
    kb = kc * bc[..., None]
    M = jnp.where(strict, jnp.einsum('bhncd,bhnsd->bhncs', kb, kc) * decay, 0.0)
    N = -M
    T = jnp.eye(C, dtype=jnp.float32) + N
    P = N
    for _ in range(GDN_CHUNK_LOG2 - 1):
        P = jnp.einsum('bhnij,bhnjk->bhnik', P, P)
        T = T + jnp.einsum('bhnij,bhnjk->bhnik', T, P)
    w = jnp.einsum('bhncs,bhnsd->bhncd', T, kb * jnp.exp(gcum)[..., None])
    u = jnp.einsum('bhncs,bhnsd->bhncd', T, vc * bc[..., None])
    attn = jnp.where(causal, jnp.einsum('bhncd,bhnsd->bhncs', qc, kc) * decay, 0.0)
    q_g = qc * jnp.exp(gcum)[..., None]
    k_g = kc * jnp.exp(gcum[..., -1:] - gcum)[..., None]
    g_last = jnp.exp(gcum[..., -1])

    def step(state, inp):
        q_i, a_i, u_i, w_i, k_i, gl_i = inp
        v_new = u_i - jnp.einsum('bhck,bhkv->bhcv', w_i, state)
        o_i = jnp.einsum('bhck,bhkv->bhcv', q_i, state) + jnp.einsum('bhcs,bhsv->bhcv', a_i, v_new)
        state = state * gl_i[..., None, None] + jnp.einsum('bhck,bhcv->bhkv', k_i, v_new)
        return state, o_i

    xs = tuple(jnp.moveaxis(t, 2, 0) for t in (q_g, attn, u, w, k_g, g_last))
    s0 = jnp.zeros((Bn, H, Dk, Dv), jnp.float32)
    _, o = lax.scan(step, s0, xs)
    return o.transpose(1, 0, 3, 2, 4).reshape(Bn, S, H, Dv)

def gdn_mixer(q, k, v, z, b, a, conv_w, a_log, dt_bias, norm_w):
    Bn, S, _ = q.shape
    qkv = jax.nn.silu(causal_dwconv(jnp.concatenate([q, k, v], axis=-1), conv_w))
    q, k, v = jnp.split(qkv, 3, axis=-1)

    def heads(t):
        return t.reshape(Bn, S, GDN_HEADS, GDN_HEAD_DIM).astype(jnp.float32)

    beta = jax.nn.sigmoid(b.astype(jnp.float32))
    g = -jnp.exp(a_log.astype(jnp.float32)) * jax.nn.softplus(a.astype(jnp.float32) + dt_bias.astype(jnp.float32))
    o = chunk_gated_delta_rule(heads(q), heads(k), heads(v), g, beta)
    o = o * lax.rsqrt(jnp.mean(o * o, axis=-1, keepdims=True) + EPS) * norm_w.astype(jnp.float32) * jax.nn.silu(heads(z))
    return o.reshape(Bn, S, D_A).astype(z.dtype)

def lru_scan(a, b):
    def combine(l, r):
        return (l[0] * r[0], r[0] * l[1] + r[1])
    _, h = lax.associative_scan(combine, (a, b), axis=1)
    return h

def rglru_mixer(xb, gate, conv_w, conv_b, wa, ba, wx, bx, lam):
    Bn, S, _ = xb.shape
    xc = causal_dwconv(xb, conv_w, conv_b).astype(jnp.float32)
    xblk = xc.reshape(Bn, S, LRU_BLOCKS, LRU_BLOCK_DIM)
    r = jax.nn.sigmoid(jnp.einsum('bshi,hij->bshj', xblk, wa.astype(jnp.float32)) + ba.astype(jnp.float32)).reshape(Bn, S, D_B)
    i = jax.nn.sigmoid(jnp.einsum('bshi,hij->bshj', xblk, wx.astype(jnp.float32)) + bx.astype(jnp.float32)).reshape(Bn, S, D_B)
    log_a = -LRU_C * r * jax.nn.softplus(-lam.astype(jnp.float32))
    a = jnp.exp(log_a)
    mult = jnp.sqrt(-jnp.expm1(2.0 * log_a))
    h = lru_scan(a, mult * (i * xc))
    return (h * jax.nn.gelu(gate.astype(jnp.float32))).astype(xb.dtype)

def sgu_mixer(uv, ln_w, ln_b, ws, bs):
    Bn, S, _ = uv.shape
    uvf = jax.nn.gelu(uv.astype(jnp.float32))
    u, v = jnp.split(uvf, 2, axis=-1)
    v = layer_norm(v, ln_w, ln_b)
    v = v.reshape(Bn, S // SGU_CHUNK, SGU_CHUNK, SGU_GROUPS, SGU_GROUP_DIM)
    mask = jnp.tril(jnp.ones((SGU_CHUNK, SGU_CHUNK), dtype=bool))
    wsm = jnp.where(mask, ws.astype(jnp.float32), 0.0)
    v = jnp.einsum('gts,bnsgd->bntgd', wsm, v) + bs.astype(jnp.float32).T[:, :, None]
    return (u * v.reshape(Bn, S, D_C)).astype(uv.dtype)

def short_conv_mixer(bg, cg, hh, conv_w):
    return bg * causal_dwconv(cg * hh, conv_w)

def conv_ffn(h, up, conv_w, conv_b, down):
    hid = causal_dwconv(h @ up.astype(h.dtype), conv_w, conv_b)
    gate, val = jnp.split(hid, 2, axis=-1)
    return (jax.nn.gelu(gate) * val) @ down.astype(h.dtype)

def first_inputs(seed: int = 0) -> dict:
    key = jax.random.key(seed)
    ks = iter(jax.random.split(key, 48))
    L = DEPTH
    f32 = jnp.float32

    def nrm(shape, scale):
        return jax.random.normal(next(ks), shape, f32) * scale

    def gain(shape):
        return 1.0 + 0.1 * jax.random.normal(next(ks), shape, f32)

    def unif(shape, lo, hi):
        return jax.random.uniform(next(ks), shape, f32, lo, hi)

    s = unif((L, D_B), 0.9, 0.999) ** (1.0 / LRU_C)
    lru_lambda = jnp.log(s) - jnp.log1p(-s)
    dt = jnp.exp(unif((L, GDN_HEADS), float(np.log(1e-3)), float(np.log(1e-1))))
    gdn_dt_bias = dt + jnp.log(-jnp.expm1(-dt))
    return {
        "x": nrm((BATCH, SEQ, D_MODEL), 1.0),
        "pre_mix_norm": gain((L, D_MODEL)),
        "w_in": nrm((L, D_MODEL, N_IN), D_MODEL ** -0.5),
        "gdn_conv_w": nrm((L, GDN_CONV, 3 * D_A), GDN_CONV ** -0.5),
        "gdn_a_log": jnp.log(unif((L, GDN_HEADS), 1.0, 16.0)),
        "gdn_dt_bias": gdn_dt_bias,
        "gdn_norm_w": gain((L, GDN_HEAD_DIM)),
        "lru_conv_w": nrm((L, LRU_CONV, D_B), LRU_CONV ** -0.5),
        "lru_conv_b": nrm((L, D_B), 0.01),
        "lru_wa": nrm((L, LRU_BLOCKS, LRU_BLOCK_DIM, LRU_BLOCK_DIM), LRU_BLOCK_DIM ** -0.5),
        "lru_ba": nrm((L, LRU_BLOCKS, LRU_BLOCK_DIM), 0.01),
        "lru_wx": nrm((L, LRU_BLOCKS, LRU_BLOCK_DIM, LRU_BLOCK_DIM), LRU_BLOCK_DIM ** -0.5),
        "lru_bx": nrm((L, LRU_BLOCKS, LRU_BLOCK_DIM), 0.01),
        "lru_lambda": lru_lambda,
        "sgu_ln_w": gain((L, D_C)),
        "sgu_ln_b": nrm((L, D_C), 0.01),
        "sgu_ws": nrm((L, SGU_GROUPS, SGU_CHUNK, SGU_CHUNK), SGU_CHUNK ** -0.5),
        "sgu_b": gain((L, SGU_GROUPS, SGU_CHUNK)),
        "sconv_w": nrm((L, SCONV_WIDTH, D_D), SCONV_WIDTH ** -0.5),
        "grp_norm_w": gain((L, 3, D_B)),
        "w_out": nrm((L, D_MIX, D_MODEL), D_MIX ** -0.5),
        "post_mix_norm": gain((L, D_MODEL)),
        "pre_ffn_norm": gain((L, D_MODEL)),
        "ffn_up": nrm((L, D_MODEL, 2 * D_FF), D_MODEL ** -0.5),
        "ffn_conv_w": nrm((L, FFN_CONV, 2 * D_FF), FFN_CONV ** -0.5),
        "ffn_conv_b": nrm((L, 2 * D_FF), 0.01),
        "ffn_down": nrm((L, D_FF, D_MODEL), D_FF ** -0.5),
        "post_ffn_norm": gain((L, D_MODEL)),
    }

def first_block(x, pre_mix_norm, w_in, gdn_conv_w, gdn_a_log, gdn_dt_bias, gdn_norm_w,
              lru_conv_w, lru_conv_b, lru_wa, lru_ba, lru_wx, lru_bx, lru_lambda,
              sgu_ln_w, sgu_ln_b, sgu_ws, sgu_b, sconv_w, grp_norm_w, w_out,
              post_mix_norm, pre_ffn_norm, ffn_up, ffn_conv_w, ffn_conv_b, ffn_down,
              post_ffn_norm):
    for l in range(DEPTH):
        h = rms_norm(x, pre_mix_norm[l])
        p = h @ w_in[l].astype(h.dtype)
        (q, k, v, z, b_gdn, a_gdn, lru_x, lru_gate, sgu_uv, sc_b, sc_c, sc_h) = _split(p, IN_SIZES)
        y_a = gdn_mixer(q, k, v, z, b_gdn, a_gdn, gdn_conv_w[l], gdn_a_log[l], gdn_dt_bias[l], gdn_norm_w[l])
        y_b = rms_norm(rglru_mixer(lru_x, lru_gate, lru_conv_w[l], lru_conv_b[l], lru_wa[l], lru_ba[l],
                                   lru_wx[l], lru_bx[l], lru_lambda[l]), grp_norm_w[l, 0])
        y_c = rms_norm(sgu_mixer(sgu_uv, sgu_ln_w[l], sgu_ln_b[l], sgu_ws[l], sgu_b[l]), grp_norm_w[l, 1])
        y_d = rms_norm(short_conv_mixer(sc_b, sc_c, sc_h, sconv_w[l]), grp_norm_w[l, 2])
        y = jnp.concatenate([y_a, y_b, y_c, y_d], axis=-1) @ w_out[l].astype(h.dtype)
        x = x + rms_norm(y, post_mix_norm[l])
        h = rms_norm(x, pre_ffn_norm[l])
        y = conv_ffn(h, ffn_up[l], ffn_conv_w[l], ffn_conv_b[l], ffn_down[l])
        x = x + rms_norm(y, post_ffn_norm[l])
    return x


HEAD_DIM = 128
ROPE_DIM = HEAD_DIM // 4
ROPE_THETA = 500000.0
BLK = 128
RMS_EPS = 1e-6
DIL_GROUPS = ((128, 1), (512, 4), (2048, 16))
N_DIL_GROUPS = len(DIL_GROUPS)
DIL_HEADS = 4
DIL_WIDTH = N_DIL_GROUPS * DIL_HEADS * HEAD_DIM
DIL_OUT = DIL_HEADS * HEAD_DIM
DIFF_HEADS = 4
DIFF_QK = DIFF_HEADS * 2 * HEAD_DIM
DIFF_OUT = DIFF_HEADS * 2 * HEAD_DIM
IN_SPLITS = (DIL_WIDTH, DIL_WIDTH, DIL_WIDTH, DIFF_QK, DIFF_QK, DIFF_OUT, D_MODEL, D_MODEL)
D_IN = sum(IN_SPLITS)
D_FF_2 = 5632


def rms_norm_2(x, g):
    xf = x.astype(jnp.float32)
    y = xf * lax.rsqrt(jnp.mean(xf * xf, axis=-1, keepdims=True) + RMS_EPS)
    return (y * g.astype(jnp.float32)).astype(x.dtype)

def rope_tables(positions):
    inv = ROPE_THETA ** (-jnp.arange(0, ROPE_DIM, 2, dtype=jnp.float32) / ROPE_DIM)
    ang = positions.astype(jnp.float32)[..., None] * inv
    return jnp.cos(ang), jnp.sin(ang)

def apply_rope(x, cos, sin):
    shape = cos.shape[:2] + (1,) * (x.ndim - 3) + (cos.shape[-1],)
    c = cos.reshape(shape)
    s = sin.reshape(shape)
    half = ROPE_DIM // 2
    xr = x[..., :ROPE_DIM].astype(jnp.float32)
    x1, x2 = xr[..., :half], xr[..., half:]
    rot = jnp.concatenate([x1 * c - x2 * s, x2 * c + x1 * s], axis=-1)
    return jnp.concatenate([rot.astype(x.dtype), x[..., ROPE_DIM:]], axis=-1)

def swiglu(h, w_gate, w_up, w_down):
    return (jax.nn.silu(h @ w_gate) * (h @ w_up)) @ w_down

def lambda_init(layer):
    return 0.8 - 0.6 * math.exp(-0.3 * layer)

def dilated_group(q, k, v, window, dilation):
    B, S, H, D = q.shape
    band = window // dilation
    L = S // dilation
    pad = (-L) % BLK
    nb = (L + pad) // BLK

    def strided(t):
        return t.reshape(B, L, dilation, H, D).transpose(0, 2, 1, 3, 4)

    qb = jnp.pad(strided(q), ((0, 0), (0, 0), (0, pad), (0, 0), (0, 0))).reshape(B, dilation, nb, BLK, H, D)

    def band_blocks(t):
        t = jnp.pad(strided(t), ((0, 0), (0, 0), (BLK, pad), (0, 0), (0, 0)))
        t = t.reshape(B, dilation, nb + 1, BLK, H, D)
        return jnp.concatenate([t[:, :, :-1], t[:, :, 1:]], axis=3)

    kb = band_blocks(k)
    vb = band_blocks(v)
    s = jnp.einsum('brnqhd,brnkhd->brnhqk', qb, kb).astype(jnp.float32) * (D ** -0.5)
    qi = jnp.arange(BLK)[:, None]
    kj = jnp.arange(2 * BLK)[None, :]
    dist = qi - kj + BLK
    kpos = jnp.arange(nb)[:, None, None] * BLK + kj[None] - BLK
    valid = (dist >= 0) & (dist <= band) & (kpos >= 0)
    s = jnp.where(valid[None, None, :, None], s, -jnp.inf)
    m = jnp.max(s, axis=-1, keepdims=True)
    p = jnp.exp(s - m)
    den = jnp.sum(p, axis=-1, keepdims=True)
    o = jnp.einsum('brnhqk,brnkhd->brnqhd', (p / den).astype(v.dtype), vb)
    lse = (m + jnp.log(den))[..., 0]
    o = o.reshape(B, dilation, nb * BLK, H, D)[:, :, :L].transpose(0, 2, 1, 3, 4).reshape(B, S, H, D)
    lse = lse.transpose(0, 1, 2, 4, 3).reshape(B, dilation, nb * BLK, H)[:, :, :L]
    lse = lse.transpose(0, 2, 1, 3).reshape(B, S, H)
    return o, lse

def diff_attention(q, k, v, lam):
    B, S, H, _, D = q.shape
    nb = S // BLK
    qb = q.reshape(B, nb, BLK, H, 2, D).transpose(1, 0, 2, 3, 4, 5)
    kpos = jnp.arange(S)

    def block(args):
        qblk, i = args
        s = jnp.einsum('bqhcd,bkhcd->bhcqk', qblk, k).astype(jnp.float32) * (D ** -0.5)
        qpos = i * BLK + jnp.arange(BLK)
        s = jnp.where(kpos[None, :] <= qpos[:, None], s, -jnp.inf)
        p = jax.nn.softmax(s, axis=-1)
        a = p[:, :, 0] - lam * p[:, :, 1]
        return jnp.einsum('bhqk,bkhe->bqhe', a.astype(v.dtype), v)

    o = lax.map(block, (qb, jnp.arange(nb)))
    return o.transpose(1, 0, 2, 3, 4).reshape(B, S, H, 2 * D)

def hybrid_layer(x, cos, sin, layer, ffn1_norm, ffn1_w_gate, ffn1_w_up, ffn1_w_down, mix_norm, w_in,
                 dil_q_norm, dil_k_norm, diff_q_norm, diff_k_norm, diff_lq1, diff_lk1, diff_lq2, diff_lk2,
                 diff_subln, w_dil_branch, w_diff_branch, w_out, ffn2_norm, ffn2_w_gate, ffn2_w_up, ffn2_w_down):
    B, S, _ = x.shape
    x = x + 0.5 * swiglu(rms_norm_2(x, ffn1_norm), ffn1_w_gate, ffn1_w_up, ffn1_w_down)

    h = rms_norm_2(x, mix_norm)
    proj = h @ w_in
    idx = np.cumsum(IN_SPLITS)[:-1].tolist()
    dq, dk, dv, fq, fk, fv, g_dil, g_diff = jnp.split(proj, idx, axis=-1)

    gshape = (B, S, N_DIL_GROUPS, DIL_HEADS, HEAD_DIM)
    dq = apply_rope(rms_norm_2(dq.reshape(gshape), dil_q_norm), cos, sin)
    dk = apply_rope(rms_norm_2(dk.reshape(gshape), dil_k_norm), cos, sin)
    dv = dv.reshape(gshape)
    outs = []
    lses = []
    for g, (window, dilation) in enumerate(DIL_GROUPS):
        o_g, lse_g = dilated_group(dq[:, :, g], dk[:, :, g], dv[:, :, g], window, dilation)
        outs.append(o_g)
        lses.append(lse_g)
    mix_w = jax.nn.softmax(jnp.stack(lses, axis=0), axis=0).astype(x.dtype)
    o_dil = jnp.einsum('gbsh,gbshd->bshd', mix_w, jnp.stack(outs, axis=0)).reshape(B, S, DIL_OUT)

    fshape = (B, S, DIFF_HEADS, 2, HEAD_DIM)
    fq = apply_rope(rms_norm_2(fq.reshape(fshape), diff_q_norm), cos, sin)
    fk = apply_rope(rms_norm_2(fk.reshape(fshape), diff_k_norm), cos, sin)
    fv = fv.reshape(B, S, DIFF_HEADS, 2 * HEAD_DIM)
    lam_init = lambda_init(layer)
    lam = (jnp.exp(jnp.sum(diff_lq1.astype(jnp.float32) * diff_lk1.astype(jnp.float32)))
           - jnp.exp(jnp.sum(diff_lq2.astype(jnp.float32) * diff_lk2.astype(jnp.float32))) + lam_init)
    o_diff = diff_attention(fq, fk, fv, lam)
    o_diff = (rms_norm_2(o_diff, diff_subln) * (1.0 - lam_init)).reshape(B, S, DIFF_OUT)

    y = jax.nn.sigmoid(g_dil) * (o_dil @ w_dil_branch) + jax.nn.sigmoid(g_diff) * (o_diff @ w_diff_branch)
    x = x + y @ w_out

    x = x + 0.5 * swiglu(rms_norm_2(x, ffn2_norm), ffn2_w_gate, ffn2_w_up, ffn2_w_down)
    return x

def second_inputs(seed: int = 0) -> dict:
    key = jax.random.key(seed)
    ks = jax.random.split(key, 32)
    f32 = jnp.float32

    def dense(k, fan_in, fan_out):
        return jax.random.normal(k, (DEPTH, fan_in, fan_out), f32) * fan_in ** -0.5

    def gain(k, n):
        return 1.0 + 0.02 * jax.random.normal(k, (DEPTH, n), f32)

    def small(k, n):
        return 0.1 * jax.random.normal(k, (DEPTH, n), f32)

    x = jax.random.normal(ks[0], (BATCH, SEQ, D_MODEL), f32)
    positions = (jnp.arange(SEQ, dtype=jnp.int32)[None, :]
                 + jax.random.randint(ks[1], (BATCH, 1), 0, 1024, dtype=jnp.int32))
    return {
        'x': x,
        'positions': positions,
        'ffn1_norm': gain(ks[2], D_MODEL),
        'ffn1_w_gate': dense(ks[3], D_MODEL, D_FF_2),
        'ffn1_w_up': dense(ks[4], D_MODEL, D_FF_2),
        'ffn1_w_down': dense(ks[5], D_FF_2, D_MODEL),
        'mix_norm': gain(ks[6], D_MODEL),
        'w_in': dense(ks[7], D_MODEL, D_IN),
        'dil_q_norm': gain(ks[8], HEAD_DIM),
        'dil_k_norm': gain(ks[9], HEAD_DIM),
        'diff_q_norm': gain(ks[10], HEAD_DIM),
        'diff_k_norm': gain(ks[11], HEAD_DIM),
        'diff_lq1': small(ks[12], HEAD_DIM),
        'diff_lk1': small(ks[13], HEAD_DIM),
        'diff_lq2': small(ks[14], HEAD_DIM),
        'diff_lk2': small(ks[15], HEAD_DIM),
        'diff_subln': gain(ks[16], 2 * HEAD_DIM),
        'w_dil_branch': dense(ks[17], DIL_OUT, D_MODEL),
        'w_diff_branch': dense(ks[18], DIFF_OUT, D_MODEL),
        'w_out': dense(ks[19], D_MODEL, D_MODEL),
        'ffn2_norm': gain(ks[20], D_MODEL),
        'ffn2_w_gate': dense(ks[21], D_MODEL, D_FF_2),
        'ffn2_w_up': dense(ks[22], D_MODEL, D_FF_2),
        'ffn2_w_down': dense(ks[23], D_FF_2, D_MODEL),
    }

def second_block(x, positions, ffn1_norm, ffn1_w_gate, ffn1_w_up, ffn1_w_down, mix_norm, w_in,
              dil_q_norm, dil_k_norm, diff_q_norm, diff_k_norm, diff_lq1, diff_lk1, diff_lq2, diff_lk2,
              diff_subln, w_dil_branch, w_diff_branch, w_out, ffn2_norm, ffn2_w_gate, ffn2_w_up, ffn2_w_down):
    cos, sin = rope_tables(positions)
    for l in range(DEPTH):
        x = hybrid_layer(x, cos, sin, l, ffn1_norm[l], ffn1_w_gate[l], ffn1_w_up[l], ffn1_w_down[l],
                         mix_norm[l], w_in[l], dil_q_norm[l], dil_k_norm[l], diff_q_norm[l], diff_k_norm[l],
                         diff_lq1[l], diff_lk1[l], diff_lq2[l], diff_lk2[l], diff_subln[l],
                         w_dil_branch[l], w_diff_branch[l], w_out[l], ffn2_norm[l], ffn2_w_gate[l],
                         ffn2_w_up[l], ffn2_w_down[l])
    return x


def setup_inputs(seed=0):
    out = dict(first_inputs(seed))
    for name, value in second_inputs(seed + 1).items():
        if name != "x":
            out[name + "_2"] = value
    return out


def reference(
    x, pre_mix_norm, w_in, gdn_conv_w, gdn_a_log, gdn_dt_bias, gdn_norm_w, lru_conv_w,
    lru_conv_b, lru_wa, lru_ba, lru_wx, lru_bx, lru_lambda, sgu_ln_w, sgu_ln_b, sgu_ws, sgu_b,
    sconv_w, grp_norm_w, w_out, post_mix_norm, pre_ffn_norm, ffn_up, ffn_conv_w, ffn_conv_b,
    ffn_down, post_ffn_norm, positions_2, ffn1_norm_2, ffn1_w_gate_2, ffn1_w_up_2,
    ffn1_w_down_2, mix_norm_2, w_in_2, dil_q_norm_2, dil_k_norm_2, diff_q_norm_2, diff_k_norm_2,
    diff_lq1_2, diff_lk1_2, diff_lq2_2, diff_lk2_2, diff_subln_2, w_dil_branch_2,
    w_diff_branch_2, w_out_2, ffn2_norm_2, ffn2_w_gate_2, ffn2_w_up_2, ffn2_w_down_2,
):
    x = first_block(
        x, pre_mix_norm, w_in, gdn_conv_w, gdn_a_log, gdn_dt_bias, gdn_norm_w, lru_conv_w,
        lru_conv_b, lru_wa, lru_ba, lru_wx, lru_bx, lru_lambda, sgu_ln_w, sgu_ln_b, sgu_ws,
        sgu_b, sconv_w, grp_norm_w, w_out, post_mix_norm, pre_ffn_norm, ffn_up, ffn_conv_w,
        ffn_conv_b, ffn_down, post_ffn_norm,
    )
    return second_block(
        x, positions_2, ffn1_norm_2, ffn1_w_gate_2, ffn1_w_up_2, ffn1_w_down_2, mix_norm_2,
        w_in_2, dil_q_norm_2, dil_k_norm_2, diff_q_norm_2, diff_k_norm_2, diff_lq1_2,
        diff_lk1_2, diff_lq2_2, diff_lk2_2, diff_subln_2, w_dil_branch_2, w_diff_branch_2,
        w_out_2, ffn2_norm_2, ffn2_w_gate_2, ffn2_w_up_2, ffn2_w_down_2,
    )


_drawn_inputs = setup_inputs


def setup_inputs(seed=0):
    import zlib

    import numpy as np

    out = dict(_drawn_inputs(seed))
    spreads = {}
    factors = {'lru_ba': 8.0,
     'lru_bx': 8.0,
     'sgu_ln_b': 8.0,
     'ffn_conv_b': 6.243,
     'ffn1_norm_2': 8.0,
     'mix_norm_2': 7.817,
     'dil_q_norm_2': 8.0,
     'dil_k_norm_2': 8.0,
     'diff_q_norm_2': 8.0,
     'diff_k_norm_2': 8.0,
     'diff_lk1_2': 8.0,
     'diff_lk2_2': 3.39,
     'diff_subln_2': 8.0,
     'ffn2_norm_2': 8.0}
    for name, (base, spread) in spreads.items():
        noise = np.random.default_rng([zlib.crc32(name.encode()), seed]).standard_normal(out[name].shape)
        drawn = base * np.exp(spread * noise) if base else spread * noise
        out[name] = jnp.asarray(drawn.astype(out[name].dtype))
    for name, factor in factors.items():
        out[name] = (out[name] * factor).astype(out[name].dtype)
    return out
```

```python
from contextlib import ExitStack

import numpy as np

import concourse.bass as bass
from concourse import mybir

F32 = mybir.dt.float32
F32R = mybir.dt.float32r
I32 = mybir.dt.int32
ALU = mybir.AluOpType
ACT = mybir.ActivationFunctionType
AX = mybir.AxisListType.X

P = 128
S = 256
DM = 2048
KT = DM // P
EPS = 1e-6
KG = 8
SLOTS = 4
HEADS = 4
FF_TILES = 5632 // P
PAD = 4
HALVES = S // P

VECTORS = {}
_at = 0
for _name, _n in (("pre_mix", 16), ("post_mix", 16), ("pre_ffn", 16), ("post_ffn", 16), ("ffn1_norm", 16),
                  ("mix_norm", 16), ("ffn2_norm", 16), ("gdn_conv", 48), ("gdn_norm", 1), ("lru_conv", 16),
                  ("lru_conv_b", 4), ("lru_ba", 4), ("lru_bx", 4), ("lru_lambda", 4), ("ln_w", 4), ("ln_b", 4),
                  ("sconv", 12), ("grp", 12), ("ffn_conv", 264), ("ffn_conv_b", 88), ("dil_q", 1), ("dil_k", 1),
                  ("diff_q", 1), ("diff_k", 1), ("lam", 4), ("subln", 2)):
    VECTORS[_name] = (_at, _n)
    _at += _n
N_VECTORS = _at

CONSTS = {}
_at = 0
for _name, _n in (("ident", 128), ("ones", 128), ("causal64", 128), ("block64", 128), ("neg_strict64", 128),
                  ("causal128", 128), ("inv_freq", 1), ("rope_sign", 1)):
    CONSTS[_name] = (_at, _n)
    _at += _n
N_CONSTS = _at


class Chain:

    def __init__(self, eng, sem):
        self.eng, self.sem, self.n = eng, sem, 0

    def add(self, ins):
        ins.then_inc(self.sem, 1)
        self.n += 1

    def settle(self):
        self.eng.wait_ge(self.sem, self.n)

    def do(self, ins):
        self.add(ins)
        self.settle()


class Product:

    def __init__(self, bodies, tiles, source, moving):
        self.bodies, self.tiles, self.source, self.moving = bodies, tiles, source, moving
        self.chunks = [(t, k0, min(KG, nk - k0)) for t, nk in enumerate(tiles) for k0 in range(0, nk, KG)]
        self.per_body = len(self.chunks)
        assert self.per_body % SLOTS == 0 and len(tiles) % 2 == 0

    def of_tile(self, t):
        return [(u, c) for u, c in enumerate(self.chunks) if c[0] == t]


class Core:

    def __init__(self, nc, ctx, d):
        self.nc, self.ctx, self.d = nc, ctx, d
        self.x = self.sb("x_T", [P, KT, S], F32)
        self.raw = self.sb("weights_raw", [P, SLOTS, KG * P], F32)
        self.high = self.sb("weights_high", [P, SLOTS, KG, P], F32R)
        self.low = self.sb("weights_low", [P, SLOTS, KG, P], F32R)
        self.cross = self.sb("cross_products", [P, 2, S], F32)
        self.vec = self.sb("vectors", [P, N_VECTORS], F32)
        self.const = self.sb("constants", [P, N_CONSTS], F32)
        self.eps = self.sb("eps", [P, 1], F32)
        self.loaded = [self.sem(f"weights_loaded{s}") for s in range(SLOTS)]
        self.high_ready = self.sem("high_ready")
        self.low_ready = self.sem("low_ready")
        self.slots_free = self.sem("slots_free")
        self.acc_free = self.sem("acc_free")
        self.cross_ready = self.sem("cross_ready")
        names = ("squared", "summed", "rooted", "inverted", "scaled", "highs", "lows")
        self.norm_sems = [self.sem(f"norm_{s}") for s in names]
        self.norms = 0
        self.residual_sems = [self.sem(f"residual_{s}") for s in ("squared", "summed", "rooted", "own")]
        self.residuals = 0
        self.swiglu_sems = [self.sem(f"swiglu_{s}") for s in ("activated", "product", "highs")]
        self.swiglus = 0
        self.chunk = 0
        self.tile = 0
        self.stage = 0

    def sb(self, name, shape, dt, ctx=None):
        return (ctx or self.ctx).enter_context(self.nc.sbuf_tensor(name, shape, dt))

    def ps(self, name, shape, ctx, dt=F32):
        return ctx.enter_context(self.nc.psum_tensor(name, shape, dt))

    def sem(self, name):
        return self.ctx.enter_context(self.nc.semaphore(name))

    def v(self, name, j=0, n=1):
        c = VECTORS[name][0] + j
        return self.vec[:, c:c + n]

    def c(self, name):
        c, n = CONSTS[name]
        return self.const[:, c:c + n]



def load_chunk(core, sp, prod, base, i, u):
    t, k0, nk = prod.chunks[u]
    n = i * prod.per_body + (base + u)
    if not (isinstance(n, int) and n < SLOTS):
        sp.wait_ge(core.low_ready, n - (SLOTS - 1))
    sp.dma_start(core.raw[:, u % SLOTS, 0:nk * P], prod.source(i, t, k0, nk)).then_inc(core.loaded[u % SLOTS], 16)


def prefetch(core, sp, prod, base):
    for u in range(SLOTS):
        load_chunk(core, sp, prod, base, 0, u)


def stream(core, sp, prod, following):
    base, per = core.chunk, prod.per_body
    with sp.Fori(0, prod.bodies - 1) as i:
        for u in range(SLOTS, per):
            load_chunk(core, sp, prod, base, i, u)
        for u in range(SLOTS):
            load_chunk(core, sp, prod, base, i + 1, u)
    for u in range(SLOTS, per):
        load_chunk(core, sp, prod, base, prod.bodies - 1, u)
    if following is not None:
        prefetch(core, sp, following, base + prod.bodies * per)


def split_high(core, act, prod, i, t):
    for u, (_, _, nk) in prod.of_tile(t):
        slot = u % SLOTS
        act.wait_ge(core.loaded[slot], i * (16 * prod.per_body // SLOTS) + 16 * ((core.chunk + u) // SLOTS + 1))
        act.wait_ge(core.slots_free, i * prod.per_body + (core.chunk + u + 1))
        core.nc.scalar.activation(core.high[:, slot, 0:nk, :].rearrange("p a b -> p (a b)"),
                                  core.raw[:, slot, 0:nk * P], ACT.Copy).then_inc(core.high_ready, 1)


def split_low(core, dve, prod, i, t):
    for u, (_, _, nk) in prod.of_tile(t):
        slot = u % SLOTS
        dve.wait_ge(core.high_ready, i * prod.per_body + (core.chunk + u + 1))
        core.nc.vector.tensor_tensor(core.low[:, slot, 0:nk, :].rearrange("p a b -> p (a b)"),
                                     core.raw[:, slot, 0:nk * P],
                                     core.high[:, slot, 0:nk, :].rearrange("p a b -> p (a b)").bitcast(F32),
                                     ALU.subtract).then_inc(core.low_ready, 1)


def multiply(core, pe, prod, acc, i, t):
    bank = t % 2
    pe.wait_ge(core.acc_free, i * len(prod.tiles) + (core.tile + t + 1))
    nk_all = prod.tiles[t]
    for u, (_, k0, nk) in prod.of_tile(t):
        pe.wait_ge(core.low_ready, i * prod.per_body + (core.chunk + u + 1))
        for k in range(nk):
            x = prod.moving(t, k0 + k)
            core.nc.tensor.matmul(acc[:, bank, :, :], core.high[:, u % SLOTS, k, :], x,
                                  start=(k0 + k == 0), stop=False)
            last = core.nc.tensor.matmul(acc[:, bank, 0, :], core.low[:, u % SLOTS, k, :], x[:, 0, :],
                                         start=False, stop=(k0 + k == nk_all - 1))
        last.then_inc(core.slots_free, 1)


def multiply_all(core, pe, prod, acc):
    with pe.Fori(0, prod.bodies) as i:
        for t in range(len(prod.tiles)):
            multiply(core, pe, prod, acc, i, t)


def walk(core, eng, prod, split):
    split(core, eng, prod, 0, 0)
    n = len(prod.tiles)
    with eng.Fori(0, prod.bodies - 1) as i:
        for t in range(n):
            split(core, eng, prod, i + (t + 1) // n, (t + 1) % n)
            yield i, t
    for t in range(n):
        if t + 1 < n:
            split(core, eng, prod, prod.bodies - 1, t + 1)
        yield prod.bodies - 1, t


def take_cross(core, act, prod, acc, i, t):
    last = prod.of_tile(t)[-1][0]
    act.wait_ge(core.slots_free, i * prod.per_body + (SLOTS + core.chunk + last + 1))
    core.nc.scalar.activation(core.cross[:, t % 2, :], acc[:, t % 2, 1, :], ACT.Copy).then_inc(core.cross_ready, 1)


def take_tile(core, dve, prod, acc, out, i, t):
    dve.wait_ge(core.cross_ready, i * len(prod.tiles) + (core.tile + t + 1))
    return core.nc.vector.tensor_tensor(out, acc[:, t % 2, 0, :], core.cross[:, t % 2, :],
                                        ALU.add).then_inc(core.acc_free, 1)


def taken(core, eng, prod, i, t):
    eng.wait_ge(core.acc_free, i * len(prod.tiles) + (2 + core.tile + t + 1))


def passed(core, prod):
    core.chunk += prod.bodies * prod.per_body
    core.tile += prod.bodies * len(prod.tiles)



def product_stage(core, prod, out, following):
    nc = core.nc
    with ExitStack() as ctx:
        acc = core.ps(f"acc_{core.chunk}", [P, 2, 2, S], ctx)
        block = ctx.enter_context(nc.Block())

        @block.sync
        def _(sp):
            stream(core, sp, prod, following)

        @block.scalar
        def _(act):
            for i, t in walk(core, act, prod, split_high):
                take_cross(core, act, prod, acc, i, t)

        @block.vector
        def _(dve):
            for i, t in walk(core, dve, prod, split_low):
                take_tile(core, dve, prod, acc, out(i, t), i, t)

        @block.tensor
        def _(pe):
            multiply_all(core, pe, prod, acc)
    passed(core, prod)


def norm_stage(core, parts, gain):
    nc = core.nc
    GROUP = 4
    groups = KT // GROUP
    core.stage += 1
    name = f"norm{core.stage}"
    squared, summed, rooted, inverted, scaled, highs, lows = core.norm_sems
    once, base = core.norms, core.norms * groups
    core.norms += 1
    with ExitStack() as ctx:
        square = core.sb(f"{name}_square", [P, 2, GROUP, S], F32, ctx)
        normed = square
        rms = core.sb(f"{name}_rms", [P, 2, S], F32, ctx)
        total = core.ps(f"{name}_total", [P, 2, S], ctx)
        block = ctx.enter_context(nc.Block())

        @block.scalar
        def _(act):
            for g in range(groups):
                if g >= 2:
                    act.wait_ge(summed, base + g - 1)
                nc.scalar.activation(square[:, g % 2, :, :], core.x[:, g * GROUP:(g + 1) * GROUP, :],
                                     ACT.Square).then_inc(squared, 1)
            act.wait_ge(summed, base + groups)
            nc.scalar.activation(rms[:, 0, :], total[:, 0, :], ACT.Sqrt, scale=1.0 / DM,
                                 bias=core.eps[:, 0:1]).then_inc(rooted, 1)
            for g in range(groups):
                act.wait_ge(scaled, base + g + 1)
                nc.scalar.activation(parts[:, g * GROUP:(g + 1) * GROUP, 0, :], normed[:, g % 2, :, :],
                                     ACT.Copy).then_inc(highs, 1)

        @block.tensor
        def _(pe):
            for g in range(groups):
                pe.wait_ge(squared, base + g + 1)
                for j in range(GROUP):
                    last = nc.tensor.matmul(total[:, 0, :], core.c("ones"), square[:, g % 2, j, :],
                                            start=(g == 0 and j == 0), stop=(g == groups - 1 and j == GROUP - 1))
                last.then_inc(summed, 1)

        @block.vector
        def _(dve):
            dve.wait_ge(rooted, once + 1)
            nc.vector.reciprocal(rms[:, 1, :], rms[:, 0, :]).then_inc(inverted, 1)
            dve.wait_ge(inverted, once + 1)

            def low(g):
                dve.wait_ge(highs, base + g + 1)
                part = parts[:, g * GROUP:(g + 1) * GROUP, :, :]
                nc.vector.tensor_tensor(part[:, :, 1, :], normed[:, g % 2, :, :], part[:, :, 0, :].bitcast(F32),
                                        ALU.subtract).then_inc(lows, 1)

            for g in range(groups):
                for j in range(GROUP):
                    if j == 0 and g >= 2:
                        dve.wait_ge(lows, base + g - 1)
                    k = g * GROUP + j
                    last = nc.vector.scalar_tensor_tensor(normed[:, g % 2, j, :], core.x[:, k, :],
                                                          core.v(gain, k), rms[:, 1, :], ALU.mult, ALU.mult)
                last.then_inc(scaled, 1)
                if g >= 1:
                    low(g - 1)
            low(groups - 1)


def residual_norm_stage(core, y, gain):
    nc = core.nc
    GROUP = 4
    groups = KT // GROUP
    core.stage += 1
    name = f"residual{core.stage}"
    squared, summed, rooted, own = core.residual_sems
    once, base = core.residuals, core.residuals * groups
    core.residuals += 1
    with ExitStack() as ctx:
        square = core.sb(f"{name}_square", [P, 2, GROUP, S], F32, ctx)
        rms = core.sb(f"{name}_rms", [P, 2, S], F32, ctx)
        total = core.ps(f"{name}_total", [P, 2, S], ctx)
        block = ctx.enter_context(nc.Block())

        @block.scalar
        def _(act):
            for g in range(groups):
                if g >= 2:
                    act.wait_ge(summed, base + g - 1)
                nc.scalar.activation(square[:, g % 2, :, :], y[:, g * GROUP:(g + 1) * GROUP, :],
                                     ACT.Square).then_inc(squared, 1)
            act.wait_ge(summed, base + groups)
            nc.scalar.activation(rms[:, 0, :], total[:, 0, :], ACT.Sqrt, scale=1.0 / DM,
                                 bias=core.eps[:, 0:1]).then_inc(rooted, 1)

        @block.tensor
        def _(pe):
            for g in range(groups):
                pe.wait_ge(squared, base + g + 1)
                for j in range(GROUP):
                    last = nc.tensor.matmul(total[:, 0, :], core.c("ones"), square[:, g % 2, j, :],
                                            start=(g == 0 and j == 0), stop=(g == groups - 1 and j == GROUP - 1))
                last.then_inc(summed, 1)

        @block.vector
        def _(dve):
            chain = Chain(dve, own)
            chain.n = once * (KT + 1)
            dve.wait_ge(rooted, once + 1)
            chain.do(nc.vector.reciprocal(rms[:, 1, :], rms[:, 0, :]))
            for k in range(KT):
                chain.add(nc.vector.scalar_tensor_tensor(y[:, k, :], y[:, k, :], core.v(gain, k), rms[:, 1, :],
                                                         ALU.mult, ALU.mult))
                if k % GROUP == GROUP - 1:
                    chain.settle()
                    at = slice(k + 1 - GROUP, k + 1)
                    nc.vector.tensor_tensor(core.x[:, at, :], core.x[:, at, :], y[:, at, :], ALU.add)


def product_add_stage(core, prod, factor, following):
    nc = core.nc
    core.stage += 1
    with ExitStack() as ctx:
        acc = core.ps(f"acc_{core.chunk}", [P, 2, 2, S], ctx)
        y = core.sb(f"branch{core.stage}", [P, 2, S], F32, ctx)
        block = ctx.enter_context(nc.Block())

        @block.sync
        def _(sp):
            stream(core, sp, prod, following)

        @block.scalar
        def _(act):
            for i, t in walk(core, act, prod, split_high):
                take_cross(core, act, prod, acc, i, t)

        @block.vector
        def _(dve):
            for i, t in walk(core, dve, prod, split_low):
                take_tile(core, dve, prod, acc, y[:, t, :], i, t)
                taken(core, dve, prod, i, t)
                x = core.x[:, 2 * i + t, :]
                nc.vector.scalar_tensor_tensor(x, y[:, t, :], factor, x, ALU.mult, ALU.add)

        @block.tensor
        def _(pe):
            multiply_all(core, pe, prod, acc)
    passed(core, prod)


def conv_ffn_up_stage(core, prod, g_parts, following):
    nc = core.nc
    core.stage += 1
    sems = [core.sem(f"up{core.stage}_{s}") for s in ("biased", "conv", "activated", "product", "highs", "own")]
    biased_ready, conv_ready, activated, product_ready, highs, own = sems
    with ExitStack() as ctx:
        acc = core.ps(f"acc_{core.chunk}", [P, 2, 2, S], ctx)
        hidden = core.sb("ffn_hidden", [P, 2, PAD + S], F32, ctx)
        biased = core.sb("ffn_biased", [P, 2, S], F32, ctx)
        conv = core.sb("ffn_conv", [P, 2, 2, S], F32, ctx)
        act_out = core.sb("ffn_gelu", [P, S], F32, ctx)
        g = core.sb("ffn_g", [P, S], F32, ctx)
        block = ctx.enter_context(nc.Block())

        def taps(i, t, j):
            c = VECTORS["ffn_conv"][0]
            at = (i + t * FF_TILES) * 3 + (c + j)
            return core.vec[:, at:at + 1] if isinstance(at, int) else core.vec[:, bass.ds(at, 1)]

        def conv_bias(i, t):
            at = (i + t * FF_TILES) + VECTORS["ffn_conv_b"][0]
            return core.vec[:, at:at + 1] if isinstance(at, int) else core.vec[:, bass.ds(at, 1)]

        @block.sync
        def _(sp):
            stream(core, sp, prod, following)

        @block.scalar
        def _(act):
            nc.scalar.preload_act_table(ACT.Gelu_apprx_tanh)
            for i, t in walk(core, act, prod, split_high):
                take_cross(core, act, prod, acc, i, t)
                taken(core, act, prod, i, t)
                nc.scalar.activation(biased[:, t, :], hidden[:, t, PAD:PAD + S], ACT.Identity,
                                     scale=taps(i, t, 2), bias=conv_bias(i, t)).then_inc(biased_ready, 1)
                if t == 1:
                    act.wait_ge(conv_ready, i * 2 + 1)
                    nc.scalar.activation(act_out[:, :], conv[:, 0, 1, :], ACT.Gelu_apprx_tanh).then_inc(activated, 1)
                    act.wait_ge(product_ready, i + 1)
                    nc.scalar.activation(g_parts[:, i, 0, :], g[:, :], ACT.Copy).then_inc(highs, 1)

        @block.vector
        def _(dve):
            nc.vector.memset(hidden[:, :, 0:PAD], 0.0).then_inc(own, 1)
            dve.wait_ge(own, 1)
            for i, t in walk(core, dve, prod, split_low):
                take_tile(core, dve, prod, acc, hidden[:, t, PAD:PAD + S], i, t)
                dve.wait_ge(biased_ready, i * 2 + (t + 1))
                nc.vector.scalar_tensor_tensor(conv[:, t, 0, :], hidden[:, t, PAD - 1:PAD - 1 + S], taps(i, t, 1),
                                               biased[:, t, :], ALU.mult, ALU.add).then_inc(own, 1)
                dve.wait_ge(own, i * 2 + (t + 2))
                nc.vector.scalar_tensor_tensor(conv[:, t, 1, :], hidden[:, t, PAD - 2:PAD - 2 + S], taps(i, t, 0),
                                               conv[:, t, 0, :], ALU.mult, ALU.add).then_inc(conv_ready, 1)
                if t == 1:
                    dve.wait_ge(activated, i + 1)
                    dve.wait_ge(conv_ready, i * 2 + 2)
                    nc.vector.tensor_tensor(g[:, :], act_out[:, :], conv[:, 1, 1, :], ALU.mult).then_inc(product_ready, 1)
                    dve.wait_ge(highs, i + 1)
                    nc.vector.tensor_tensor(g_parts[:, i, 1, :], g[:, :], g_parts[:, i, 0, :].bitcast(F32),
                                            ALU.subtract)

        @block.tensor
        def _(pe):
            multiply_all(core, pe, prod, acc)
    passed(core, prod)


def swiglu_up_stage(core, prod, g_parts, following):
    nc = core.nc
    core.stage += 1
    activated, product_ready, highs = core.swiglu_sems
    base = core.swiglus * prod.bodies
    core.swiglus += 1
    with ExitStack() as ctx:
        acc = core.ps(f"acc_{core.chunk}", [P, 2, 2, S], ctx)
        hidden = core.sb(f"ffn_hidden{core.stage}", [P, 2, S], F32, ctx)
        act_out = core.sb(f"ffn_silu{core.stage}", [P, S], F32, ctx)
        g = core.sb(f"ffn_g{core.stage}", [P, S], F32, ctx)
        block = ctx.enter_context(nc.Block())

        @block.sync
        def _(sp):
            stream(core, sp, prod, following)

        @block.scalar
        def _(act):
            nc.scalar.preload_act_table(ACT.Silu)
            for i, t in walk(core, act, prod, split_high):
                take_cross(core, act, prod, acc, i, t)
                if t == 0:
                    taken(core, act, prod, i, t)
                    nc.scalar.activation(act_out[:, :], hidden[:, 0, :], ACT.Silu).then_inc(activated, 1)
                else:
                    act.wait_ge(product_ready, i + (base + 1))
                    nc.scalar.activation(g_parts[:, i, 0, :], g[:, :], ACT.Copy).then_inc(highs, 1)

        @block.vector
        def _(dve):
            for i, t in walk(core, dve, prod, split_low):
                take_tile(core, dve, prod, acc, hidden[:, t, :], i, t)
                if t == 1:
                    dve.wait_ge(activated, i + (base + 1))
                    taken(core, dve, prod, i, t)
                    nc.vector.tensor_tensor(g[:, :], act_out[:, :], hidden[:, 1, :], ALU.mult).then_inc(product_ready, 1)
                    dve.wait_ge(highs, i + (base + 1))
                    nc.vector.tensor_tensor(g_parts[:, i, 1, :], g[:, :], g_parts[:, i, 0, :].bitcast(F32),
                                            ALU.subtract)

        @block.tensor
        def _(pe):
            multiply_all(core, pe, prod, acc)
    passed(core, prod)


def start_stage(core, first):
    nc = core.nc
    core.inputs_loaded = core.sem("inputs_loaded")
    with nc.Block() as block:
        @block.sync
        def _(sp):
            sp.dma_start(core.x[:, :, :], core.d["x"]).then_inc(core.inputs_loaded, 16)
            sp.dma_start(core.vec[:, :], core.d["vectors"]).then_inc(core.inputs_loaded, 16)
            sp.dma_start(core.const[:, :], core.d["consts"]).then_inc(core.inputs_loaded, 16)
            prefetch(core, sp, first, 0)
            sp.wait_ge(core.inputs_loaded, 48)

        @block.tensor
        def _(pe):
            pe.sem_inc(core.slots_free, SLOTS)

        @block.vector
        def _(dve):
            nc.vector.memset(core.eps[:, :], EPS)
            dve.sem_inc(core.acc_free, 2)



Q, K_, V, Z, LRU_X, LRU_G, SGU_U, SGU_V, SC_B, SC_C, SC_H = (4 * j for j in range(11))
PROJ_TILES = 44
UNITS = HEADS * HALVES
HD = 128
CHUNK = 64
LRU_C = 8.0


def newton_rsqrt(nc, chain, y, v, t):
    chain.do(nc.vector.tensor_tensor(t, y, y, ALU.mult))
    chain.do(nc.vector.scalar_tensor_tensor(t, t, -0.5, v, ALU.mult, ALU.mult))
    chain.do(nc.vector.scalar_tensor_tensor(y, t, 1.5, y, ALU.add, ALU.mult))


def gdn_prepare_stage(core, proj, parts, mix):
    nc = core.nc
    w_ba_loaded, conv_steps, silu_done, squared, ba_done, summed, rooted, own, gate_in, gate_exp, var_ready = (
        core.sem(f"gdn_{s}") for s in ("w_ba_loaded", "conv_steps", "silu_done", "squared", "ba_done", "summed",
                                       "rooted", "own", "gate_in", "gate_exp", "var_ready"))
    conv, small, rows = mix["conv"], mix["small"], mix["rows"]
    with ExitStack() as ctx:
        w_ba = core.sb("w_ba", [P, KT, 2 * HEADS], F32, ctx)
        sq = core.sb("gdn_sq", [P, 8, S], F32, ctx)
        var = core.sb("gdn_var", [P, 4, S], F32, ctx)
        tmp = core.sb("gdn_tmp", [P, 4, S], F32, ctx)
        sp_in, sp_abs, sp_e, sp_z, sp_w, sp_p = (core.sb(f"softplus_{n}", [P, 12], F32, ctx)
                                                 for n in ("in", "abs", "e", "z", "w", "p"))
        beta_e = core.sb("beta_e", [P, HALVES, HEADS], F32, ctx)
        exp_a = core.sb("exp_a", [P, HEADS], F32, ctx)
        ba = core.ps("ps_ba", [P, HALVES, 2 * HEADS], ctx)
        ssq = core.ps("ps_ssq", [P, 8, S], ctx)
        block = ctx.enter_context(nc.Block())
        GROUP_AT = (Q, K_, V, LRU_X)

        @block.sync
        def _(sp):
            sp.dma_start(w_ba[:, :, :], core.d["w_ba"]).then_inc(w_ba_loaded, 16)
            sp.dma_start(rows[:, 0:HEADS], core.d["a_log"].partition_broadcast(P)).then_inc(w_ba_loaded, 16)
            sp.dma_start(rows[:, HEADS:2 * HEADS], core.d["dt_bias"].partition_broadcast(P)).then_inc(w_ba_loaded, 16)
            sp.dma_start(rows[:, 8:8 + 512], core.d["sgu_b"].partition_broadcast(P)).then_inc(w_ba_loaded, 16)

        @block.tensor
        def _(pe):
            pe.wait_ge(w_ba_loaded, 64)
            for half in range(HALVES):
                at = slice(half * P, (half + 1) * P)
                for k in range(KT):
                    for part in range(2):
                        last = nc.tensor.matmul(ba[:, half, :], parts[:, k, part, at].bitcast(F32), w_ba[:, k, :],
                                                start=(k == 0 and part == 0), stop=(k == KT - 1 and part == 1))
            last.then_inc(ba_done, 1)
            for g in range(2):
                pe.wait_ge(squared, g + 1)
                for j in range(2):
                    at = slice(4 * g + 2 * j, 4 * g + 2 * j + 2)
                    last = nc.tensor.matmul(ssq[:, at, :], core.c("ones"), sq[:, at, :], start=True, stop=True)
                last.then_inc(summed, 1)

        @block.scalar
        def _(act):
            for g in range(3):
                act.wait_ge(conv_steps, 16 * (g + 1))
                at = slice(4 * g, 4 * g + 4)
                nc.scalar.activation(conv[:, at, :], conv[:, at, :], ACT.Silu).then_inc(silu_done, 1)
                if g < 2:
                    act.wait_ge(silu_done, g + 1)
                    nc.scalar.activation(sq[:, at, :], conv[:, at, :], ACT.Square).then_inc(squared, 1)
            act.wait_ge(gate_in, 1)
            nc.scalar.activation(sp_e[:, :], sp_abs[:, :], ACT.Exp, scale=-1.0).then_inc(gate_exp, 1)
            nc.scalar.activation(beta_e[:, :, :], ba[:, :, 0:HEADS], ACT.Exp, scale=-1.0).then_inc(gate_exp, 1)
            nc.scalar.activation(exp_a[:, :], rows[:, 0:HEADS], ACT.Exp).then_inc(gate_exp, 1)
            for g in range(2):
                act.wait_ge(var_ready, g + 1)
                nc.scalar.activation(sq[:, 4 * g:4 * g + 4, :], var[:, :, :], ACT.Abs_reciprocal_sqrt).then_inc(rooted, 1)

        @block.vector
        def _(dve):
            steps = Chain(dve, conv_steps)
            for g in range(4):
                for o in range(4):
                    for j in range(4):
                        src = proj[:, GROUP_AT[g] + j, PAD - o:PAD - o + S]
                        dst = conv[:, 4 * g + j, :]
                        w = core.v("gdn_conv", 4 * (4 * g + j) + 3 - o) if g < 3 else core.v("lru_conv", 4 * j + 3 - o)
                        if o:
                            steps.add(nc.vector.scalar_tensor_tensor(dst, src, w, dst, ALU.mult, ALU.add))
                        elif g < 3:
                            steps.add(nc.vector.tensor_scalar(dst, src, w, None, ALU.mult))
                        else:
                            steps.add(nc.vector.tensor_scalar(dst, src, w, core.v("lru_conv_b", j), ALU.mult, ALU.add))
                    steps.settle()
            chain = Chain(dve, own)
            dve.wait_ge(ba_done, 1)
            chain.add(nc.vector.tensor_tensor(
                sp_in[:, 0:8].rearrange("p (a h) -> p a h", a=HALVES), ba[:, :, HEADS:2 * HEADS],
                rows[:, HEADS:2 * HEADS].unsqueeze(1).to_broadcast([P, HALVES, HEADS]), ALU.add))
            chain.do(nc.vector.tensor_scalar(sp_in[:, 8:12], core.v("lru_lambda", 0, 4), -1.0, None, ALU.mult))
            chain.do(nc.vector.tensor_scalar(sp_z[:, :], sp_in[:, :], -1.0, None, ALU.mult))
            nc.vector.tensor_tensor(sp_abs[:, :], sp_in[:, :], sp_z[:, :], ALU.max).then_inc(gate_in, 1)
            dve.wait_ge(gate_exp, 3)
            chain.do(nc.vector.tensor_scalar(sp_w[:, :], sp_e[:, :], 2.0, None, ALU.add))
            chain.do(nc.vector.reciprocal(sp_w[:, :], sp_w[:, :]))
            chain.do(nc.vector.tensor_tensor(sp_z[:, :], sp_e[:, :], sp_w[:, :], ALU.mult))
            chain.do(nc.vector.tensor_tensor(sp_w[:, :], sp_z[:, :], sp_z[:, :], ALU.mult))
            chain.do(nc.vector.tensor_scalar(sp_p[:, :], sp_w[:, :], 1.0 / 17, None, ALU.mult))
            for d in (15, 13, 11, 9, 7, 5, 3):
                chain.do(nc.vector.scalar_tensor_tensor(sp_p[:, :], sp_p[:, :], 1.0 / d, sp_w[:, :], ALU.add, ALU.mult))
            chain.do(nc.vector.scalar_tensor_tensor(sp_p[:, :], sp_p[:, :], 1.0, sp_z[:, :], ALU.add, ALU.mult))
            chain.do(nc.vector.tensor_scalar(sp_in[:, :], sp_in[:, :], 0.0, None, ALU.max))
            chain.do(nc.vector.scalar_tensor_tensor(sp_in[:, :], sp_p[:, :], 2.0, sp_in[:, :], ALU.mult, ALU.add))
            chain.add(nc.vector.scalar_tensor_tensor(
                small["g"][:, :, :].rearrange("p h a -> p a h"), sp_in[:, 0:8].rearrange("p (a h) -> p a h", a=HALVES),
                -1.0, exp_a[:, :].unsqueeze(1).to_broadcast([P, HALVES, HEADS]), ALU.mult, ALU.mult))
            chain.add(nc.vector.tensor_scalar(small["lru_c"][:, :], sp_in[:, 8:12], -LRU_C, None, ALU.mult))
            chain.do(nc.vector.tensor_scalar(beta_e[:, :, :], beta_e[:, :, :], 1.0, None, ALU.add))
            chain.do(nc.vector.reciprocal(beta_e[:, :, :], beta_e[:, :, :]))
            chain.do(nc.vector.tensor_copy(small["beta"][:, :, :].rearrange("p h a -> p a h"), beta_e[:, :, :]))
            for g in range(2):
                at = slice(4 * g, 4 * g + 4)
                dve.wait_ge(summed, g + 1)
                nc.vector.tensor_scalar(var[:, :, :], ssq[:, at, :], EPS, None, ALU.add).then_inc(var_ready, 1)
                dve.wait_ge(rooted, g + 1)
                newton_rsqrt(nc, chain, sq[:, at, :], var[:, :, :], tmp[:, :, :])
                chain.do(nc.vector.scalar_tensor_tensor(conv[:, at, :], conv[:, at, :], HD ** -0.5 if g == 0 else 1.0,
                                                        sq[:, at, :], ALU.mult, ALU.mult))


def gdn_stage(core, proj, mix):
    nc = core.nc
    (diag, cols_done, cols_out, ecols, rows_done, diff_done, decay_done, masked, kk_done, qk_done, n_ready, nt_back,
     p_ready, pp_done, ppt_done, pt_ready, tt_done, tt_ready, kt_done, vt_done, k_out, v_out, w_done, w_out, u_out,
     ws_done, vn_ready, o_done, st_done, o_out, state_ready, o_sq, o_sum, o_root, z_done, own, kg_out, q_ready, o_var) = (
        core.sem(f"delta_{s}") for s in (
            "diag", "cols_done", "cols_out", "ecols", "rows_done", "diff_done", "decay_done", "masked", "kk_done",
            "qk_done", "n_ready", "nt_back", "p_ready", "pp_done", "ppt_done", "pt_ready", "tt_done", "tt_ready",
            "kt_done", "vt_done", "k_out", "v_out", "w_done", "w_out", "u_out", "ws_done", "vn_ready", "o_done",
            "st_done", "o_out", "state_ready", "o_sq", "o_sum", "o_root", "z_done", "own", "kg_out", "q_ready", "o_var"))
    conv, small = mix["conv"], mix["small"]
    ITER = 5
    G4 = UNITS // 2
    qT = conv[:, 0:4, :].rearrange("p h (a c) -> p (h a) c", a=HALVES)
    kT = conv[:, 4:8, :].rearrange("p h (a c) -> p (h a) c", a=HALVES)
    vT = conv[:, 8:12, :].rearrange("p h (a c) -> p (h a) c", a=HALVES)

    def over_units(ap):
        return ap.unsqueeze(1).to_broadcast([P, UNITS, P])

    with ExitStack() as ctx:
        def mat(name):
            return core.sb(f"delta_{name}_m", [P, UNITS, P], F32, ctx)
        g_diag, b_diag, egrow, decay, attnT, TT = (mat(n) for n in ("gdiag", "bdiag", "egrow", "decay", "attn", "TT"))
        pw = [mat("p0"), mat("p1")]
        pt = [mat("pt0"), mat("pt1")]
        kbg, kg, vb = (mat(n) for n in ("kbg", "kg", "vb"))
        cols = core.sb("delta_cols", [P, 6, UNITS], F32, ctx)
        state = core.sb("delta_state", [P, HEADS, HD], F32, ctx)
        gcol, tot, ecol, kgs, bec, left = (cols[:, j, :] for j in range(6))
        pa, pb, pc, pd = (core.ps(f"delta_ps{n}", [P, UNITS, P], ctx) for n in "abcd")
        wT, u_sb = g_diag, b_diag
        v_new, oT = kbg, decay
        block = ctx.enter_context(nc.Block())
        g8 = small["g"][:, :, :].rearrange("p h a -> p (h a)")
        beta8 = small["beta"][:, :, :].rearrange("p h a -> p (h a)")

        @block.tensor
        def _(pe):
            nc.tensor.matmul(pa[:, 0, 0:UNITS], core.c("causal64"), g8, start=True, stop=True)
            nc.tensor.matmul(pa[:, 0, UNITS:2 * UNITS], core.c("block64"), g8, start=True, stop=True).then_inc(cols_done, 1)
            for n, (out, rhs) in enumerate(((pb, g_diag), (pc, b_diag))):
                pe.wait_ge(diag, n + 1)
                for g in range(2):
                    at = slice(G4 * g, G4 * g + G4)
                    last = nc.tensor.matmul(out[:, at, :], core.c("ones"), rhs[:, at, :], start=True, stop=True)
                last.then_inc(rows_done, 1)
            for u in range(UNITS):
                last = nc.tensor.matmul(pd[:, u, :], kT[:, u, :], kT[:, u, :], start=True, stop=True)
            last.then_inc(kk_done, 1)
            pe.wait_ge(cols_out, 1)
            for u in range(UNITS):
                last = nc.tensor.matmul(pa[:, u, :], kT[:, u, :], qT[:, u, :], start=True, stop=True)
            last.then_inc(qk_done, 1)
            pe.wait_ge(n_ready, 1)
            pe.wait_ge(ecols, 3)
            pe.wait_ge(diff_done, 1)
            for u in range(UNITS):
                last = nc.tensor.transpose(pb[:, u, :], pt[0][:, u, :], core.c("ident"))
            last.then_inc(nt_back, 1)
            pe.wait_ge(p_ready, 2)
            for u in range(UNITS):
                last = nc.tensor.transpose(pb[:, u, :], kT[:, u, :], core.c("ident"))
            last.then_inc(kt_done, 1)
            pe.wait_ge(n_ready, 2)
            for it in range(ITER):
                old = it % 2
                for g in range(2):
                    pe.wait_ge(p_ready, 2 * it + g + 1)
                    if it:
                        pe.wait_ge(pt_ready, 2 * (it - 1) + g + 1)
                    for u in range(G4 * g, G4 * g + G4):
                        last = nc.tensor.matmul(pa[:, u, :], pt[old][:, u, :], pw[old][:, u, :], start=True, stop=True)
                    last.then_inc(pp_done, 1)
                    if it < ITER - 1:
                        for u in range(G4 * g, G4 * g + G4):
                            last = nc.tensor.matmul(pc[:, u, :], pw[old][:, u, :], pt[old][:, u, :], start=True, stop=True)
                        last.then_inc(ppt_done, 1)
                for g in range(2):
                    pe.wait_ge(p_ready, 2 * (it + 1) + g + 1)
                    pe.wait_ge(tt_ready, 2 * it + g + 1)
                    for u in range(G4 * g, G4 * g + G4):
                        last = nc.tensor.matmul(pd[:, u, :], pw[1 - old][:, u, :], TT[:, u, :], start=True, stop=True)
                    last.then_inc(tt_done, 1)
            pe.wait_ge(k_out, 1)
            pe.wait_ge(kg_out, 1)
            for u in range(UNITS):
                last = nc.tensor.transpose(pb[:, u, :], vT[:, u, :], core.c("ident"))
            last.then_inc(vt_done, 1)
            pe.wait_ge(tt_ready, 2 * ITER + 2)
            for u in range(UNITS):
                last = nc.tensor.matmul(pa[:, u, :], kbg[:, u, :], TT[:, u, :], start=True, stop=True)
            last.then_inc(w_done, 1)
            pe.wait_ge(v_out, 1)
            for u in range(UNITS):
                last = nc.tensor.matmul(pc[:, u, :], TT[:, u, :], vb[:, u, :], start=True, stop=True)
            last.then_inc(w_done, 1)
            pe.wait_ge(w_out, 1)
            pe.wait_ge(u_out, 1)
            pe.wait_ge(q_ready, 1)
            for n in range(S // CHUNK):
                half, r = n // 2, n % 2
                rows = slice(CHUNK * r, CHUNK * r + CHUNK)
                pe.wait_ge(state_ready, n + 1)
                for h in range(HEADS):
                    last = nc.tensor.matmul(pd[rows, h, :], wT[:, 2 * h + half, rows], state[:, h, :],
                                            start=True, stop=True)
                last.then_inc(ws_done, 1)
                pe.wait_ge(vn_ready, n + 1)
                if n:
                    pe.wait_ge(o_out, n)
                for h in range(HEADS):
                    nc.tensor.matmul(pb[:, h, 0:CHUNK], state[:, h, :], qT[:, 2 * h + half, rows],
                                     start=True, stop=False)
                    last = nc.tensor.matmul(pb[:, h, 0:CHUNK], v_new[rows, h, :], attnT[rows, 2 * h + half, rows],
                                            start=False, stop=True)
                last.then_inc(o_done, 1)
                if n < S // CHUNK - 1:
                    for h in range(HEADS):
                        last = nc.tensor.matmul(pc[:, h, :], kg[rows, 2 * h + half, :], v_new[rows, h, :],
                                                start=True, stop=True)
                    last.then_inc(st_done, 1)
            pe.wait_ge(o_sq, 1)
            for g in range(2):
                at = slice(G4 * g, G4 * g + G4)
                last = nc.tensor.matmul(pa[:, at, :], core.c("ones"), pw[0][:, at, :], start=True, stop=True)
            last.then_inc(o_sum, 1)

        @block.scalar
        def _(act):
            act.wait_ge(cols_out, 2)
            nc.scalar.activation(ecol, gcol, ACT.Exp).then_inc(ecols, 1)
            nc.scalar.activation(kgs, left, ACT.Exp).then_inc(ecols, 1)
            act.wait_ge(diff_done, 1)
            nc.scalar.activation(egrow[:, :, :], pb[:, :, :], ACT.Exp).then_inc(ecols, 1)
            nc.scalar.activation(decay[:, :, :], decay[:, :, :], ACT.Exp).then_inc(decay_done, 1)
            act.wait_ge(nt_back, 1)
            for g in range(2):
                at = slice(G4 * g, G4 * g + G4)
                nc.scalar.activation(pw[0][:, at, :], pb[:, at, :], ACT.Copy).then_inc(p_ready, 1)
            act.wait_ge(kt_done, 1)
            act.wait_ge(masked, 2)
            for u in range(UNITS):
                last = nc.scalar.activation(kbg[:, u, :], pb[:, u, :], ACT.Copy, scale=bec[:, u:u + 1])
            last.then_inc(k_out, 1)
            for it in range(ITER):
                for g in range(2):
                    act.wait_ge(pp_done, 2 * it + g + 1)
                    at = slice(G4 * g, G4 * g + G4)
                    nc.scalar.activation(pw[1 - it % 2][:, at, :], pa[:, at, :], ACT.Copy).then_inc(p_ready, 1)
            act.wait_ge(vt_done, 1)
            for u in range(UNITS):
                last = nc.scalar.activation(vb[:, u, :], pb[:, u, :], ACT.Copy, scale=beta8[:, u:u + 1])
            last.then_inc(v_out, 1)
            act.wait_ge(w_done, 1)
            nc.scalar.activation(wT[:, :, :], pa[:, :, :], ACT.Copy).then_inc(w_out, 1)
            for n in range(S // CHUNK):
                act.wait_ge(o_done, n + 1)
                nc.scalar.activation(oT[:, :, :].rearrange("p (h a) c -> p h (a c)", a=HALVES)[:, :, n * CHUNK:(n + 1) * CHUNK],
                                     pb[:, 0:HEADS, 0:CHUNK], ACT.Copy).then_inc(o_out, 1)
            act.wait_ge(o_out, S // CHUNK)
            nc.scalar.activation(pw[0][:, :, :], oT[:, :, :], ACT.Square).then_inc(o_sq, 1)
            nc.scalar.activation(attnT[:, :, :].rearrange("p (h a) c -> p h (a c)", a=HALVES),
                                 proj[:, Z:Z + 4, PAD:PAD + S], ACT.Silu).then_inc(z_done, 1)
            act.wait_ge(o_var, 1)
            nc.scalar.activation(pw[1][:, :, :], TT[:, :, :], ACT.Abs_reciprocal_sqrt).then_inc(o_root, 1)

        @block.vector
        def _(dve):
            chain = Chain(dve, own)
            nc.vector.tensor_tensor(g_diag[:, :, :], over_units(core.c("causal64")),
                                    g8.unsqueeze(2).to_broadcast([P, UNITS, P]), ALU.mult).then_inc(diag, 1)
            nc.vector.tensor_tensor(b_diag[:, :, :], over_units(core.c("ident")),
                                    beta8.unsqueeze(2).to_broadcast([P, UNITS, P]), ALU.mult).then_inc(diag, 1)
            nc.vector.memset(state[:, :, :], 0.0).then_inc(state_ready, 1)
            dve.wait_ge(cols_done, 1)
            nc.vector.tensor_copy(cols[:, 0:2, :].rearrange("p a b -> p (a b)"), pa[:, 0, 0:2 * UNITS]).then_inc(cols_out, 1)
            dve.wait_ge(cols_out, 1)
            nc.vector.tensor_tensor(left, tot, gcol, ALU.subtract).then_inc(cols_out, 1)
            dve.wait_ge(rows_done, 1)
            for u in range(UNITS):
                last = nc.vector.tensor_scalar(decay[:, u, :], pb[:, u, :], gcol[:, u:u + 1], 0.0, ALU.subtract, ALU.min)
            last.then_inc(diff_done, 1)
            dve.wait_ge(decay_done, 1)
            nc.vector.tensor_tensor(decay[:, :, :], decay[:, :, :], over_units(core.c("causal64")), ALU.mult).then_inc(masked, 1)
            dve.wait_ge(ecols, 3)
            nc.vector.tensor_tensor(bec, beta8, ecol, ALU.mult).then_inc(masked, 1)
            dve.wait_ge(masked, 2)
            dve.wait_ge(kk_done, 1)
            chain.do(nc.vector.tensor_tensor(pt[0][:, :, :], pd[:, :, :], decay[:, :, :], ALU.mult))
            dve.wait_ge(rows_done, 2)
            chain.do(nc.vector.tensor_tensor(pt[0][:, :, :], pc[:, :, :], pt[0][:, :, :], ALU.mult))
            nc.vector.tensor_tensor(pt[0][:, :, :], pt[0][:, :, :], over_units(core.c("neg_strict64")), ALU.mult).then_inc(n_ready, 1)
            dve.wait_ge(qk_done, 1)
            nc.vector.tensor_tensor(attnT[:, :, :], pa[:, :, :], decay[:, :, :], ALU.mult).then_inc(n_ready, 1)
            dve.wait_ge(n_ready, 1)
            for g in range(2):
                at = slice(G4 * g, G4 * g + G4)
                nc.vector.tensor_tensor(TT[:, at, :], pt[0][:, at, :],
                                        core.c("ident").unsqueeze(1).to_broadcast([P, G4, P]), ALU.add).then_inc(tt_ready, 1)
            dve.wait_ge(k_out, 1)
            for u in range(UNITS):
                last = nc.vector.tensor_scalar(kg[:, u, :], pb[:, u, :], kgs[:, u:u + 1], None, ALU.mult)
            last.then_inc(kg_out, 1)
            nc.vector.tensor_tensor(qT, qT, egrow[:, :, :], ALU.mult).then_inc(q_ready, 1)
            for it in range(ITER):
                if it < ITER - 1:
                    for g in range(2):
                        at = slice(G4 * g, G4 * g + G4)
                        dve.wait_ge(ppt_done, 2 * it + g + 1)
                        nc.vector.tensor_copy(pt[1 - it % 2][:, at, :], pc[:, at, :]).then_inc(pt_ready, 1)
                for g in range(2):
                    at = slice(G4 * g, G4 * g + G4)
                    dve.wait_ge(tt_done, 2 * it + g + 1)
                    dve.wait_ge(tt_ready, 2 * it + g + 1)
                    nc.vector.tensor_tensor(TT[:, at, :], pd[:, at, :], TT[:, at, :], ALU.add).then_inc(tt_ready, 1)
            dve.wait_ge(w_done, 2)
            nc.vector.tensor_copy(u_sb[:, :, :], pc[:, :, :]).then_inc(u_out, 1)
            u_by = u_sb[:, :, :].rearrange("p (h a) d -> p h a d", a=HALVES)
            for n in range(S // CHUNK):
                half, r = n // 2, n % 2
                rows = slice(CHUNK * r, CHUNK * r + CHUNK)
                dve.wait_ge(ws_done, n + 1)
                if n == 0:
                    dve.wait_ge(u_out, 1)
                nc.vector.tensor_tensor(v_new[rows, 0:HEADS, :], u_by[rows, :, half, :], pd[rows, 0:HEADS, :],
                                        ALU.subtract).then_inc(vn_ready, 1)
                if n < S // CHUNK - 1:
                    dve.wait_ge(st_done, n + 1)
                    for h in range(HEADS):
                        end = egrow[:, 2 * h + half, CHUNK * r + CHUNK - 1:CHUNK * r + CHUNK]
                        last = nc.vector.scalar_tensor_tensor(state[:, h, :], state[:, h, :], end, pc[:, h, :],
                                                              ALU.mult, ALU.add)
                    last.then_inc(state_ready, 1)
                    dve.wait_ge(state_ready, n + 2)
            dve.wait_ge(o_sum, 1)
            nc.vector.tensor_scalar(TT[:, :, :], pa[:, :, :], 1.0 / HD, EPS, ALU.mult, ALU.add).then_inc(o_var, 1)
            dve.wait_ge(o_root, 1)
            newton_rsqrt(nc, chain, pw[1][:, :, :], TT[:, :, :], pt[0][:, :, :])
            chain.do(nc.vector.tensor_tensor(pw[1][:, :, :], pw[1][:, :, :], oT[:, :, :], ALU.mult))
            dve.wait_ge(z_done, 1)
            chain.do(nc.vector.scalar_tensor_tensor(
                proj[:, Z:Z + 4, PAD:PAD + S], pw[1][:, :, :].rearrange("p (h a) c -> p h (a c)", a=HALVES), core.v("gdn_norm"),
                attnT[:, :, :].rearrange("p (h a) c -> p h (a c)", a=HALVES), ALU.mult, ALU.mult))


def other_mixers_stage(core, proj, mix, parts):
    nc = core.nc
    (weights_in, w_ready, w_zero, rx_done, gates_done, log_ready, exps_done, square_arg, root_done, lru_done, gelu_done,
     mean_done, centred, var_sq, var_done, var_root, v_ready, vt_done, vt_out, sg_done, own, sc_own, sc_done, sq_done,
     sum_done, root3, highs, scaled, gdn_high, var_ready) = (
        core.sem(f"mix_{s}") for s in (
            "weights_in", "w_ready", "w_zero", "rx_done", "gates_done", "log_ready", "exps_done", "square_arg",
            "root_done", "lru_done", "gelu_done", "mean_done", "centred", "var_sq", "var_done", "var_root", "v_ready",
            "vt_done", "vt_out", "sg_done", "own", "sc_own", "sc_done", "sq_done", "sum_done", "root3", "highs",
            "scaled", "gdn_high", "var_ready"))
    conv, small, rows = mix["conv"], mix["small"], mix["rows"]
    xc = conv[:, 12:16, :]
    with ExitStack() as ctx:
        lru_w = core.sb("lru_w", [P, 2, 4, P], F32, ctx)
        sgu_w = core.sb("sgu_w", [P, 4, P], F32, ctx)
        bufs = core.sb("mix_bufs", [P, 4, 4, S], F32, ctx)
        a_, r_, i_, t_ = (bufs[:, j, :, :] for j in range(4))
        gelu_u, gelu_v = (proj[:, at:at + 4, PAD:] for at in (SGU_U, SGU_V))
        outs = [proj[:, at:at + 4, PAD:] for at in (Z, LRU_X, SGU_U, SC_C)]
        padded = core.sb("sconv_padded", [P, 4, PAD + S], F32, ctx)
        stat = core.sb("mix_stat", [P, 3, S], F32, ctx)
        tmp = core.sb("mix_tmp", [P, 3, S], F32, ctx)
        root = core.sb("mix_root", [P, 3, S], F32, ctx)
        gelu_g = conv[:, 0:4, :]
        vtok = conv[:, 4:8, :]
        sq = bufs
        p_r = core.ps("ps_r", [P, 4, S], ctx)
        p_x = core.ps("ps_x", [P, 4, S], ctx)
        p_s = core.ps("ps_stat", [P, 2, S], ctx)
        p_n = core.ps("ps_norms", [P, 4, S], ctx)
        block = ctx.enter_context(nc.Block())
        bs = rows[:, 8:8 + 512].rearrange("p (g t) -> p g t", g=4)

        def quarter(ap):
            return ap.rearrange("p j s -> p (j s)").rearrange("p (u c) -> p u c", c=P)

        vt, p_vt, p_sg = quarter(vtok), quarter(p_r[:, :, :]), quarter(p_x[:, :, :])

        @block.sync
        def _(sp):
            sp.wait_ge(w_zero, 1)
            for m, name in enumerate(("lru_wa", "lru_wx")):
                src = core.d[name].rearrange("(j b) i o -> b i j o", b=2)
                for b in range(2):
                    at = slice(64 * b, 64 * b + 64)
                    sp.dma_start(lru_w[at, m, :, at], src[b]).then_inc(weights_in, 16)
            sp.dma_start(sgu_w[:, :, :], core.d["sgu_ws"]).then_inc(weights_in, 16)

        @block.gpsimd
        def _(pool):
            nc.gpsimd.memset(lru_w[:, :, :, :], 0.0).then_inc(w_zero, 1)
            steps = Chain(pool, sc_own)
            steps.add(nc.gpsimd.memset(padded[:, :, 0:PAD], 0.0))
            steps.do(nc.gpsimd.tensor_tensor(padded[:, :, PAD:], proj[:, SC_C:SC_C + 4, PAD:], proj[:, SC_H:SC_H + 4, PAD:],
                                             ALU.mult))
            out = outs[3]
            tap = conv[:, 8:12, :]
            for o in range(3):
                for j in range(4):
                    steps.add(nc.gpsimd.tensor_scalar((tap if o else out)[:, j, :], padded[:, j, PAD - o:PAD - o + S],
                                                      core.v("sconv", 3 * j + 2 - o), None, ALU.mult))
                steps.settle()
                if o:
                    steps.do(nc.gpsimd.tensor_tensor(out, out, tap, ALU.add))
            nc.gpsimd.tensor_tensor(out, out, proj[:, SC_B:SC_B + 4, PAD:], ALU.mult).then_inc(sc_done, 1)

        @block.tensor
        def _(pe):
            pe.wait_ge(weights_in, 80)
            for m, out in enumerate((p_r, p_x)):
                for j in range(4):
                    last = nc.tensor.matmul(out[:, j, :], lru_w[:, m, j, :], xc[:, j, :], start=True, stop=True)
                last.then_inc(rx_done, 1)
            pe.wait_ge(gelu_done, 2)
            for j in range(4):
                last = nc.tensor.matmul(p_s[:, 0, :], core.c("ones"), gelu_v[:, j, :], start=(j == 0), stop=(j == 3))
            last.then_inc(mean_done, 1)
            pe.wait_ge(var_sq, 1)
            for j in range(4):
                last = nc.tensor.matmul(p_s[:, 1, :], core.c("ones"), t_[:, j, :], start=(j == 0), stop=(j == 3))
            last.then_inc(var_done, 1)
            pe.wait_ge(v_ready, 1)
            pe.wait_ge(gates_done, 8)
            for g in range(4):
                for half in range(HALVES):
                    last = nc.tensor.transpose(p_vt[:, 2 * g + half, :], gelu_v[:, g, half * P:(half + 1) * P],
                                               core.c("ident"))
            last.then_inc(vt_done, 1)
            pe.wait_ge(vt_out, 1)
            pe.wait_ge(w_ready, 1)
            for g in range(4):
                for half in range(HALVES):
                    last = nc.tensor.matmul(p_sg[:, 2 * g + half, :], vt[:, 2 * g + half, :], sgu_w[:, g, :],
                                            start=True, stop=True)
            last.then_inc(sg_done, 1)
            for m in range(3):
                pe.wait_ge(sq_done, m + 1)
                for j in range(4):
                    last = nc.tensor.matmul(p_n[:, m, :], core.c("ones"), sq[:, m, j, :], start=(j == 0), stop=(j == 3))
                last.then_inc(sum_done, 1)

        @block.scalar
        def _(act):
            nc.scalar.activation(gelu_v, proj[:, SGU_V:SGU_V + 4, PAD:], ACT.Gelu_apprx_tanh).then_inc(gelu_done, 1)
            nc.scalar.activation(gelu_u, proj[:, SGU_U:SGU_U + 4, PAD:], ACT.Gelu_apprx_tanh).then_inc(gelu_done, 1)
            nc.scalar.activation(gelu_g, proj[:, LRU_G:LRU_G + 4, PAD:], ACT.Gelu_apprx_tanh).then_inc(gelu_done, 1)
            for m, (src, dst, bias) in enumerate(((p_r, r_, "lru_ba"), (p_x, i_, "lru_bx"))):
                act.wait_ge(rx_done, m + 1)
                for j in range(4):
                    nc.scalar.activation(dst[:, j, :], src[:, j, :], ACT.Sigmoid, bias=core.v(bias, j)).then_inc(gates_done, 1)
            act.wait_ge(log_ready, 1)
            nc.scalar.activation(a_, r_, ACT.Exp).then_inc(exps_done, 1)
            nc.scalar.activation(r_, r_, ACT.Tanh).then_inc(exps_done, 1)
            act.wait_ge(centred, 1)
            nc.scalar.activation(t_, gelu_v, ACT.Square).then_inc(var_sq, 1)
            act.wait_ge(square_arg, 1)
            nc.scalar.activation(r_, r_, ACT.Sqrt).then_inc(root_done, 1)
            act.wait_ge(var_ready, 1)
            nc.scalar.activation(root[:, 0, :], stat[:, 1, :], ACT.Abs_reciprocal_sqrt).then_inc(var_root, 1)
            act.wait_ge(vt_done, 1)
            nc.scalar.activation(vt, p_vt, ACT.Copy).then_inc(vt_out, 1)
            nc.scalar.activation(parts[:, 0:4, 0, :], outs[0], ACT.Copy).then_inc(gdn_high, 1)
            for m, ready in enumerate((lru_done, lru_done, sc_done)):
                act.wait_ge(ready, (1, 2, 1)[m])
                nc.scalar.activation(sq[:, m, :, :], outs[1 + m], ACT.Square).then_inc(sq_done, 1)
            act.wait_ge(var_ready, 2)
            nc.scalar.activation(root[:, :, :], stat[:, :, :], ACT.Abs_reciprocal_sqrt).then_inc(root3, 1)
            for m in range(3):
                act.wait_ge(scaled, m + 1)
                nc.scalar.activation(parts[:, 4 + 4 * m:8 + 4 * m, 0, :], outs[1 + m],
                                     ACT.Copy).then_inc(highs, 1)

        @block.vector
        def _(dve):
            chain = Chain(dve, own)

            def each_tile(ap):
                return ap.unsqueeze(1).to_broadcast([P, 4, S])

            dve.wait_ge(weights_in, 80)
            nc.vector.tensor_tensor(sgu_w[:, :, :], sgu_w[:, :, :], core.c("causal128").unsqueeze(1).to_broadcast([P, 4, P]),
                                    ALU.mult).then_inc(w_ready, 1)
            dve.wait_ge(gates_done, 8)
            for j in range(4):
                last = nc.vector.tensor_scalar(r_[:, j, :], r_[:, j, :], small["lru_c"][:, j:j + 1], None, ALU.mult)
            last.then_inc(log_ready, 1)
            chain.do(nc.vector.tensor_tensor(i_, i_, xc, ALU.mult))
            dve.wait_ge(mean_done, 1)
            chain.do(nc.vector.tensor_scalar(stat[:, 0, :], p_s[:, 0, :], 1.0 / 512, None, ALU.mult))
            nc.vector.tensor_tensor(gelu_v, gelu_v, each_tile(stat[:, 0, :]), ALU.subtract).then_inc(centred, 1)
            dve.wait_ge(exps_done, 2)
            dve.wait_ge(var_sq, 1)
            dve.wait_ge(var_done, 1)
            chain.do(nc.vector.tensor_tensor(t_, a_, a_, ALU.mult))
            chain.do(nc.vector.scalar_tensor_tensor(r_, t_, 1.0, r_, ALU.add, ALU.mult))
            nc.vector.tensor_scalar(r_, r_, -1.0, 1e-34, ALU.mult, ALU.max).then_inc(square_arg, 1)
            nc.vector.tensor_scalar(stat[:, 1, :], p_s[:, 1, :], 1.0 / 512, EPS, ALU.mult, ALU.add).then_inc(var_ready, 1)
            dve.wait_ge(var_root, 1)
            newton_rsqrt(nc, chain, root[:, 0, :], stat[:, 1, :], tmp[:, 0, :])
            for j in range(4):
                chain.add(nc.vector.scalar_tensor_tensor(gelu_v[:, j, :], gelu_v[:, j, :], core.v("ln_w", j), root[:, 0, :],
                                                         ALU.mult, ALU.mult))
            chain.settle()
            for j in range(4):
                last = nc.vector.tensor_scalar(gelu_v[:, j, :], gelu_v[:, j, :], core.v("ln_b", j), None, ALU.add)
            last.then_inc(v_ready, 1)
            dve.wait_ge(root_done, 1)
            chain.do(nc.vector.tensor_tensor(i_, i_, r_, ALU.mult))
            for j in range(4):
                chain.add(nc.vector.tensor_tensor_scan(t_[:, j, :], a_[:, j, :], i_[:, j, :], 0.0, ALU.mult, ALU.add))
            chain.settle()
            dve.wait_ge(gelu_done, 3)
            nc.vector.tensor_tensor(outs[1], t_, gelu_g, ALU.mult).then_inc(lru_done, 1)
            dve.wait_ge(sg_done, 1)
            chain.do(nc.vector.tensor_tensor(
                gelu_v.rearrange("p g (a c) -> p g a c", a=HALVES), p_sg.rearrange("p (g a) c -> p g a c", a=HALVES),
                bs.unsqueeze(2).to_broadcast([P, 4, HALVES, P]), ALU.add))
            nc.vector.tensor_tensor(outs[2], gelu_v, gelu_u, ALU.mult).then_inc(lru_done, 1)
            dve.wait_ge(gdn_high, 1)
            nc.vector.tensor_tensor(parts[:, 0:4, 1, :], outs[0], parts[:, 0:4, 0, :].bitcast(F32), ALU.subtract)
            dve.wait_ge(sum_done, 3)
            nc.vector.tensor_scalar(stat[:, :, :], p_n[:, 0:3, :], 1.0 / 512, EPS, ALU.mult, ALU.add).then_inc(var_ready, 1)
            dve.wait_ge(root3, 1)
            newton_rsqrt(nc, chain, root[:, :, :], stat[:, :, :], tmp[:, :, :])
            for m in range(3):
                for j in range(4):
                    out = outs[1 + m][:, j, :]
                    last = nc.vector.scalar_tensor_tensor(out, out, core.v("grp", 4 * m + j),
                                                          root[:, m, :], ALU.mult, ALU.mult)
                last.then_inc(scaled, 1)
            for m in range(3):
                at = slice(4 + 4 * m, 8 + 4 * m)
                dve.wait_ge(highs, m + 1)
                nc.vector.tensor_tensor(parts[:, at, 1, :], outs[1 + m], parts[:, at, 0, :].bitcast(F32), ALU.subtract)



DQ, DK, DV, FQ, FK, FV, G_DIL, G_DIFF = 0, 12, 24, 36, 44, 52, 60, 76
MIX_TILES = 92
GROUPS = 3
ROPE = 32
ROPE_THETA = 500000.0
DILATIONS = ((128, 1), (512, 4), (2048, 16))
LAM_INIT = 0.8 - 0.6 * float(np.exp(-0.3 * 0))
MASKED = -1e30
TWO_PI = (6.28125, 0.0019350051879882812, 3.0199159819567e-07)
ROUND = 1.5 * 2.0 ** 23


def rotary_stage(core, trig, lam):
    nc = core.nc
    pos_in, own, angle, dot_done, dot_in, exp_done = (
        core.sem(f"rotary_{s}") for s in ("pos_in", "own", "angle", "dot_done", "dot_in", "exp_done"))
    with ExitStack() as ctx:
        pos_i = core.sb("pos_i", [ROPE, S], I32, ctx)
        ang = core.sb("rotary_angle", [ROPE, S], F32, ctx)
        turns = core.sb("rotary_turns", [ROPE, 2, S], F32, ctx)
        dots = core.sb("lam_dots", [P, 2], F32, ctx)
        exps = core.sb("lam_exps", [P, 2], F32, ctx)
        p_dot = core.ps("ps_dot", [P, 2], ctx)
        block = ctx.enter_context(nc.Block())

        @block.sync
        def _(sp):
            sp.dma_start(pos_i[:, :], core.d["positions"].partition_broadcast(ROPE)).then_inc(pos_in, 16)

        @block.vector
        def _(dve):
            chain = Chain(dve, own)
            lq = core.v("lam", 0, 4)
            nc.vector.tensor_tensor(dots[:, 0:1], lq[:, 0:1], lq[:, 1:2], ALU.mult).then_inc(dot_in, 1)
            nc.vector.tensor_tensor(dots[:, 1:2], lq[:, 2:3], lq[:, 3:4], ALU.mult).then_inc(dot_in, 1)
            dve.wait_ge(pos_in, 16)
            chain.do(nc.vector.tensor_copy(ang[:, :], pos_i[:, :]))
            chain.do(nc.vector.tensor_scalar(ang[:, :], ang[:, :], core.c("inv_freq")[0:ROPE, :], None, ALU.mult))
            for j, ahead in enumerate((0.25, 0.0)):
                chain.do(nc.vector.tensor_scalar(turns[:, j, :], ang[:, :], 0.5 / float(np.pi), ahead, ALU.mult, ALU.add))
            chain.do(nc.vector.tensor_scalar(turns[:, :, :], turns[:, :, :], ROUND, None, ALU.add))
            chain.do(nc.vector.tensor_scalar(turns[:, :, :], turns[:, :, :], -ROUND, None, ALU.add))
            for j in range(2):
                chain.do(nc.vector.scalar_tensor_tensor(trig[:, j, :], turns[:, j, :], -TWO_PI[0], ang[:, :],
                                                        ALU.mult, ALU.add))
            for part in TWO_PI[1:]:
                chain.do(nc.vector.scalar_tensor_tensor(trig[:, :, :], turns[:, :, :], -part, trig[:, :, :],
                                                        ALU.mult, ALU.add))
            chain.do(nc.vector.tensor_scalar(trig[:, 0, :], trig[:, 0, :], float(np.pi / 2), None, ALU.add))
            nc.vector.tensor_scalar(trig[:, :, :], trig[:, :, :], 3.1415925, -3.1415925, ALU.min, ALU.max).then_inc(angle, 1)
            dve.wait_ge(angle, 2)
            nc.vector.tensor_scalar(trig[:, 1, :], trig[:, 1, :], core.c("rope_sign")[0:ROPE, :], None, ALU.mult)
            dve.wait_ge(exp_done, 1)
            chain.do(nc.vector.tensor_tensor(lam[:, 0:1], exps[:, 0:1], exps[:, 1:2], ALU.subtract))
            chain.do(nc.vector.tensor_scalar(lam[:, 0:1], lam[:, 0:1], LAM_INIT, None, ALU.add))
            nc.vector.tensor_scalar(lam[:, 1:3], core.v("subln", 0, 2), 1.0 - LAM_INIT, None, ALU.mult)

        @block.tensor
        def _(pe):
            pe.wait_ge(dot_in, 2)
            nc.tensor.matmul(p_dot[:, :], core.c("ones"), dots[:, :], start=True, stop=True).then_inc(dot_done, 1)

        @block.scalar
        def _(act):
            act.wait_ge(angle, 1)
            nc.scalar.activation(trig[:, :, :], trig[:, :, :], ACT.Sin).then_inc(angle, 1)
            act.wait_ge(dot_done, 1)
            nc.scalar.activation(exps[:, :], p_dot[:, :], ACT.Exp).then_inc(exp_done, 1)


def heads_stage(core, proj, trig):
    nc = core.nc
    squared, summed, var_ready, rooted, own, normed, pool_own, vt_done, vt_out, rotated, swapped = (
        core.sem(f"heads_{s}") for s in ("squared", "summed", "var_ready", "rooted", "own", "normed", "pool_own",
                                         "vt_done", "vt_out", "rotated", "swapped"))
    blocks = [(DQ + 4 * g, "dil_q") for g in range(3)] + [(DK + 4 * g, "dil_k") for g in range(3)] + \
             [(FQ + 4 * g, "diff_q") for g in range(2)] + [(FK + 4 * g, "diff_k") for g in range(2)]
    values = [DV + 4 * g for g in range(3)] + [FV + 4 * g for g in range(2)]
    with ExitStack() as ctx:
        sq = core.sb("heads_sq", [P, 2, 4, S], F32, ctx)
        var = core.sb("heads_var", [P, 4, S], F32, ctx)
        tmp = core.sb("heads_tmp", [P, 4, S], F32, ctx)
        swap = core.sb("heads_swap", [ROPE, 2, 4, S], F32, ctx)
        p_sq = core.ps("ps_heads_sq", [P, 2, 4, S], ctx)
        p_v = core.ps("ps_heads_v", [P, 2, 8, P], ctx)
        block = ctx.enter_context(nc.Block())

        @block.scalar
        def _(act):
            for n, (at, _) in enumerate(blocks):
                if n >= 2:
                    act.wait_ge(normed, n - 1)
                nc.scalar.activation(sq[:, n % 2, :, :], proj[:, at:at + 4, :], ACT.Square).then_inc(squared, 1)
                if n >= 1:
                    act.wait_ge(var_ready, n)
                    nc.scalar.activation(sq[:, (n - 1) % 2, :, :], var[:, :, :], ACT.Abs_reciprocal_sqrt).then_inc(rooted, 1)
                if n < len(values):
                    act.wait_ge(vt_done, n + 1)
                    nc.scalar.activation(proj[:, values[n]:values[n] + 4, :].rearrange("p j s -> p (j s)"),
                                         p_v[:, n % 2, :, :].rearrange("p u c -> p (u c)"), ACT.Copy).then_inc(vt_out, 1)
            n = len(blocks)
            act.wait_ge(var_ready, n)
            nc.scalar.activation(sq[:, (n - 1) % 2, :, :], var[:, :, :], ACT.Abs_reciprocal_sqrt).then_inc(rooted, 1)

        @block.tensor
        def _(pe):
            for n in range(len(blocks)):
                if n < len(values):
                    if n >= 2:
                        pe.wait_ge(vt_out, n - 1)
                    for j in range(4):
                        for half in range(HALVES):
                            last = nc.tensor.transpose(p_v[:, n % 2, 2 * j + half, :],
                                                       proj[:, values[n] + j, half * P:(half + 1) * P], core.c("ident"))
                    last.then_inc(vt_done, 1)
                pe.wait_ge(squared, n + 1)
                if n >= 2:
                    pe.wait_ge(var_ready, n - 1)
                for j in range(2):
                    last = nc.tensor.matmul(p_sq[:, n % 2, 2 * j:2 * j + 2, :], core.c("ones"), sq[:, n % 2, 2 * j:2 * j + 2, :],
                                            start=True, stop=True)
                last.then_inc(summed, 1)

        @block.vector
        def _(dve):
            chain = Chain(dve, own)
            for n, (at, gain) in enumerate(blocks):
                here = proj[:, at:at + 4, :]
                y = sq[:, n % 2, :, :]
                dve.wait_ge(summed, n + 1)
                nc.vector.tensor_scalar(var[:, :, :], p_sq[:, n % 2, :, :], 1.0 / HD, EPS, ALU.mult, ALU.add).then_inc(var_ready, 1)
                dve.wait_ge(rooted, n + 1)
                newton_rsqrt(nc, chain, y, var[:, :, :], tmp[:, :, :])
                nc.vector.scalar_tensor_tensor(here, here, core.v(gain), y, ALU.mult, ALU.mult).then_inc(normed, 1)
                dve.wait_ge(normed, n + 1)
                if n >= 2:
                    dve.wait_ge(rotated, n - 1)
                nc.vector.stream_shuffle(swap[:, n % 2, :, :].rearrange("p j s -> p (j s)"),
                                         proj[0:ROPE, at:at + 4, :].rearrange("p j s -> p (j s)"),
                                         [(p + ROPE // 2) % ROPE for p in range(ROPE)]).then_inc(swapped, 1)

        @block.gpsimd
        def _(pool):
            steps = Chain(pool, pool_own)

            def each(ap):
                return ap.unsqueeze(1).to_broadcast([ROPE, 4, S])

            for n, (at, _) in enumerate(blocks):
                here = proj[0:ROPE, at:at + 4, :]
                pool.wait_ge(swapped, n + 1)
                steps.add(nc.gpsimd.tensor_tensor(swap[:, n % 2, :, :], swap[:, n % 2, :, :], each(trig[:, 1, :]), ALU.mult))
                steps.do(nc.gpsimd.tensor_tensor(here, here, each(trig[:, 0, :]), ALU.mult))
                nc.gpsimd.tensor_tensor(here, here, swap[:, n % 2, :, :], ALU.add).then_inc(rotated, 1)


def attention_stage(core, proj, lam):
    nc = core.nc
    (masks_in, scores_done, logits, max_ready, exp_done, probs_ready, pt_done, pt_out, pv_done, out_done, own,
     sq_ready, sum_done, var_ready, rooted) = (
        core.sem(f"attn_{s}") for s in ("masks_in", "scores_done", "logits", "max_ready", "exp_done", "probs_ready",
                                        "pt_done", "pt_out", "pv_done", "out_done", "own", "sq_ready", "sum_done",
                                        "var_ready", "rooted"))
    SCALE = HD ** -0.5
    units = [(False, h, a) for h in range(HEADS) for a in range(HALVES)] + \
            [(True, h, a) for h in range(HEADS) for a in range(HALVES)]

    def parts_of(diff):
        return 2 if diff else GROUPS

    def exps_through(n):
        return sum(2 if units[m][0] else 1 for m in range(n + 1))

    with ExitStack() as ctx:
        masks = core.sb("masks", [P, HALVES, 4, S], F32, ctx)
        s_buf = core.sb("scores", [P, 2, GROUPS, S], F32, ctx)
        pT = core.sb("probs_T", [P, 2, 2 * GROUPS, P], F32, ctx)
        stats = core.sb("attn_stats", [P, 2, 8], F32, ctx)
        p_s = core.ps("ps_scores", [P, 2, 4, S], ctx)
        p_t = core.ps("ps_probs_T", [P, 8, P], ctx)
        p_o = core.ps("ps_out", [P, 2, 4, P], ctx)
        block = ctx.enter_context(nc.Block())

        @block.sync
        def _(sp):
            sp.dma_start(masks[:, :, :, :], core.d["masks"]).then_inc(masks_in, 16)

        def q_tile(diff, h, j):
            return FQ + 2 * h + j if diff else DQ + 4 * j + h

        def k_tile(diff, h, j):
            return FK + 2 * h + j if diff else DK + 4 * j + h

        def out_tile(diff, h, e):
            return FQ + 2 * h + e if diff else DQ + h

        @block.tensor
        def _(pe):
            def scores(n):
                diff, h, a = units[n]
                if n >= 2:
                    pe.wait_ge(logits, n - 1)
                for j in range(parts_of(diff)):
                    last = nc.tensor.matmul(p_s[:, n % 2, j, 0:(a + 1) * P], proj[:, q_tile(diff, h, j), a * P:(a + 1) * P],
                                            proj[:, k_tile(diff, h, j), 0:(a + 1) * P], start=True, stop=True)
                last.then_inc(scores_done, 1)

            scores(0)
            for n, (diff, h, a) in enumerate(units):
                if n + 1 < len(units):
                    scores(n + 1)
                pe.wait_ge(probs_ready, n + 1)
                if n:
                    pe.wait_ge(pt_out, n)
                n_mats = 1 if diff else GROUPS
                for j in range(n_mats):
                    for b in range(a + 1):
                        last = nc.tensor.transpose(p_t[:, j * 2 + b, :], s_buf[:, n % 2, j, b * P:(b + 1) * P], core.c("ident"))
                last.then_inc(pt_done, 1)
                pe.wait_ge(pt_out, n + 1)
                if n >= 2:
                    pe.wait_ge(out_done, n - 1)
                terms = [(j, b) for j in range(n_mats) for b in range(a + 1)]
                for e in range(2 if diff else 1):
                    for m, (j, b) in enumerate(terms):
                        v = FV + 2 * h + e if diff else DV + 4 * j + h
                        last = nc.tensor.matmul(p_o[:, n % 2, e, :], proj[:, v, b * P:(b + 1) * P], pT[:, n % 2, j * 2 + b, :],
                                                start=(m == 0), stop=(m == len(terms) - 1))
                last.then_inc(pv_done, 1)
            pe.wait_ge(sq_ready, 1)
            for h in range(HEADS):
                for e in range(2):
                    last = nc.tensor.matmul(p_s[:, 0, h, :], core.c("ones"), proj[:, FK + 2 * h + e, :],
                                            start=(e == 0), stop=(e == 1))
            last.then_inc(sum_done, 1)

        @block.scalar
        def _(act):
            def exps(n):
                diff, _, a = units[n]
                act.wait_ge(max_ready, n + 1)
                s, st = s_buf[:, n % 2, :, :], stats[:, n % 2, :]
                if diff:
                    for j in range(2):
                        nc.scalar.activation(s[:, j, 0:(a + 1) * P], s[:, j, 0:(a + 1) * P], ACT.Exp, bias=st[:, 2 + j:3 + j],
                                             scale=SCALE, accum_out=st[:, 4 + j:5 + j]).then_inc(exp_done, 1)
                else:
                    nc.scalar.activation(s[:, :, 0:(a + 1) * P], s[:, :, 0:(a + 1) * P], ACT.Exp, bias=st[:, 2:3],
                                         scale=SCALE, accum_out=st[:, 4:5]).then_inc(exp_done, 1)

            exps(0)
            for n, (diff, h, a) in enumerate(units):
                if n + 1 < len(units):
                    exps(n + 1)
                act.wait_ge(pt_done, n + 1)
                if n >= 2:
                    act.wait_ge(pv_done, n - 1)
                n_mats = 1 if diff else GROUPS
                nc.scalar.activation(pT[:, n % 2, :, :].rearrange("p (j b) c -> p j b c", b=2)[:, 0:n_mats, 0:a + 1, :],
                                     p_t[:, 0:2 * GROUPS, :].rearrange("p (j b) c -> p j b c", b=2)[:, 0:n_mats, 0:a + 1, :],
                                     ACT.Copy).then_inc(pt_out, 1)
                act.wait_ge(pv_done, n + 1)
                ne = 2 if diff else 1
                t = out_tile(diff, h, 0)
                nc.scalar.activation(proj[:, t:t + ne, a * P:(a + 1) * P], p_o[:, n % 2, 0:ne, :], ACT.Copy).then_inc(out_done, 1)
            act.wait_ge(out_done, len(units))
            nc.scalar.activation(proj[:, FK:FK + 8, :], proj[:, FQ:FQ + 8, :], ACT.Square).then_inc(sq_ready, 1)
            act.wait_ge(var_ready, 1)
            nc.scalar.activation(proj[:, FK:FK + 4, :], proj[:, FK + 4:FK + 8, :], ACT.Abs_reciprocal_sqrt).then_inc(rooted, 1)

        @block.vector
        def _(dve):
            chain = Chain(dve, own)
            dve.wait_ge(masks_in, 16)

            def logits_of(n):
                diff, _, a = units[n]
                keys = (a + 1) * P
                s, st = s_buf[:, n % 2, :, :], stats[:, n % 2, :]
                dve.wait_ge(scores_done, n + 1)
                if n >= 2:
                    dve.wait_ge(pt_done, n - 1)
                nj = parts_of(diff)
                mask = masks[:, a, 3:4, 0:keys].to_broadcast([P, 2, keys]) if diff else masks[:, a, 0:GROUPS, 0:keys]
                nc.vector.tensor_tensor(s[:, 0:nj, 0:keys], p_s[:, n % 2, 0:nj, 0:keys], mask, ALU.add).then_inc(logits, 1)
                dve.wait_ge(logits, n + 1)
                if diff:
                    chain.do(nc.vector.reduce_max(st[:, 0:2], s[:, 0:2, 0:keys], AX))
                    nc.vector.tensor_scalar(st[:, 2:4], st[:, 0:2], -SCALE, None, ALU.mult).then_inc(max_ready, 1)
                else:
                    chain.do(nc.vector.tensor_reduce(st[:, 0:1], s[:, 0:nj, 0:keys], mybir.AxisListType.XY, ALU.max))
                    nc.vector.tensor_scalar(st[:, 2:3], st[:, 0:1], -SCALE, None, ALU.mult).then_inc(max_ready, 1)

            logits_of(0)
            for n, (diff, h, a) in enumerate(units):
                if n + 1 < len(units):
                    logits_of(n + 1)
                keys = (a + 1) * P
                s, st = s_buf[:, n % 2, :, :], stats[:, n % 2, :]
                dve.wait_ge(exp_done, exps_through(n))
                if diff:
                    chain.do(nc.vector.reciprocal(st[:, 6:8], st[:, 4:6]))
                    chain.do(nc.vector.tensor_tensor(st[:, 7:8], st[:, 7:8], lam[:, 0:1], ALU.mult))
                    chain.do(nc.vector.tensor_scalar(s[:, 1, 0:keys], s[:, 1, 0:keys], st[:, 7:8], None, ALU.mult))
                    nc.vector.scalar_tensor_tensor(s[:, 0, 0:keys], s[:, 0, 0:keys], st[:, 6:7], s[:, 1, 0:keys],
                                                   ALU.mult, ALU.subtract).then_inc(probs_ready, 1)
                else:
                    chain.do(nc.vector.reciprocal(st[:, 6:7], st[:, 4:5]))
                    nc.vector.tensor_scalar(s[:, :, 0:keys], s[:, :, 0:keys], st[:, 6:7], None, ALU.mult).then_inc(probs_ready, 1)
            dve.wait_ge(sum_done, 1)
            var = proj[:, FK + 4:FK + 8, :]
            y = proj[:, FK:FK + 4, :]
            nc.vector.tensor_scalar(var, p_s[:, 0, :, :], 1.0 / (2 * HD), EPS, ALU.mult, ALU.add).then_inc(var_ready, 1)
            dve.wait_ge(rooted, 1)
            newton_rsqrt(nc, chain, y, var, proj[:, DK:DK + 4, :])
            for e in range(2):
                out = proj[:, FQ:FQ + 8, :].rearrange("p (h e) s -> p h e s", e=2)[:, :, e, :]
                nc.vector.scalar_tensor_tensor(out, out, lam[:, 1 + e:2 + e], y, ALU.mult, ALU.mult)


def halves_stage(core, parts, sources):
    nc = core.nc
    core.stage += 1
    with ExitStack() as ctx:
        highs = core.sem(f"halves{core.stage}_highs")
        block = ctx.enter_context(nc.Block())

        @block.scalar
        def _(act):
            for at, src in sources:
                nc.scalar.activation(parts[:, at:at + src.shape[1], 0, :], src, ACT.Copy).then_inc(highs, 1)

        @block.vector
        def _(dve):
            for n, (at, src) in enumerate(sources):
                dve.wait_ge(highs, n + 1)
                part = parts[:, at:at + src.shape[1], :, :]
                nc.vector.tensor_tensor(part[:, :, 1, :], src, part[:, :, 0, :].bitcast(F32), ALU.subtract)


def branch_stage(core, prod, proj, following):
    nc = core.nc
    gate_done, own = core.sem("branch_gate_done"), core.sem("branch_own")
    with ExitStack() as ctx:
        acc = core.ps(f"acc_{core.chunk}", [P, 2, 2, S], ctx)
        z = core.sb("branch_z", [P, 4, S], F32, ctx)
        gate = core.sb("branch_gate", [P, 4, S], F32, ctx)
        block = ctx.enter_context(nc.Block())

        @block.sync
        def _(sp):
            stream(core, sp, prod, following)

        @block.scalar
        def _(act):
            nc.scalar.preload_act_table(ACT.Sigmoid)
            for i, t in walk(core, act, prod, split_high):
                take_cross(core, act, prod, acc, i, t)
                g = proj[:, (G_DIFF if t % 2 else G_DIL) + t // 2 + 2 * i, :]
                nc.scalar.activation(gate[:, t, :], g, ACT.Sigmoid).then_inc(gate_done, 1)

        @block.vector
        def _(dve):
            for i, t in walk(core, dve, prod, split_low):
                take_tile(core, dve, prod, acc, z[:, t, :], i, t)
                taken(core, dve, prod, i, t)
                dve.wait_ge(gate_done, i * 4 + (t + 1))
                nc.vector.tensor_tensor(z[:, t, :], z[:, t, :], gate[:, t, :], ALU.mult).then_inc(own, 1)
                if t % 2:
                    dve.wait_ge(own, i * 4 + (t + 1))
                    nc.vector.tensor_tensor(proj[:, 2 * i + t // 2, :], z[:, t - 1, :], z[:, t, :], ALU.add)

        @block.tensor
        def _(pe):
            multiply_all(core, pe, prod, acc)
    passed(core, prod)



def weight_tiles(w):
    k, n = w.shape
    return np.ascontiguousarray(w.reshape(k // P, P, n // P, P).transpose(2, 1, 0, 3))


def by_partition(v):
    v = np.asarray(v)
    lead = int(np.prod(v.shape[:-1]))
    return v.reshape(lead, -1, P).transpose(2, 1, 0).reshape(P, -1)


def constants():
    t = np.arange(P)
    same = t[:, None] // CHUNK == t[None, :] // CHUNK
    parts = {
        "ident": np.eye(P), "ones": np.ones((P, P)),
        "causal64": same & (t[:, None] <= t[None, :]), "block64": same,
        "neg_strict64": -1.0 * (same & (t[:, None] < t[None, :])), "causal128": t[:, None] <= t[None, :],
        "inv_freq": (np.float32(ROPE_THETA) ** (-(2 * (t % (ROPE // 2))).astype(np.float32) / np.float32(ROPE)))[:, None],
        "rope_sign": np.where(t < ROPE // 2, -1.0, 1.0)[:, None],
    }
    return np.concatenate([np.asarray(parts[n], np.float32) for n in CONSTS], axis=1)


def attention_masks():
    q = (np.arange(HALVES)[None, :] * P + np.arange(P)[:, None])[:, :, None]
    dist = q - np.arange(S)[None, None, :]
    seen = [(dist >= 0) & (dist <= window) & (dist % dilation == 0) for window, dilation in DILATIONS] + [dist >= 0]
    return np.where(np.stack(seen, axis=2), 0.0, MASKED).astype(np.float32)



def whole(nc, d, out):
    def tiles_of(name, tile):
        def source(i, t, k0, nk):
            return d[name][tile(i, t)][:, k0:k0 + nk, :].rearrange("p a b -> p (a b)")
        return source

    def pair(i, t):
        return 2 * i + t

    def moving_of(parts):
        return lambda t, k: parts[:, k, :, :]

    with ExitStack() as ctx:
        core = Core(nc, ctx, d)
        stored = core.sem("stored")

        def proj_product(name, tiles, parts, nk=KT):
            return Product(tiles // 2, [nk, nk], tiles_of(name, pair), parts and moving_of(parts))

        def up_product(name, parts):
            return Product(FF_TILES, [KT, KT], tiles_of(name, lambda i, t: i + FF_TILES * t), parts and moving_of(parts))

        def gate_up_product(n, parts):
            def source(i, t, k0, nk):
                return d[f"ffn{n}_w_{('gate', 'up')[t]}_2"][i][:, k0:k0 + nk, :].rearrange("p a b -> p (a b)")
            return Product(FF_TILES, [KT, KT], source, parts and moving_of(parts))

        def down_product(name, parts):
            return proj_product(name, KT, parts, FF_TILES)

        def swiglu(n, following):
            with ExitStack() as c:
                g_parts = core.sb(f"ffn{n}_g_parts", [P, FF_TILES, 2, S], F32R, c)
                with ExitStack() as c2:
                    h_parts = core.sb(f"ffn{n}_h_parts", [P, KT, 2, S], F32R, c2)
                    norm_stage(core, h_parts, f"ffn{n}_norm")
                    swiglu_up_stage(core, gate_up_product(n, h_parts), g_parts, down_product(f"ffn{n}_w_down_2", None))
                product_add_stage(core, down_product(f"ffn{n}_w_down_2", g_parts), 0.5, following)

        start_stage(core, proj_product("w_in", PROJ_TILES, None))

        with ExitStack() as c:
            proj = core.sb("proj", [P, PROJ_TILES, PAD + S], F32, c)
            mix = {"conv": core.sb("conv", [P, 16, S], F32, c), "rows": core.sb("rows", [P, 8 + 512], F32, c),
                   "small": {n: core.sb(f"small_{n}", [P] + shape, F32, c)
                             for n, shape in (("g", [HEADS, HALVES]), ("beta", [HEADS, HALVES]), ("lru_c", [4]))}}
            with ExitStack() as c2:
                h_parts = core.sb("h_parts", [P, KT, 2, S], F32R, c2)
                norm_stage(core, h_parts, "pre_mix")
                with nc.Block() as block:
                    @block.vector
                    def _(dve):
                        nc.vector.memset(proj[:, :, 0:PAD], 0.0)
                product_stage(core, proj_product("w_in", PROJ_TILES, h_parts), lambda i, t: proj[:, 2 * i + t, PAD:PAD + S],
                              proj_product("w_out", KT, None))
                gdn_prepare_stage(core, proj, h_parts, mix)
            gdn_stage(core, proj, mix)
            with ExitStack() as c2:
                m_parts = core.sb("m_parts", [P, KT, 2, S], F32R, c2)
                other_mixers_stage(core, proj, mix, m_parts)
                product_stage(core, proj_product("w_out", KT, m_parts), lambda i, t: proj[:, 2 * i + t, 0:S],
                              up_product("ffn_up", None))
                residual_norm_stage(core, proj[:, 0:KT, 0:S], "post_mix")

        with ExitStack() as c:
            g_parts = core.sb("ffn_g_parts", [P, FF_TILES, 2, S], F32R, c)
            with ExitStack() as c2:
                h_parts = core.sb("ffn_h_parts", [P, KT, 2, S], F32R, c2)
                norm_stage(core, h_parts, "pre_ffn")
                conv_ffn_up_stage(core, up_product("ffn_up", h_parts), g_parts, down_product("ffn_down", None))
            with ExitStack() as c2:
                y = core.sb("ffn_y", [P, KT, S], F32, c2)
                product_stage(core, down_product("ffn_down", g_parts), lambda i, t: y[:, 2 * i + t, :],
                              gate_up_product(1, None))
                residual_norm_stage(core, y[:, :, :], "post_ffn")

        swiglu(1, proj_product("w_in_2", MIX_TILES, None))
        with ExitStack() as c:
            proj = core.sb("proj_2", [P, MIX_TILES, S], F32, c)
            lam = core.sb("lam", [P, 3], F32, c)
            with ExitStack() as c2:
                h_parts = core.sb("mix_h_parts", [P, KT, 2, S], F32R, c2)
                norm_stage(core, h_parts, "mix_norm")
                product_stage(core, proj_product("w_in_2", MIX_TILES, h_parts), lambda i, t: proj[:, 2 * i + t, :],
                              branch_product(d, None))
            with ExitStack() as c2:
                trig = core.sb("trig", [ROPE, 2, S], F32, c2)
                rotary_stage(core, trig, lam)
                heads_stage(core, proj, trig)
            attention_stage(core, proj, lam)
            with ExitStack() as c2:
                o_parts = core.sb("o_parts", [P, 12, 2, S], F32R, c2)
                halves_stage(core, o_parts, [(0, proj[:, DQ:DQ + 4, :]), (4, proj[:, FQ:FQ + 4, :]),
                                             (8, proj[:, FQ + 4:FQ + 8, :])])
                branch_stage(core, branch_product(d, o_parts), proj, proj_product("w_out_2", KT, None))
            with ExitStack() as c2:
                y_parts = core.sb("y_parts", [P, KT, 2, S], F32R, c2)
                halves_stage(core, y_parts, [(j, proj[:, j:j + 4, :]) for j in range(0, KT, 4)])
                product_add_stage(core, proj_product("w_out_2", KT, y_parts), 1.0, gate_up_product(2, None))
        swiglu(2, None)

        with nc.Block() as block:
            @block.sync
            def _(sp):
                sp.dma_start(out, core.x[:, :, :]).then_inc(stored, 16)
                sp.wait_ge(stored, 16)


def branch_product(d, parts):
    def source(i, t, k0, nk):
        name = ("w_dil_branch_2", "w_diff_branch_2")[t % 2]
        return d[name][2 * i + t // 2][:, k0:k0 + nk, :].rearrange("p a b -> p (a b)")
    return Product(KT // 2, [4, 8, 4, 8], source, parts is not None and (lambda t, k: parts[:, (4 if t % 2 else 0) + k, :, :]))


def kernel(**inputs):
    import concourse.bacc as bacc
    from concourse.bass_utils import run_bass_kernel_spmd

    a = {k: np.asarray(v) for k, v in inputs.items()}
    gates = slice(4 * 512, 4 * 512 + 2 * HEADS)
    w_in = a["w_in"][0]
    arrays = {
        "x": a["x"][0].T.reshape(KT, P, S).transpose(1, 0, 2),
        "w_in": weight_tiles(np.delete(w_in, np.r_[gates], axis=1)),
        "w_ba": w_in[:, gates].reshape(KT, P, 2 * HEADS).transpose(1, 0, 2),
        "positions": a["positions_2"][0],
        "a_log": a["gdn_a_log"][0], "dt_bias": a["gdn_dt_bias"][0], "sgu_b": a["sgu_b"][0].reshape(-1),
        "lru_wa": a["lru_wa"][0], "lru_wx": a["lru_wx"][0], "sgu_ws": a["sgu_ws"][0].transpose(2, 0, 1),
        "consts": constants(), "masks": attention_masks(),
    }
    for name in ("w_out", "ffn_up", "ffn_down", "ffn1_w_gate_2", "ffn1_w_up_2", "ffn1_w_down_2", "w_in_2",
                 "w_dil_branch_2", "w_diff_branch_2", "w_out_2", "ffn2_w_gate_2", "ffn2_w_up_2", "ffn2_w_down_2"):
        arrays[name] = weight_tiles(a[name][0])
    vectors = {
        "pre_mix": a["pre_mix_norm"], "post_mix": a["post_mix_norm"], "pre_ffn": a["pre_ffn_norm"],
        "post_ffn": a["post_ffn_norm"], "ffn1_norm": a["ffn1_norm_2"], "mix_norm": a["mix_norm_2"],
        "ffn2_norm": a["ffn2_norm_2"], "gdn_conv": a["gdn_conv_w"][0], "gdn_norm": a["gdn_norm_w"],
        "lru_conv": a["lru_conv_w"][0], "lru_conv_b": a["lru_conv_b"], "lru_ba": a["lru_ba"].reshape(1, -1),
        "lru_bx": a["lru_bx"].reshape(1, -1), "lru_lambda": a["lru_lambda"], "ln_w": a["sgu_ln_w"], "ln_b": a["sgu_ln_b"],
        "sconv": a["sconv_w"][0], "grp": a["grp_norm_w"].reshape(1, -1), "ffn_conv": a["ffn_conv_w"][0],
        "ffn_conv_b": a["ffn_conv_b"], "dil_q": a["dil_q_norm_2"], "dil_k": a["dil_k_norm_2"],
        "diff_q": a["diff_q_norm_2"], "diff_k": a["diff_k_norm_2"],
        "lam": np.concatenate([a["diff_lq1_2"], a["diff_lk1_2"], a["diff_lq2_2"], a["diff_lk2_2"]]),
        "subln": a["diff_subln_2"],
    }
    arrays["vectors"] = np.concatenate([by_partition(vectors[n]) for n in VECTORS], axis=1)

    nc = bacc.Bacc("TRN2", target_bir_lowering=False, num_devices=1)
    arrays = {f"in_{n}": np.ascontiguousarray(v) for n, v in arrays.items()}
    d = {n[3:]: nc.dram_tensor(n, v.shape, mybir.dt.from_np(v.dtype), kind="ExternalInput").ap()
         for n, v in arrays.items()}
    out = nc.dram_tensor("out_x", (P, KT, S), F32, kind="ExternalOutput").ap()
    whole(nc, d, out)
    r = run_bass_kernel_spmd(nc, [arrays], core_ids=[0])
    got = r.results[0]["out_x"]
    return np.ascontiguousarray(got.transpose(2, 1, 0).reshape(1, S, DM))
```

```python
from contextlib import ExitStack

import numpy as np

import concourse.bass as bass
from concourse import mybir

F32 = mybir.dt.float32
F32R = mybir.dt.float32r
I32 = mybir.dt.int32
ALU = mybir.AluOpType
ACT = mybir.ActivationFunctionType
AX = mybir.AxisListType.X

P = 128
S = 256
DM = 2048
KT = DM // P
EPS = 1e-6
KG = 8
SLOTS = 4
HEADS = 4
FF_TILES = 5632 // P
PAD = 4
HALVES = S // P
ARENA_TILES = 92

VECTORS = {}
_at = 0
for _name, _n in (("pre_mix", 16), ("post_mix", 16), ("pre_ffn", 16), ("post_ffn", 16), ("ffn1_norm", 16),
                  ("mix_norm", 16), ("ffn2_norm", 16), ("gdn_conv", 48), ("gdn_norm", 1), ("lru_conv", 16),
                  ("lru_conv_b", 4), ("lru_ba", 4), ("lru_bx", 4), ("lru_lambda", 4), ("ln_w", 4), ("ln_b", 4),
                  ("sconv", 12), ("grp", 12), ("ffn_conv", 264), ("ffn_conv_b", 88), ("head_gain", 20),
                  ("lam", 4), ("subln", 2)):
    VECTORS[_name] = (_at, _n)
    _at += _n
N_VECTORS = _at

CONSTS = {}
_at = 0
for _name, _n in (("ident", 128), ("ones", 128), ("causal64", 128), ("block64", 128), ("neg_strict64", 128),
                  ("causal128", 128), ("inv_freq", 1), ("rope_sign", 1)):
    CONSTS[_name] = (_at, _n)
    _at += _n
N_CONSTS = _at


class Chain:

    def __init__(self, eng, sem):
        self.eng, self.sem, self.n = eng, sem, 0

    def add(self, ins):
        ins.then_inc(self.sem, 1)
        self.n += 1

    def settle(self):
        self.eng.wait_ge(self.sem, self.n)

    def do(self, ins):
        self.add(ins)
        self.settle()


class Product:

    def __init__(self, bodies, tiles, source, first=None, parts=None):
        self.bodies, self.tiles, self.source = bodies, tiles, source
        self.first, self.parts = first or [0] * len(tiles), parts
        self.chunks = [(t, k0, min(KG, nk - k0)) for t, nk in enumerate(tiles) for k0 in range(0, nk, KG)]
        self.per_body = len(self.chunks)
        assert self.per_body % SLOTS == 0 and len(tiles) % 2 == 0

    def of_tile(self, t):
        return [(u, c) for u, c in enumerate(self.chunks) if c[0] == t]


class Region:

    def __init__(self, flat):
        self.flat, self.at = flat, 0

    def take(self, *shape):
        n = int(np.prod(shape))
        assert self.at + n <= self.flat.shape[1]
        ap = self.flat[:, self.at:self.at + n]
        self.at += n
        if len(shape) == 1:
            return ap
        names = "abcd"[:len(shape)]
        return ap.rearrange(f"p ({' '.join(names)}) -> p {' '.join(names)}", **dict(zip(names, shape)))


class Core:

    def __init__(self, nc, ctx, d):
        self.nc, self.ctx, self.d = nc, ctx, d
        self.x = self.sb("x_T", [P, KT, S], F32)
        self.h_at = nc.sbuf_base
        self.h_mem = self.sb("halves_memory", [P, KT, 2, S], F32)
        self.h = self.over(self.h_at, "moving_halves", KT)
        self.arena_at = nc.sbuf_base
        self.arena = self.sb("arena", [P, ARENA_TILES, S], F32)
        self.g_parts = self.over(self.arena_at, "gated_halves", FF_TILES)
        self.y_parts = self.over(self.arena_at + KT * S * 4, "branch_halves", KT)
        self.raw = self.sb("weights_raw", [P, SLOTS, KG * P], F32)
        self.high = self.sb("weights_high", [P, SLOTS, KG, P], F32R)
        self.low = self.sb("weights_low", [P, SLOTS, KG, P], F32R)
        self.cross = self.sb("cross_products", [P, 2, S], F32)
        self.z = self.sb("unscaled", [P, 2, S], F32)
        self.sq = self.sb("squares", [P, 2, S], F32)
        self.total = self.sb("squares_total", [P, S], F32)
        self.rs = self.sb("token_scale", [P, S], F32)
        self.vec = self.sb("vectors", [P, N_VECTORS], F32)
        self.const = self.sb("constants", [P, N_CONSTS], F32)
        self.loaded = [self.sem(f"weights_loaded{s}") for s in range(SLOTS)]
        self.high_ready = self.sem("high_ready")
        self.low_ready = self.sem("low_ready")
        self.slots_free = self.sem("slots_free")
        self.acc_free = self.sem("acc_free")
        self.cross_ready = self.sem("cross_ready")
        self.z_free = self.sem("z_free")
        self.y_scaled = self.sem("y_scaled")
        self.x_ready = self.sem("x_ready")
        self.part_high = self.sem("part_high")
        self.part_low = self.sem("part_low")
        self.squared = self.sem("squared")
        self.squares_used = self.sem("squares_used")
        self.summed = self.sem("summed")
        self.carried = self.sem("carried")
        self.var_ready = self.sem("var_ready")
        self.rooted = self.sem("rooted")
        self.newton = self.sem("newton")
        self.rs_ready = self.sem("rs_ready")
        self.hidden_free = [self.sem(f"hidden{t}_free") for t in range(2)]
        self.activated = self.sem("activated")
        self.product_ready = self.sem("product_ready")
        self.g_high = self.sem("g_high")
        self.swiglus = 0
        self.pairs = 0
        self.parts = 0
        self.squares = 0
        self.totals = 0
        self.norms = 0
        self.xs = 0
        self.ys = 0
        self.scaled = 0
        self.chunk = 0
        self.tile = 0
        self.stage = 0

    def sb(self, name, shape, dt, ctx=None):
        return (ctx or self.ctx).enter_context(self.nc.sbuf_tensor(name, shape, dt))

    def over(self, at, name, n):
        assert at % 32 == 0
        return self.nc.alloc_sbuf_tensor_at(name, [P, n, 2, S], F32R, offset=at)

    def carry_wait(self, eng):
        eng.sem_inc(self.carried, 1)

    def ps(self, name, shape, ctx, dt=F32):
        return ctx.enter_context(self.nc.psum_tensor(name, shape, dt))

    def sem(self, name):
        return self.ctx.enter_context(self.nc.semaphore(name))

    def v(self, name, j=0, n=1):
        c = VECTORS[name][0] + j
        return self.vec[:, c:c + n] if isinstance(c, int) else self.vec[:, bass.ds(c, n)]

    def c(self, name):
        c, n = CONSTS[name]
        return self.const[:, c:c + n]



def load_chunk(core, sp, prod, base, i, u):
    t, k0, nk = prod.chunks[u]
    n = i * prod.per_body + (base + u)
    if not (isinstance(n, int) and n < SLOTS):
        sp.wait_ge(core.low_ready, n - (SLOTS - 1))
    sp.dma_start(core.raw[:, u % SLOTS, 0:nk * P], prod.source(i, t, k0, nk)).then_inc(core.loaded[u % SLOTS], 16)


def prefetch(core, sp, prod, base):
    for u in range(SLOTS):
        load_chunk(core, sp, prod, base, 0, u)


def stream(core, sp, prod, following):
    base, per = core.chunk, prod.per_body

    ahead = -(-2 * SLOTS // per)
    with sp.Fori(0, prod.bodies - ahead) as i:
        for u in range(2 * SLOTS, per + 2 * SLOTS):
            load_chunk(core, sp, prod, base, i + u // per, u % per)
    for u in range((prod.bodies - ahead) * per + 2 * SLOTS, prod.bodies * per + 2 * SLOTS):
        if u < prod.bodies * per:
            load_chunk(core, sp, prod, base, u // per, u % per)
        elif following is not None:
            v = u - prod.bodies * per
            load_chunk(core, sp, following, base + prod.bodies * per, v // following.per_body, v % following.per_body)


def split_high(core, act, n, slot, nk):
    act.wait_ge(core.loaded[slot], n[0])
    act.wait_ge(core.slots_free, n[1] + 1)
    core.nc.scalar.activation(core.high[:, slot, 0:nk, :].rearrange("p a b -> p (a b)"),
                              core.raw[:, slot, 0:nk * P], ACT.Copy).then_inc(core.high_ready, 1)


def split_low(core, dve, n, slot, nk):
    dve.wait_ge(core.high_ready, n[1] + 1)
    core.nc.vector.tensor_tensor(core.low[:, slot, 0:nk, :].rearrange("p a b -> p (a b)"),
                                 core.raw[:, slot, 0:nk * P],
                                 core.high[:, slot, 0:nk, :].rearrange("p a b -> p (a b)").bitcast(F32),
                                 ALU.subtract).then_inc(core.low_ready, 1)


def steps(core, eng, prod, split, lo=0, hi=None, following=None):
    hi = prod.bodies if hi is None else hi
    per = prod.per_body

    def body(i, final):
        for t in range(len(prod.tiles)):
            own = prod.of_tile(t)
            for j, (u, _) in enumerate(own):
                if j == len(own) - 1:
                    yield i, t
                v = u + SLOTS
                source = following if v >= per and final else prod
                if source is not None:
                    nk = source.chunks[v % per if source is prod else v - per][2]
                    n = (i * (16 * per // SLOTS) + 16 * ((core.chunk + v) // SLOTS + 1), i * per + (core.chunk + v))
                    split(core, eng, n, v % SLOTS, nk)

    ends = hi == prod.bodies
    last = hi - 1 if ends else hi
    if last - lo > 1:
        with eng.Fori(lo, last) as i:
            yield from body(i, False)
    elif last > lo:
        yield from body(lo, False)
    if ends:
        yield from body(prod.bodies - 1, True)


def multiply(core, pe, prod, acc, i, t, before=None):
    bank = t % 2
    pe.wait_ge(core.acc_free, i * len(prod.tiles) + (core.tile + t + 1))
    nk_all = prod.tiles[t]
    parts = core.h if prod.parts is None else prod.parts
    for u, (_, k0, nk) in prod.of_tile(t):
        pe.wait_ge(core.low_ready, i * prod.per_body + (core.chunk + u + 1))
        for k in range(nk):
            if before is not None:
                before(t, prod.first[t] + k0 + k)
            x = parts[:, prod.first[t] + k0 + k, :, :]
            core.nc.tensor.matmul(acc[:, bank, :, :], core.high[:, u % SLOTS, k, :], x,
                                  start=(k0 + k == 0), stop=False)
            last = core.nc.tensor.matmul(acc[:, bank, 0, :], core.low[:, u % SLOTS, k, :], x[:, 0, :],
                                         start=False, stop=(k0 + k == nk_all - 1))
        last.then_inc(core.slots_free, 1)


def pe_steps(core, pe, prod, acc, lo=0, hi=None, before=None):
    hi = prod.bodies if hi is None else hi
    if lo == 0 and before is not None:
        for t in range(len(prod.tiles)):
            multiply(core, pe, prod, acc, 0, t, before)
            yield 0, t
        lo = 1
    if hi - lo > 1:
        with pe.Fori(lo, hi) as i:
            for t in range(len(prod.tiles)):
                multiply(core, pe, prod, acc, i, t)
                yield i, t
    elif hi > lo:
        for t in range(len(prod.tiles)):
            multiply(core, pe, prod, acc, lo, t)
            yield lo, t


def multiply_all(core, pe, prod, acc, before=None):
    for _ in pe_steps(core, pe, prod, acc, before=before):
        pass


def take_cross(core, act, prod, acc, i, t):
    last = prod.of_tile(t)[-1][0]
    act.wait_ge(core.slots_free, i * prod.per_body + (SLOTS + core.chunk + last + 1))
    core.nc.scalar.activation(core.cross[:, t % 2, :], acc[:, t % 2, 1, :], ACT.Copy).then_inc(core.cross_ready, 1)


def take_tile(core, dve, prod, acc, out, i, t):
    dve.wait_ge(core.cross_ready, i * len(prod.tiles) + (core.tile + t + 1))
    core.nc.vector.tensor_tensor(out, acc[:, t % 2, 0, :], core.cross[:, t % 2, :], ALU.add).then_inc(core.acc_free, 1)


def taken(core, eng, prod, i, t):
    eng.wait_ge(core.acc_free, i * len(prod.tiles) + (2 + core.tile + t + 1))


def take_for_scaling(core, dve, prod, acc, i, t):
    dve.wait_ge(core.z_free, i * len(prod.tiles) + (core.scaled + t + 1))
    take_tile(core, dve, prod, acc, core.z[:, t % 2, :], i, t)


def scale_tile(core, pool, prod, out, i, t):
    taken(core, pool, prod, i, t)
    core.nc.gpsimd.tensor_tensor(out, core.z[:, t % 2, :], core.rs[:, :], ALU.mult).then_inc(core.z_free, 1)


def tile_scaled(core, eng, prod, i, t):
    eng.wait_ge(core.z_free, i * len(prod.tiles) + (2 + core.scaled + t + 1))


def with_previous(core, eng, prod, split, following):
    for i, t in steps(core, eng, prod, split, 0, 1):
        yield i, t, (i, t - 1) if t else None
    for i, t in steps(core, eng, prod, split, 1, following=following):
        yield i, t, (i, t - 1) if t else (i - 1, len(prod.tiles) - 1)


def passed(core, prod, scaled=False):
    core.chunk += prod.bodies * prod.per_body
    core.tile += prod.bodies * len(prod.tiles)
    if scaled:
        core.scaled += prod.bodies * len(prod.tiles)



def square_tile(core, act, src, base, i, n, t):
    act.wait_ge(core.squares_used, i * n + (base + t + 1))
    core.carry_wait(act)
    core.nc.scalar.activation(core.sq[:, t % 2, :], src, ACT.Square).then_inc(core.squared, 1)


def add_squares(core, pool, prod, base):
    n = len(prod.tiles)

    def add(i, t):
        pool.wait_ge(core.squared, i * n + (base + t + 1))
        if isinstance(i, int) and i * n + t == 0:
            core.nc.gpsimd.tensor_copy(core.total[:, :], core.sq[:, 0, :]).then_inc(core.squares_used, 1)
        else:
            pool.wait_ge(core.squares_used, i * n + (base + t + 2))
            core.nc.gpsimd.tensor_tensor(core.total[:, :], core.total[:, :], core.sq[:, t % 2, :],
                                         ALU.add).then_inc(core.squares_used, 1)
    for t in range(n):
        add(0, t)
    with pool.Fori(1, prod.bodies) as i:
        for t in range(n):
            add(i, t)


class TokenScale:

    def __init__(self, core, sum_):
        self.core, self.sum, self.norm = core, sum_, core.norms
        self.var, self.tmp = core.sq[:, 0, :], core.sq[:, 1, :]
        core.norms += 1

    def of_total(self):
        self.total_at = self.core.totals
        self.core.totals += 1
        self.sum_done = (self.core.summed, self.total_at + 1)
        return self

    def of_tiles(self, base):
        self.base = base
        self.sum_done = (self.core.squares_used, base + KT + 2)
        return self

    def sum_total(self, pe):
        core = self.core
        pe.wait_ge(core.squares_used, core.squares + 2)
        core.nc.tensor.matmul(self.sum, core.c("ones"), core.total[:, :], start=True, stop=True).then_inc(core.summed, 1)

    def sum_tile(self, pe, k):
        core = self.core
        pe.wait_ge(core.squared, self.base + k + 1)
        core.nc.tensor.matmul(self.sum, core.c("ones"), core.sq[:, k % 2, :], start=(k == 0),
                              stop=(k == KT - 1)).then_inc(core.squares_used, 1)

    def variance(self, dve):
        dve.wait_ge(*self.sum_done)
        self.core.nc.vector.tensor_scalar(self.var, self.sum, 1.0 / DM, EPS, ALU.mult,
                                          ALU.add).then_inc(self.core.var_ready, 1)

    def root(self, act):
        core = self.core
        act.wait_ge(core.var_ready, self.norm + 1)
        core.nc.scalar.activation(core.rs[:, :], self.var, ACT.Abs_reciprocal_sqrt).then_inc(core.rooted, 1)

    def refine(self, dve):
        core = self.core
        dve.wait_ge(core.rooted, self.norm + 1)
        chain = Chain(dve, core.newton)
        chain.n = 2 * self.norm
        chain.do(core.nc.vector.tensor_tensor(self.tmp, core.rs[:, :], core.rs[:, :], ALU.mult))
        chain.do(core.nc.vector.scalar_tensor_tensor(self.tmp, self.tmp, -0.5, self.var, ALU.mult, ALU.mult))
        core.nc.vector.scalar_tensor_tensor(core.rs[:, :], self.tmp, 1.5, core.rs[:, :],
                                            ALU.add, ALU.mult).then_inc(core.rs_ready, 1)

    def ready(self, eng):
        eng.wait_ge(self.core.rs_ready, self.norm + 1)



def high_part(core, act, k, src, gain):
    core.nc.scalar.activation(core.h[:, k, 0, :], src, ACT.Copy,
                              scale=1.0 if gain is None else gain).then_inc(core.part_high, 1)


def low_part(core, dve, k, src, gain, base):
    dve.wait_ge(core.part_high, k + (base + 1))
    high = core.h[:, k, 0, :].bitcast(F32)
    if gain is None:
        ins = core.nc.vector.tensor_tensor(core.h[:, k, 1, :], src, high, ALU.subtract)
    else:
        ins = core.nc.vector.scalar_tensor_tensor(core.h[:, k, 1, :], src, gain, high, ALU.mult, ALU.subtract)
    ins.then_inc(core.part_low, 1)


class Given:

    def __init__(self, core, sources):
        self.core, self.sources, self.base = core, sources, core.parts
        core.parts += len(sources)

    def act(self, act):
        for k, src in enumerate(self.sources):
            high_part(self.core, act, k, src, None)

    def dve(self, dve):
        for k, src in enumerate(self.sources):
            low_part(self.core, dve, k, src, None, self.base)

    def on(self, pe):
        return None if not self.sources else lambda t, k: pe.wait_ge(self.core.part_low, self.base + k + 1)


class Normed:

    def __init__(self, core, ctx, gain, how, y=None, y_gain=None):
        self.core, self.gain, self.how, self.y, self.y_gain = core, gain, how, y, y_gain
        core.stage += 1
        ps = core.ps(f"ps_scale{core.stage}", [P, 2, S], ctx)
        self.y_scale = TokenScale(core, ps[:, 0, :]).of_total() if how == "residual" else None
        self.scale = TokenScale(core, ps[:, 1, :])
        if how == "prepared":
            self.scale.of_total()
        else:
            self.scale.of_tiles(core.squares)
        self.base, self.xs, self.ys = core.parts, core.xs, core.ys

    def passed(self):
        core = self.core
        if self.how != "prepared":
            core.parts += KT
            core.squares += KT
        if self.how == "residual":
            core.xs += KT
            core.ys += KT

    def g(self, k):
        return self.core.v(self.gain, k)

    def act(self, act):
        core = self.core
        if self.how == "residual":
            self.y_scale.root(act)
        if self.how != "prepared":
            for k in range(KT):
                if self.how == "residual":
                    act.wait_ge(core.x_ready, self.xs + k + 1)
                high_part(core, act, k, core.x[:, k, :], self.g(k))
                if self.how == "residual":
                    square_tile(core, act, core.x[:, k, :], self.scale.base, 0, 0, k)

    def dve(self, dve):
        core = self.core
        if self.how == "loaded":
            for k in range(KT):
                dve.wait_ge(core.squares_used, self.scale.base + k + 1)
                core.nc.vector.tensor_tensor(core.sq[:, k % 2, :], core.x[:, k, :], core.x[:, k, :],
                                             ALU.mult).then_inc(core.squared, 1)
                low_part(core, dve, k, core.x[:, k, :], self.g(k), self.base)
        elif self.how == "residual":
            self.y_scale.variance(dve)
            self.y_scale.refine(dve)
            self.y_scale.ready(dve)
            AHEAD = 3
            for k in range(KT + AHEAD):
                if k < KT:
                    core.nc.vector.scalar_tensor_tensor(self.y(k), self.y(k), core.v(self.y_gain, k), core.rs[:, :],
                                                        ALU.mult, ALU.mult).then_inc(core.y_scaled, 1)
                if k >= AHEAD:
                    low_part(core, dve, k - AHEAD, core.x[:, k - AHEAD, :], self.g(k - AHEAD), self.base)

    def pool(self, pool):
        core = self.core
        if self.how == "residual":
            for k in range(KT):
                pool.wait_ge(core.y_scaled, self.ys + k + 1)
                core.nc.gpsimd.tensor_tensor(core.x[:, k, :], core.x[:, k, :], self.y(k), ALU.add).then_inc(core.x_ready, 1)

    def start(self, pe):
        if self.how == "residual":
            self.y_scale.sum_total(pe)

    def on(self, pe):
        if self.how == "prepared":
            return lambda t, k: None

        def before(t, k):
            if t == 0:
                self.scale.sum_tile(pe, k)
                pe.wait_ge(self.core.part_low, self.base + k + 1)
        return before

    def after_first(self, pe):
        if self.how == "prepared":
            self.scale.sum_total(pe)



def plain_product_stage(core, prod, sources, out, following):
    nc = core.nc
    n = len(prod.tiles)
    base = core.squares
    final = (prod.bodies - 1, n - 1)
    with ExitStack() as ctx:
        acc = core.ps(f"acc_{core.chunk}", [P, 2, 2, S], ctx)
        operand = Given(core, sources)
        block = ctx.enter_context(nc.Block())

        @block.sync
        def _(sp):
            stream(core, sp, prod, following)

        @block.scalar
        def _(act):
            def square(i, t):
                taken(core, act, prod, i, t)
                square_tile(core, act, out(i, t), base, i, n, t)

            operand.act(act)
            for i, t, previous in with_previous(core, act, prod, split_high, following):
                take_cross(core, act, prod, acc, i, t)
                if previous:
                    square(*previous)
            square(*final)

        @block.vector
        def _(dve):
            operand.dve(dve)
            for i, t in steps(core, dve, prod, split_low, following=following):
                take_tile(core, dve, prod, acc, out(i, t), i, t)

        @block.tensor
        def _(pe):
            multiply_all(core, pe, prod, acc, operand.on(pe))

        @block.gpsimd
        def _(pool):
            add_squares(core, pool, prod, base)
    core.squares += prod.bodies * n
    passed(core, prod)


def normed_product_stage(core, prod, gain, out, following, zeros):
    nc = core.nc
    with ExitStack() as ctx:
        acc = core.ps(f"acc_{core.chunk}", [P, 2, 2, S], ctx)
        operand = Normed(core, ctx, gain, "loaded")
        block = ctx.enter_context(nc.Block())

        @block.sync
        def _(sp):
            stream(core, sp, prod, following)

        @block.scalar
        def _(act):
            operand.act(act)
            for i, t, previous in with_previous(core, act, prod, split_high, following):
                take_cross(core, act, prod, acc, i, t)
                if not previous:
                    operand.scale.root(act)

        @block.vector
        def _(dve):
            operand.dve(dve)
            for i, t, previous in with_previous(core, dve, prod, split_low, following):
                take_for_scaling(core, dve, prod, acc, i, t)
                if not previous:
                    operand.scale.variance(dve)
                    operand.scale.refine(dve)

        @block.tensor
        def _(pe):
            multiply_all(core, pe, prod, acc, operand.on(pe))

        @block.gpsimd
        def _(pool):
            nc.gpsimd.memset(zeros, 0.0)
            operand.scale.ready(pool)
            with pool.Fori(0, prod.bodies) as i:
                for t in range(len(prod.tiles)):
                    scale_tile(core, pool, prod, out(i, t), i, t)
    operand.passed()
    passed(core, prod, scaled=True)


def product_add_stage(core, prod, factor, following, next_gain=None):
    nc = core.nc
    core.stage += 1
    n = len(prod.tiles)
    squares, xs, parts = core.squares, core.xs, core.parts
    final = (prod.bodies - 1, n - 1)
    with ExitStack() as ctx:
        acc = core.ps(f"acc_{core.chunk}", [P, 2, 2, S], ctx)
        y = core.sb(f"branch{core.stage}", [P, 2, S], F32, ctx)
        block = ctx.enter_context(nc.Block())

        @block.sync
        def _(sp):
            stream(core, sp, prod, following)

        @block.scalar
        def _(act):
            def prepare(i, t):
                k = i * n + t
                act.wait_ge(core.x_ready, k + (xs + 1))
                high_part(core, act, k, core.x[:, k, :], core.v(next_gain, k))
                square_tile(core, act, core.x[:, k, :], squares, i, n, t)

            for i, t, previous in with_previous(core, act, prod, split_high, following):
                take_cross(core, act, prod, acc, i, t)
                if previous and next_gain:
                    prepare(*previous)
            if next_gain:
                prepare(*final)

        @block.vector
        def _(dve):
            def prepare(i, t):
                k = i * n + t
                low_part(core, dve, k, core.x[:, k, :], core.v(next_gain, k), parts)

            for i, t, previous in with_previous(core, dve, prod, split_low, following):
                take_tile(core, dve, prod, acc, y[:, t, :], i, t)
                taken(core, dve, prod, i, t)
                x = core.x[:, n * i + t, :]
                nc.vector.scalar_tensor_tensor(x, y[:, t, :], factor, x, ALU.mult, ALU.add).then_inc(core.x_ready, 1)
                if previous and next_gain:
                    prepare(*previous)
            if next_gain:
                prepare(*final)

        @block.tensor
        def _(pe):
            multiply_all(core, pe, prod, acc)

        @block.gpsimd
        def _(pool):
            if next_gain:
                add_squares(core, pool, prod, squares)
    core.xs += KT
    if next_gain:
        core.parts += KT
        core.squares += KT
    passed(core, prod)


def conv_ffn_up_stage(core, prod, operand_of, g_parts, following):
    nc = core.nc
    biased_ready, conv_ready, own = core.sem("ffn_biased_ready"), core.sem("ffn_conv_ready"), core.sem("ffn_own")
    with ExitStack() as ctx:
        acc = core.ps(f"acc_{core.chunk}", [P, 2, 2, S], ctx)
        hidden = core.sb("ffn_hidden", [P, 2, PAD + S], F32, ctx)
        tail = core.arena[:, 2 * FF_TILES:2 * FF_TILES + 4, :]
        conv, gelu, g = tail[:, 0:2, :], tail[:, 2, :], tail[:, 3, :]
        operand = operand_of(ctx)
        scale = operand.scale
        base = core.pairs
        block = ctx.enter_context(nc.Block())

        def tap(i, t, j):
            return core.v("ffn_conv", i * 3 + (t * FF_TILES * 3 + j))

        @block.sync
        def _(sp):
            stream(core, sp, prod, following)

        @block.gpsimd
        def _(pool):
            nc.gpsimd.memset(hidden[:, :, 0:PAD], 0.0)
            operand.pool(pool)
            scale.ready(pool)
            with pool.Fori(0, prod.bodies) as i:
                for t in range(2):
                    pool.wait_ge(conv_ready, i * 2 + (t + 1))
                    scale_tile(core, pool, prod, hidden[:, t, PAD:PAD + S], i, t)

        @block.scalar
        def _(act):
            def bias_tile(i, t):
                tile_scaled(core, act, prod, i, t)
                nc.scalar.activation(conv[:, t, :], hidden[:, t, PAD:PAD + S], ACT.Identity, scale=tap(i, t, 2),
                                     bias=core.v("ffn_conv_b", i + t * FF_TILES)).then_inc(biased_ready, 1)

            def activate(i):
                act.wait_ge(conv_ready, i * 2 + 3)
                nc.scalar.activation(gelu, conv[:, 0, :], ACT.Gelu_apprx_tanh).then_inc(core.activated, 1)

            def high(i):
                act.wait_ge(core.product_ready, i + (base + 1))
                nc.scalar.activation(g_parts[:, i, 0, :], g, ACT.Copy).then_inc(core.g_high, 1)

            operand.act(act)
            for i, t in steps(core, act, prod, split_high, 0, 1):
                take_cross(core, act, prod, acc, i, t)
                if t == 0:
                    scale.root(act)
                    nc.scalar.preload_act_table(ACT.Gelu_apprx_tanh)
            bias_tile(0, 0)
            for i, t in steps(core, act, prod, split_high, 1, following=following):
                take_cross(core, act, prod, acc, i, t)
                if t == 0:
                    activate(i - 1)
                    bias_tile(i - 1, 1)
                else:
                    high(i - 1)
                    bias_tile(i, 0)
            activate(prod.bodies - 1)
            bias_tile(prod.bodies - 1, 1)
            high(prod.bodies - 1)

        @block.vector
        def _(dve):
            def convolve(i, t):
                dve.wait_ge(biased_ready, i * 2 + (t + 1))
                nc.vector.scalar_tensor_tensor(conv[:, t, :], hidden[:, t, PAD - 1:PAD - 1 + S], tap(i, t, 1),
                                               conv[:, t, :], ALU.mult, ALU.add).then_inc(own, 1)
                dve.wait_ge(own, i * 2 + (t + 1))
                nc.vector.scalar_tensor_tensor(conv[:, t, :], hidden[:, t, PAD - 2:PAD - 2 + S], tap(i, t, 0),
                                               conv[:, t, :], ALU.mult, ALU.add).then_inc(conv_ready, 1)

            def gated(i):
                dve.wait_ge(core.activated, i + (base + 1))
                dve.wait_ge(conv_ready, i * 2 + 4)
                nc.vector.tensor_tensor(g, gelu, conv[:, 1, :], ALU.mult).then_inc(core.product_ready, 1)

            def low(i):
                dve.wait_ge(core.g_high, i + (base + 1))
                nc.vector.tensor_tensor(g_parts[:, i, 1, :], g, g_parts[:, i, 0, :].bitcast(F32), ALU.subtract)

            dve.sem_inc(conv_ready, 2)
            operand.dve(dve)
            for i, t in steps(core, dve, prod, split_low, 0, 1):
                take_for_scaling(core, dve, prod, acc, i, t)
                if t == 0:
                    scale.variance(dve)
                    scale.refine(dve)
            convolve(0, 0)
            for i, t in steps(core, dve, prod, split_low, 1, following=following):
                take_for_scaling(core, dve, prod, acc, i, t)
                if t == 0:
                    convolve(i - 1, 1)
                    gated(i - 1)
                else:
                    low(i - 1)
                    convolve(i, 0)
            convolve(prod.bodies - 1, 1)
            gated(prod.bodies - 1)
            low(prod.bodies - 1)

        @block.tensor
        def _(pe):
            operand.start(pe)
            for i, t in pe_steps(core, pe, prod, acc, before=operand.on(pe)):
                if isinstance(i, int) and i + t == 0:
                    operand.after_first(pe)
    operand.passed()
    core.pairs += prod.bodies
    passed(core, prod, scaled=True)


def swiglu_up_stage(core, prod, operand_of, g_parts, following):
    nc = core.nc
    core.stage += 1
    with ExitStack() as ctx:
        acc = core.ps(f"acc_{core.chunk}", [P, 2, 2, S], ctx)
        hidden = core.sb(f"ffn_hidden{core.stage}", [P, 2, S], F32, ctx)
        silu = core.sb(f"ffn_silu{core.stage}", [P, S], F32, ctx)
        g = core.sb(f"ffn_g{core.stage}", [P, S], F32, ctx)
        operand = operand_of(ctx)
        scale = operand.scale
        base = core.pairs
        used = core.swiglus * prod.bodies
        core.swiglus += 1
        block = ctx.enter_context(nc.Block())

        @block.sync
        def _(sp):
            stream(core, sp, prod, following)

        @block.gpsimd
        def _(pool):
            operand.pool(pool)
            scale.ready(pool)
            with pool.Fori(0, prod.bodies) as i:
                for t in range(2):
                    pool.wait_ge(core.hidden_free[t], i + (used + 1))
                    scale_tile(core, pool, prod, hidden[:, t, :], i, t)

        @block.scalar
        def _(act):
            def activate(i):
                tile_scaled(core, act, prod, i, 0)
                act.wait_ge(core.product_ready, i + base)
                nc.scalar.activation(silu[:, :], hidden[:, 0, :], ACT.Silu).then_inc(core.hidden_free[0], 1)

            def high(i):
                act.wait_ge(core.product_ready, i + (base + 1))
                nc.scalar.activation(g_parts[:, i, 0, :], g[:, :], ACT.Copy).then_inc(core.g_high, 1)

            operand.act(act)
            for i, t in steps(core, act, prod, split_high, 0, 1):
                take_cross(core, act, prod, acc, i, t)
                if t == 0:
                    scale.root(act)
                    nc.scalar.preload_act_table(ACT.Silu)
            activate(0)
            for i, t in steps(core, act, prod, split_high, 1, following=following):
                take_cross(core, act, prod, acc, i, t)
                if t == 0:
                    high(i - 1)
                else:
                    activate(i)
            high(prod.bodies - 1)

        @block.vector
        def _(dve):
            def gated(i):
                dve.wait_ge(core.hidden_free[0], i + (used + 2))
                tile_scaled(core, dve, prod, i, 1)
                nc.vector.tensor_tensor(g[:, :], silu[:, :], hidden[:, 1, :], ALU.mult).then_inc(core.product_ready, 1)

            def low(i):
                dve.wait_ge(core.g_high, i + (base + 1))
                nc.vector.tensor_tensor(g_parts[:, i, 1, :], g[:, :], g_parts[:, i, 0, :].bitcast(F32),
                                        ALU.subtract).then_inc(core.hidden_free[1], 1)

            operand.dve(dve)
            for i, t in steps(core, dve, prod, split_low, 0, 1):
                take_for_scaling(core, dve, prod, acc, i, t)
                if t == 0:
                    scale.variance(dve)
                    scale.refine(dve)
            for i, t in steps(core, dve, prod, split_low, 1, following=following):
                take_for_scaling(core, dve, prod, acc, i, t)
                if t == 0:
                    gated(i - 1)
                else:
                    low(i - 1)
            gated(prod.bodies - 1)
            low(prod.bodies - 1)

        @block.tensor
        def _(pe):
            operand.start(pe)
            for i, t in pe_steps(core, pe, prod, acc, before=operand.on(pe)):
                if isinstance(i, int) and i + t == 0:
                    operand.after_first(pe)
    operand.passed()
    core.pairs += prod.bodies
    passed(core, prod, scaled=True)


def start_stage(core, first):
    nc = core.nc
    inputs_loaded = core.sem("inputs_loaded")
    with nc.Block() as block:
        @block.sync
        def _(sp):
            prefetch(core, sp, first, 0)
            sp.dma_start(core.x[:, :, :], core.d["x"]).then_inc(inputs_loaded, 16)
            sp.dma_start(core.vec[:, :], core.d["vectors"]).then_inc(inputs_loaded, 16)
            sp.dma_start(core.const[:, :], core.d["consts"]).then_inc(inputs_loaded, 16)
            for u in range(SLOTS, 2 * SLOTS):
                load_chunk(core, sp, first, 0, u // first.per_body, u % first.per_body)
            sp.wait_ge(inputs_loaded, 48)

        @block.tensor
        def _(pe):
            pe.sem_inc(core.slots_free, SLOTS)

        @block.scalar
        def _(act):
            for u in range(SLOTS):
                split_high(core, act, (16, u), u, first.chunks[u][2])

        @block.vector
        def _(dve):
            dve.sem_inc(core.acc_free, 2)
            for u in range(SLOTS):
                split_low(core, dve, (16, u), u, first.chunks[u][2])

        @block.gpsimd
        def _(pool):
            pool.sem_inc(core.z_free, 2)
            pool.sem_inc(core.squares_used, 2)
            pool.sem_inc(core.hidden_free[0], 1)
            pool.sem_inc(core.hidden_free[1], 1)



Q, K_, V, Z, LRU_X, LRU_G, SGU_U, SGU_V, SC_B, SC_C, SC_H = (4 * j for j in range(11))
PROJ_TILES = 44
MIXED = (Z, LRU_X, SGU_U, SC_C)
UNITS = HEADS * HALVES
HD = 128
CHUNK = 64
LRU_C = 8.0


def newton_rsqrt(nc, chain, y, v, t):
    chain.do(nc.vector.tensor_tensor(t, y, y, ALU.mult))
    chain.do(nc.vector.scalar_tensor_tensor(t, t, -0.5, v, ALU.mult, ALU.mult))
    chain.do(nc.vector.scalar_tensor_tensor(y, t, 1.5, y, ALU.add, ALU.mult))


def gdn_prepare_stage(core, proj, mix):
    nc = core.nc
    w_ba_loaded, conv_steps, silu_done, squared, ba_done, summed, rooted, own, gate_in, gate_exp, var_ready = (
        core.sem(f"gdn_{s}") for s in ("w_ba_loaded", "conv_steps", "silu_done", "squared", "ba_done", "summed",
                                       "rooted", "own", "gate_in", "gate_exp", "var_ready"))
    conv, small, rows = mix["conv"], mix["small"], mix["rows"]
    with ExitStack() as ctx:
        w_ba = core.sb("w_ba", [P, KT, 2 * HEADS], F32, ctx)
        spare = Region(mix["spare"])
        sq, var, tmp = spare.take(8, S), spare.take(4, S), spare.take(4, S)
        sp_in, sp_abs, sp_e, sp_z, sp_w, sp_p = (core.sb(f"softplus_{n}", [P, 12], F32, ctx)
                                                 for n in ("in", "abs", "e", "z", "w", "p"))
        beta_e = core.sb("beta_e", [P, HALVES, HEADS], F32, ctx)
        exp_a = core.sb("exp_a", [P, HEADS], F32, ctx)
        scales = core.sb("ba_scales", [P, HALVES], F32, ctx)
        ba = core.sb("ba", [P, HALVES, 2 * HEADS], F32, ctx)
        p_ba = core.ps("ps_ba", [P, HALVES, 2 * HEADS], ctx)
        p_rs = core.ps("ps_rs", [P, HALVES, P], ctx)
        ssq = core.ps("ps_ssq", [P, 8, S], ctx)
        block = ctx.enter_context(nc.Block())
        GROUP_AT = (Q, K_, V, LRU_X)

        @block.sync
        def _(sp):
            sp.dma_start(w_ba[:, :, :], core.d["w_ba"]).then_inc(w_ba_loaded, 16)
            sp.dma_start(rows[:, 0:HEADS], core.d["a_log"].partition_broadcast(P)).then_inc(w_ba_loaded, 16)
            sp.dma_start(rows[:, HEADS:2 * HEADS], core.d["dt_bias"].partition_broadcast(P)).then_inc(w_ba_loaded, 16)
            sp.dma_start(rows[:, 8:8 + 512], core.d["sgu_b"].partition_broadcast(P)).then_inc(w_ba_loaded, 16)

        @block.tensor
        def _(pe):
            pe.wait_ge(w_ba_loaded, 64)
            for half in range(HALVES):
                at = slice(half * P, (half + 1) * P)
                for k in range(KT):
                    for part in range(2):
                        last = nc.tensor.matmul(p_ba[:, half, :], core.h[:, k, part, at].bitcast(F32), w_ba[:, k, :],
                                                start=(k == 0 and part == 0), stop=(k == KT - 1 and part == 1))
            last.then_inc(ba_done, 1)
            for half in range(HALVES):
                last = nc.tensor.transpose(p_rs[:, half, :], core.rs[:, half * P:(half + 1) * P], core.c("ident"))
            last.then_inc(ba_done, 1)
            for g in range(2):
                pe.wait_ge(squared, g + 1)
                for j in range(2):
                    at = slice(4 * g + 2 * j, 4 * g + 2 * j + 2)
                    last = nc.tensor.matmul(ssq[:, at, :], core.c("ones"), sq[:, at, :], start=True, stop=True)
                last.then_inc(summed, 1)

        @block.scalar
        def _(act):
            for g in range(3):
                act.wait_ge(conv_steps, 16 * (g + 1))
                at = slice(4 * g, 4 * g + 4)
                nc.scalar.activation(conv[:, at, :], conv[:, at, :], ACT.Silu).then_inc(silu_done, 1)
                if g < 2:
                    act.wait_ge(silu_done, g + 1)
                    nc.scalar.activation(sq[:, at, :], conv[:, at, :], ACT.Square).then_inc(squared, 1)
            act.wait_ge(gate_in, 1)
            nc.scalar.activation(sp_e[:, :], sp_abs[:, :], ACT.Exp, scale=-1.0).then_inc(gate_exp, 1)
            nc.scalar.activation(beta_e[:, :, :], ba[:, :, 0:HEADS], ACT.Exp, scale=-1.0).then_inc(gate_exp, 1)
            nc.scalar.activation(exp_a[:, :], rows[:, 0:HEADS], ACT.Exp).then_inc(gate_exp, 1)
            for g in range(2):
                act.wait_ge(var_ready, g + 1)
                nc.scalar.activation(sq[:, 4 * g:4 * g + 4, :], var[:, :, :], ACT.Abs_reciprocal_sqrt).then_inc(rooted, 1)

        @block.vector
        def _(dve):
            steps = Chain(dve, conv_steps)
            for g in range(4):
                for o in range(4):
                    for j in range(4):
                        src = proj[:, GROUP_AT[g] + j, PAD - o:PAD - o + S]
                        dst = conv[:, 4 * g + j, :]
                        w = core.v("gdn_conv", 4 * (4 * g + j) + 3 - o) if g < 3 else core.v("lru_conv", 4 * j + 3 - o)
                        if o:
                            steps.add(nc.vector.scalar_tensor_tensor(dst, src, w, dst, ALU.mult, ALU.add))
                        elif g < 3:
                            steps.add(nc.vector.tensor_scalar(dst, src, w, None, ALU.mult))
                        else:
                            steps.add(nc.vector.tensor_scalar(dst, src, w, core.v("lru_conv_b", j), ALU.mult, ALU.add))
                    steps.settle()
            chain = Chain(dve, own)
            dve.wait_ge(ba_done, 2)
            chain.do(nc.vector.tensor_copy(scales[:, :], p_rs[:, :, 0]))
            for half in range(HALVES):
                chain.add(nc.vector.tensor_scalar(ba[:, half, :], p_ba[:, half, :], scales[:, half:half + 1], None, ALU.mult))
            chain.settle()
            chain.add(nc.vector.tensor_tensor(
                sp_in[:, 0:8].rearrange("p (a h) -> p a h", a=HALVES), ba[:, :, HEADS:2 * HEADS],
                rows[:, HEADS:2 * HEADS].unsqueeze(1).to_broadcast([P, HALVES, HEADS]), ALU.add))
            chain.do(nc.vector.tensor_scalar(sp_in[:, 8:12], core.v("lru_lambda", 0, 4), -1.0, None, ALU.mult))
            chain.do(nc.vector.tensor_scalar(sp_z[:, :], sp_in[:, :], -1.0, None, ALU.mult))
            nc.vector.tensor_tensor(sp_abs[:, :], sp_in[:, :], sp_z[:, :], ALU.max).then_inc(gate_in, 1)
            dve.wait_ge(gate_exp, 3)
            chain.do(nc.vector.tensor_scalar(sp_w[:, :], sp_e[:, :], 2.0, None, ALU.add))
            chain.do(nc.vector.reciprocal(sp_w[:, :], sp_w[:, :]))
            chain.do(nc.vector.tensor_tensor(sp_z[:, :], sp_e[:, :], sp_w[:, :], ALU.mult))
            chain.do(nc.vector.tensor_tensor(sp_w[:, :], sp_z[:, :], sp_z[:, :], ALU.mult))
            chain.do(nc.vector.tensor_scalar(sp_p[:, :], sp_w[:, :], 1.0 / 17, None, ALU.mult))
            for d in (15, 13, 11, 9, 7, 5, 3):
                chain.do(nc.vector.scalar_tensor_tensor(sp_p[:, :], sp_p[:, :], 1.0 / d, sp_w[:, :], ALU.add, ALU.mult))
            chain.do(nc.vector.scalar_tensor_tensor(sp_p[:, :], sp_p[:, :], 1.0, sp_z[:, :], ALU.add, ALU.mult))
            chain.do(nc.vector.tensor_scalar(sp_in[:, :], sp_in[:, :], 0.0, None, ALU.max))
            chain.do(nc.vector.scalar_tensor_tensor(sp_in[:, :], sp_p[:, :], 2.0, sp_in[:, :], ALU.mult, ALU.add))
            chain.add(nc.vector.scalar_tensor_tensor(
                small["g"][:, :, :].rearrange("p h a -> p a h"), sp_in[:, 0:8].rearrange("p (a h) -> p a h", a=HALVES),
                -1.0, exp_a[:, :].unsqueeze(1).to_broadcast([P, HALVES, HEADS]), ALU.mult, ALU.mult))
            chain.add(nc.vector.tensor_scalar(small["lru_c"][:, :], sp_in[:, 8:12], -LRU_C, None, ALU.mult))
            chain.do(nc.vector.tensor_scalar(beta_e[:, :, :], beta_e[:, :, :], 1.0, None, ALU.add))
            chain.do(nc.vector.reciprocal(beta_e[:, :, :], beta_e[:, :, :]))
            chain.do(nc.vector.tensor_copy(small["beta"][:, :, :].rearrange("p h a -> p a h"), beta_e[:, :, :]))
            for g in range(2):
                at = slice(4 * g, 4 * g + 4)
                dve.wait_ge(summed, g + 1)
                nc.vector.tensor_scalar(var[:, :, :], ssq[:, at, :], EPS, None, ALU.add).then_inc(var_ready, 1)
                dve.wait_ge(rooted, g + 1)
                newton_rsqrt(nc, chain, sq[:, at, :], var[:, :, :], tmp[:, :, :])
                chain.do(nc.vector.scalar_tensor_tensor(conv[:, at, :], conv[:, at, :], HD ** -0.5 if g == 0 else 1.0,
                                                        sq[:, at, :], ALU.mult, ALU.mult))


def gdn_stage(core, proj, mix):
    nc = core.nc
    (diag, cols_done, cols_out, ecols, rows_done, diff_done, decay_done, masked, kk_done, qk_done, n_ready, nt_back,
     p_ready, pp_done, ppt_done, pt_ready, tt_done, tt_ready, kt_done, vt_done, k_out, v_out, w_done, w_out, u_out,
     ws_done, vn_ready, o_done, st_done, o_out, state_ready, o_sq, o_sum, o_root, z_done, own, kg_out, q_ready, o_var) = (
        core.sem(f"delta_{s}") for s in (
            "diag", "cols_done", "cols_out", "ecols", "rows_done", "diff_done", "decay_done", "masked", "kk_done",
            "qk_done", "n_ready", "nt_back", "p_ready", "pp_done", "ppt_done", "pt_ready", "tt_done", "tt_ready",
            "kt_done", "vt_done", "k_out", "v_out", "w_done", "w_out", "u_out", "ws_done", "vn_ready", "o_done",
            "st_done", "o_out", "state_ready", "o_sq", "o_sum", "o_root", "z_done", "own", "kg_out", "q_ready", "o_var"))
    conv, small = mix["conv"], mix["small"]
    ITER = 5
    G4 = UNITS // 2
    qT = conv[:, 0:4, :].rearrange("p h (a c) -> p (h a) c", a=HALVES)
    kT = conv[:, 4:8, :].rearrange("p h (a c) -> p (h a) c", a=HALVES)
    vT = conv[:, 8:12, :].rearrange("p h (a c) -> p (h a) c", a=HALVES)

    def over_units(ap):
        return ap.unsqueeze(1).to_broadcast([P, UNITS, P])

    with ExitStack() as ctx:
        halves, spare = Region(core.h_mem[:, :, :, :].rearrange("p k c s -> p (k c s)")), Region(mix["spare"])
        g_diag, b_diag, egrow, decay, attnT, TT = (halves.take(UNITS, P) for _ in range(6))
        pw = [halves.take(UNITS, P) for _ in range(2)]
        pt = [spare.take(UNITS, P) for _ in range(2)]
        kbg, kg, vb = (spare.take(UNITS, P) for _ in range(3))
        cols = core.sb("delta_cols", [P, 6, UNITS], F32, ctx)
        state = core.sb("delta_state", [P, HEADS, HD], F32, ctx)
        gcol, tot, ecol, kgs, bec, left = (cols[:, j, :] for j in range(6))
        pa, pb, pc, pd = (core.ps(f"delta_ps{n}", [P, UNITS, P], ctx) for n in "abcd")
        wT, u_sb = g_diag, b_diag
        v_new, oT = kbg, decay
        block = ctx.enter_context(nc.Block())
        g8 = small["g"][:, :, :].rearrange("p h a -> p (h a)")
        beta8 = small["beta"][:, :, :].rearrange("p h a -> p (h a)")

        @block.tensor
        def _(pe):
            nc.tensor.matmul(pa[:, 0, 0:UNITS], core.c("causal64"), g8, start=True, stop=True)
            nc.tensor.matmul(pa[:, 0, UNITS:2 * UNITS], core.c("block64"), g8, start=True, stop=True).then_inc(cols_done, 1)
            for n, (out, rhs) in enumerate(((pb, g_diag), (pc, b_diag))):
                pe.wait_ge(diag, n + 1)
                for g in range(2):
                    at = slice(G4 * g, G4 * g + G4)
                    last = nc.tensor.matmul(out[:, at, :], core.c("ones"), rhs[:, at, :], start=True, stop=True)
                last.then_inc(rows_done, 1)
            for u in range(UNITS):
                last = nc.tensor.matmul(pd[:, u, :], kT[:, u, :], kT[:, u, :], start=True, stop=True)
            last.then_inc(kk_done, 1)
            pe.wait_ge(cols_out, 1)
            for u in range(UNITS):
                last = nc.tensor.matmul(pa[:, u, :], kT[:, u, :], qT[:, u, :], start=True, stop=True)
            last.then_inc(qk_done, 1)
            pe.wait_ge(n_ready, 1)
            pe.wait_ge(ecols, 3)
            pe.wait_ge(diff_done, 1)
            for u in range(UNITS):
                last = nc.tensor.transpose(pb[:, u, :], pt[0][:, u, :], core.c("ident"))
            last.then_inc(nt_back, 1)
            pe.wait_ge(p_ready, 2)
            for u in range(UNITS):
                last = nc.tensor.transpose(pb[:, u, :], kT[:, u, :], core.c("ident"))
            last.then_inc(kt_done, 1)
            pe.wait_ge(n_ready, 2)
            for it in range(ITER):
                old = it % 2
                for g in range(2):
                    pe.wait_ge(p_ready, 2 * it + g + 1)
                    if it:
                        pe.wait_ge(pt_ready, 2 * (it - 1) + g + 1)
                    for u in range(G4 * g, G4 * g + G4):
                        last = nc.tensor.matmul(pa[:, u, :], pt[old][:, u, :], pw[old][:, u, :], start=True, stop=True)
                    last.then_inc(pp_done, 1)
                    if it < ITER - 1:
                        for u in range(G4 * g, G4 * g + G4):
                            last = nc.tensor.matmul(pc[:, u, :], pw[old][:, u, :], pt[old][:, u, :], start=True, stop=True)
                        last.then_inc(ppt_done, 1)
                for g in range(2):
                    pe.wait_ge(p_ready, 2 * (it + 1) + g + 1)
                    pe.wait_ge(tt_ready, 2 * it + g + 1)
                    for u in range(G4 * g, G4 * g + G4):
                        last = nc.tensor.matmul(pd[:, u, :], pw[1 - old][:, u, :], TT[:, u, :], start=True, stop=True)
                    last.then_inc(tt_done, 1)
            pe.wait_ge(k_out, 1)
            pe.wait_ge(kg_out, 1)
            for u in range(UNITS):
                last = nc.tensor.transpose(pb[:, u, :], vT[:, u, :], core.c("ident"))
            last.then_inc(vt_done, 1)
            pe.wait_ge(tt_ready, 2 * ITER + 2)
            for u in range(UNITS):
                last = nc.tensor.matmul(pa[:, u, :], kbg[:, u, :], TT[:, u, :], start=True, stop=True)
            last.then_inc(w_done, 1)
            pe.wait_ge(v_out, 1)
            for u in range(UNITS):
                last = nc.tensor.matmul(pc[:, u, :], TT[:, u, :], vb[:, u, :], start=True, stop=True)
            last.then_inc(w_done, 1)
            pe.wait_ge(w_out, 1)
            pe.wait_ge(u_out, 1)
            pe.wait_ge(q_ready, 1)
            for n in range(S // CHUNK):
                half, r = n // 2, n % 2
                rows = slice(CHUNK * r, CHUNK * r + CHUNK)
                pe.wait_ge(state_ready, n + 1)
                for h in range(HEADS):
                    last = nc.tensor.matmul(pd[rows, h, :], wT[:, 2 * h + half, rows], state[:, h, :],
                                            start=True, stop=True)
                last.then_inc(ws_done, 1)
                pe.wait_ge(vn_ready, n + 1)
                if n:
                    pe.wait_ge(o_out, n)
                for h in range(HEADS):
                    nc.tensor.matmul(pb[:, h, 0:CHUNK], state[:, h, :], qT[:, 2 * h + half, rows],
                                     start=True, stop=False)
                    last = nc.tensor.matmul(pb[:, h, 0:CHUNK], v_new[rows, h, :], attnT[rows, 2 * h + half, rows],
                                            start=False, stop=True)
                last.then_inc(o_done, 1)
                if n < S // CHUNK - 1:
                    for h in range(HEADS):
                        last = nc.tensor.matmul(pc[:, h, :], kg[rows, 2 * h + half, :], v_new[rows, h, :],
                                                start=True, stop=True)
                    last.then_inc(st_done, 1)
            pe.wait_ge(o_sq, 1)
            for g in range(2):
                at = slice(G4 * g, G4 * g + G4)
                last = nc.tensor.matmul(pa[:, at, :], core.c("ones"), pw[0][:, at, :], start=True, stop=True)
            last.then_inc(o_sum, 1)

        @block.scalar
        def _(act):
            act.wait_ge(cols_out, 2)
            nc.scalar.activation(ecol, gcol, ACT.Exp).then_inc(ecols, 1)
            nc.scalar.activation(kgs, left, ACT.Exp).then_inc(ecols, 1)
            act.wait_ge(diff_done, 1)
            nc.scalar.activation(egrow[:, :, :], pb[:, :, :], ACT.Exp).then_inc(ecols, 1)
            nc.scalar.activation(decay[:, :, :], decay[:, :, :], ACT.Exp).then_inc(decay_done, 1)
            act.wait_ge(nt_back, 1)
            for g in range(2):
                at = slice(G4 * g, G4 * g + G4)
                nc.scalar.activation(pw[0][:, at, :], pb[:, at, :], ACT.Copy).then_inc(p_ready, 1)
            act.wait_ge(kt_done, 1)
            act.wait_ge(masked, 2)
            for u in range(UNITS):
                last = nc.scalar.activation(kbg[:, u, :], pb[:, u, :], ACT.Copy, scale=bec[:, u:u + 1])
            last.then_inc(k_out, 1)
            for it in range(ITER):
                for g in range(2):
                    act.wait_ge(pp_done, 2 * it + g + 1)
                    at = slice(G4 * g, G4 * g + G4)
                    nc.scalar.activation(pw[1 - it % 2][:, at, :], pa[:, at, :], ACT.Copy).then_inc(p_ready, 1)
            act.wait_ge(vt_done, 1)
            for u in range(UNITS):
                last = nc.scalar.activation(vb[:, u, :], pb[:, u, :], ACT.Copy, scale=beta8[:, u:u + 1])
            last.then_inc(v_out, 1)
            act.wait_ge(w_done, 1)
            nc.scalar.activation(wT[:, :, :], pa[:, :, :], ACT.Copy).then_inc(w_out, 1)
            for n in range(S // CHUNK):
                act.wait_ge(o_done, n + 1)
                nc.scalar.activation(oT[:, :, :].rearrange("p (h a) c -> p h (a c)", a=HALVES)[:, :, n * CHUNK:(n + 1) * CHUNK],
                                     pb[:, 0:HEADS, 0:CHUNK], ACT.Copy).then_inc(o_out, 1)
            act.wait_ge(o_out, S // CHUNK)
            nc.scalar.activation(pw[0][:, :, :], oT[:, :, :], ACT.Square).then_inc(o_sq, 1)
            nc.scalar.activation(attnT[:, :, :].rearrange("p (h a) c -> p h (a c)", a=HALVES),
                                 proj[:, Z:Z + 4, PAD:PAD + S], ACT.Silu).then_inc(z_done, 1)
            act.wait_ge(o_var, 1)
            nc.scalar.activation(pw[1][:, :, :], TT[:, :, :], ACT.Abs_reciprocal_sqrt).then_inc(o_root, 1)

        @block.vector
        def _(dve):
            chain = Chain(dve, own)
            nc.vector.tensor_tensor(g_diag[:, :, :], over_units(core.c("causal64")),
                                    g8.unsqueeze(2).to_broadcast([P, UNITS, P]), ALU.mult).then_inc(diag, 1)
            nc.vector.tensor_tensor(b_diag[:, :, :], over_units(core.c("ident")),
                                    beta8.unsqueeze(2).to_broadcast([P, UNITS, P]), ALU.mult).then_inc(diag, 1)
            nc.vector.memset(state[:, :, :], 0.0).then_inc(state_ready, 1)
            dve.wait_ge(cols_done, 1)
            nc.vector.tensor_copy(cols[:, 0:2, :].rearrange("p a b -> p (a b)"), pa[:, 0, 0:2 * UNITS]).then_inc(cols_out, 1)
            dve.wait_ge(cols_out, 1)
            nc.vector.tensor_tensor(left, tot, gcol, ALU.subtract).then_inc(cols_out, 1)
            dve.wait_ge(rows_done, 1)
            for u in range(UNITS):
                last = nc.vector.tensor_scalar(decay[:, u, :], pb[:, u, :], gcol[:, u:u + 1], 0.0, ALU.subtract, ALU.min)
            last.then_inc(diff_done, 1)
            dve.wait_ge(decay_done, 1)
            nc.vector.tensor_tensor(decay[:, :, :], decay[:, :, :], over_units(core.c("causal64")), ALU.mult).then_inc(masked, 1)
            dve.wait_ge(ecols, 3)
            nc.vector.tensor_tensor(bec, beta8, ecol, ALU.mult).then_inc(masked, 1)
            dve.wait_ge(masked, 2)
            dve.wait_ge(kk_done, 1)
            chain.do(nc.vector.tensor_tensor(pt[0][:, :, :], pd[:, :, :], decay[:, :, :], ALU.mult))
            dve.wait_ge(rows_done, 2)
            chain.do(nc.vector.tensor_tensor(pt[0][:, :, :], pc[:, :, :], pt[0][:, :, :], ALU.mult))
            nc.vector.tensor_tensor(pt[0][:, :, :], pt[0][:, :, :], over_units(core.c("neg_strict64")), ALU.mult).then_inc(n_ready, 1)
            dve.wait_ge(qk_done, 1)
            nc.vector.tensor_tensor(attnT[:, :, :], pa[:, :, :], decay[:, :, :], ALU.mult).then_inc(n_ready, 1)
            dve.wait_ge(n_ready, 1)
            for g in range(2):
                at = slice(G4 * g, G4 * g + G4)
                nc.vector.tensor_tensor(TT[:, at, :], pt[0][:, at, :],
                                        core.c("ident").unsqueeze(1).to_broadcast([P, G4, P]), ALU.add).then_inc(tt_ready, 1)
            dve.wait_ge(k_out, 1)
            for u in range(UNITS):
                last = nc.vector.tensor_scalar(kg[:, u, :], pb[:, u, :], kgs[:, u:u + 1], None, ALU.mult)
            last.then_inc(kg_out, 1)
            nc.vector.tensor_tensor(qT, qT, egrow[:, :, :], ALU.mult).then_inc(q_ready, 1)
            for it in range(ITER):
                if it < ITER - 1:
                    for g in range(2):
                        at = slice(G4 * g, G4 * g + G4)
                        dve.wait_ge(ppt_done, 2 * it + g + 1)
                        nc.vector.tensor_copy(pt[1 - it % 2][:, at, :], pc[:, at, :]).then_inc(pt_ready, 1)
                for g in range(2):
                    at = slice(G4 * g, G4 * g + G4)
                    dve.wait_ge(tt_done, 2 * it + g + 1)
                    dve.wait_ge(tt_ready, 2 * it + g + 1)
                    nc.vector.tensor_tensor(TT[:, at, :], pd[:, at, :], TT[:, at, :], ALU.add).then_inc(tt_ready, 1)
            dve.wait_ge(w_done, 2)
            nc.vector.tensor_copy(u_sb[:, :, :], pc[:, :, :]).then_inc(u_out, 1)
            u_by = u_sb[:, :, :].rearrange("p (h a) d -> p h a d", a=HALVES)
            for n in range(S // CHUNK):
                half, r = n // 2, n % 2
                rows = slice(CHUNK * r, CHUNK * r + CHUNK)
                dve.wait_ge(ws_done, n + 1)
                if n == 0:
                    dve.wait_ge(u_out, 1)
                nc.vector.tensor_tensor(v_new[rows, 0:HEADS, :], u_by[rows, :, half, :], pd[rows, 0:HEADS, :],
                                        ALU.subtract).then_inc(vn_ready, 1)
                if n < S // CHUNK - 1:
                    dve.wait_ge(st_done, n + 1)
                    for h in range(HEADS):
                        end = egrow[:, 2 * h + half, CHUNK * r + CHUNK - 1:CHUNK * r + CHUNK]
                        last = nc.vector.scalar_tensor_tensor(state[:, h, :], state[:, h, :], end, pc[:, h, :],
                                                              ALU.mult, ALU.add)
                    last.then_inc(state_ready, 1)
                    dve.wait_ge(state_ready, n + 2)
            dve.wait_ge(o_sum, 1)
            nc.vector.tensor_scalar(TT[:, :, :], pa[:, :, :], 1.0 / HD, EPS, ALU.mult, ALU.add).then_inc(o_var, 1)
            dve.wait_ge(o_root, 1)
            newton_rsqrt(nc, chain, pw[1][:, :, :], TT[:, :, :], pt[0][:, :, :])
            chain.do(nc.vector.tensor_tensor(pw[1][:, :, :], pw[1][:, :, :], oT[:, :, :], ALU.mult))
            dve.wait_ge(z_done, 1)
            chain.do(nc.vector.scalar_tensor_tensor(
                proj[:, Z:Z + 4, PAD:PAD + S], pw[1][:, :, :].rearrange("p (h a) c -> p h (a c)", a=HALVES), core.v("gdn_norm"),
                attnT[:, :, :].rearrange("p (h a) c -> p h (a c)", a=HALVES), ALU.mult, ALU.mult))


def other_mixers_stage(core, proj, mix):
    nc = core.nc
    (weights_in, w_ready, w_zero, rx_done, gates_done, log_ready, exps_done, square_arg, root_done, lru_done, gelu_done,
     mean_done, centred, var_sq, var_done, var_root, v_ready, vt_done, vt_out, sg_done, own, sc_own, sc_done, sq_done,
     sum_done, root3, var_ready) = (
        core.sem(f"mix_{s}") for s in (
            "weights_in", "w_ready", "w_zero", "rx_done", "gates_done", "log_ready", "exps_done", "square_arg",
            "root_done", "lru_done", "gelu_done", "mean_done", "centred", "var_sq", "var_done", "var_root", "v_ready",
            "vt_done", "vt_out", "sg_done", "own", "sc_own", "sc_done", "sq_done", "sum_done", "root3", "var_ready"))
    conv, small, rows = mix["conv"], mix["small"], mix["rows"]
    xc = conv[:, 12:16, :]
    with ExitStack() as ctx:
        halves, spare = Region(core.h_mem[:, :, :, :].rearrange("p k c s -> p (k c s)")), Region(mix["spare"])
        lru_w = spare.take(2, 4, P)
        sgu_w = spare.take(4, P)
        bufs = halves.take(4, 4, S)
        a_, r_, i_, t_ = (bufs[:, j, :, :] for j in range(4))
        gelu_u, gelu_v = (proj[:, at:at + 4, PAD:] for at in (SGU_U, SGU_V))
        outs = [proj[:, at:at + 4, PAD:] for at in MIXED]
        padded = halves.take(4, PAD + S)
        stat, tmp, root = (spare.take(3, S) for _ in range(3))
        gelu_g = conv[:, 0:4, :]
        vtok = conv[:, 4:8, :]
        sq = bufs
        p_r = core.ps("ps_r", [P, 4, S], ctx)
        p_x = core.ps("ps_x", [P, 4, S], ctx)
        p_s = core.ps("ps_stat", [P, 2, S], ctx)
        p_n = core.ps("ps_norms", [P, 4, S], ctx)
        block = ctx.enter_context(nc.Block())
        bs = rows[:, 8:8 + 512].rearrange("p (g t) -> p g t", g=4)

        def quarter(ap):
            return ap.rearrange("p j s -> p (j s)").rearrange("p (u c) -> p u c", c=P)

        vt, p_vt, p_sg = quarter(vtok), quarter(p_r[:, :, :]), quarter(p_x[:, :, :])

        @block.sync
        def _(sp):
            sp.wait_ge(w_zero, 1)
            for m, name in enumerate(("lru_wa", "lru_wx")):
                src = core.d[name].rearrange("(j b) i o -> b i j o", b=2)
                for b in range(2):
                    at = slice(64 * b, 64 * b + 64)
                    sp.dma_start(lru_w[at, m, :, at], src[b]).then_inc(weights_in, 16)
            sp.dma_start(sgu_w[:, :, :], core.d["sgu_ws"]).then_inc(weights_in, 16)

        @block.gpsimd
        def _(pool):
            nc.gpsimd.memset(lru_w[:, :, :, :], 0.0).then_inc(w_zero, 1)
            steps = Chain(pool, sc_own)
            steps.add(nc.gpsimd.memset(padded[:, :, 0:PAD], 0.0))
            steps.do(nc.gpsimd.tensor_tensor(padded[:, :, PAD:], proj[:, SC_C:SC_C + 4, PAD:], proj[:, SC_H:SC_H + 4, PAD:],
                                             ALU.mult))
            out = outs[3]
            tap = conv[:, 8:12, :]
            for o in range(3):
                for j in range(4):
                    steps.add(nc.gpsimd.tensor_scalar((tap if o else out)[:, j, :], padded[:, j, PAD - o:PAD - o + S],
                                                      core.v("sconv", 3 * j + 2 - o), None, ALU.mult))
                steps.settle()
                if o:
                    steps.do(nc.gpsimd.tensor_tensor(out, out, tap, ALU.add))
            nc.gpsimd.tensor_tensor(out, out, proj[:, SC_B:SC_B + 4, PAD:], ALU.mult).then_inc(sc_done, 1)

        @block.tensor
        def _(pe):
            pe.wait_ge(weights_in, 80)
            for m, out in enumerate((p_r, p_x)):
                for j in range(4):
                    last = nc.tensor.matmul(out[:, j, :], lru_w[:, m, j, :], xc[:, j, :], start=True, stop=True)
                last.then_inc(rx_done, 1)
            pe.wait_ge(gelu_done, 2)
            for j in range(4):
                last = nc.tensor.matmul(p_s[:, 0, :], core.c("ones"), gelu_v[:, j, :], start=(j == 0), stop=(j == 3))
            last.then_inc(mean_done, 1)
            pe.wait_ge(var_sq, 1)
            for j in range(4):
                last = nc.tensor.matmul(p_s[:, 1, :], core.c("ones"), t_[:, j, :], start=(j == 0), stop=(j == 3))
            last.then_inc(var_done, 1)
            pe.wait_ge(v_ready, 1)
            pe.wait_ge(gates_done, 8)
            for g in range(4):
                for half in range(HALVES):
                    last = nc.tensor.transpose(p_vt[:, 2 * g + half, :], gelu_v[:, g, half * P:(half + 1) * P],
                                               core.c("ident"))
            last.then_inc(vt_done, 1)
            pe.wait_ge(vt_out, 1)
            pe.wait_ge(w_ready, 1)
            for g in range(4):
                for half in range(HALVES):
                    last = nc.tensor.matmul(p_sg[:, 2 * g + half, :], vt[:, 2 * g + half, :], sgu_w[:, g, :],
                                            start=True, stop=True)
            last.then_inc(sg_done, 1)
            for m in range(3):
                pe.wait_ge(sq_done, m + 1)
                for j in range(4):
                    last = nc.tensor.matmul(p_n[:, m, :], core.c("ones"), sq[:, m, j, :], start=(j == 0), stop=(j == 3))
                last.then_inc(sum_done, 1)

        @block.scalar
        def _(act):
            nc.scalar.activation(gelu_v, proj[:, SGU_V:SGU_V + 4, PAD:], ACT.Gelu_apprx_tanh).then_inc(gelu_done, 1)
            nc.scalar.activation(gelu_u, proj[:, SGU_U:SGU_U + 4, PAD:], ACT.Gelu_apprx_tanh).then_inc(gelu_done, 1)
            nc.scalar.activation(gelu_g, proj[:, LRU_G:LRU_G + 4, PAD:], ACT.Gelu_apprx_tanh).then_inc(gelu_done, 1)
            for m, (src, dst, bias) in enumerate(((p_r, r_, "lru_ba"), (p_x, i_, "lru_bx"))):
                act.wait_ge(rx_done, m + 1)
                for j in range(4):
                    nc.scalar.activation(dst[:, j, :], src[:, j, :], ACT.Sigmoid, bias=core.v(bias, j)).then_inc(gates_done, 1)
            act.wait_ge(log_ready, 1)
            nc.scalar.activation(a_, r_, ACT.Exp).then_inc(exps_done, 1)
            nc.scalar.activation(r_, r_, ACT.Tanh).then_inc(exps_done, 1)
            act.wait_ge(centred, 1)
            nc.scalar.activation(t_, gelu_v, ACT.Square).then_inc(var_sq, 1)
            act.wait_ge(square_arg, 1)
            nc.scalar.activation(r_, r_, ACT.Sqrt).then_inc(root_done, 1)
            act.wait_ge(var_ready, 1)
            nc.scalar.activation(root[:, 0, :], stat[:, 1, :], ACT.Abs_reciprocal_sqrt).then_inc(var_root, 1)
            act.wait_ge(vt_done, 1)
            nc.scalar.activation(vt, p_vt, ACT.Copy).then_inc(vt_out, 1)
            for m, ready in enumerate((lru_done, lru_done, sc_done)):
                act.wait_ge(ready, (1, 2, 1)[m])
                nc.scalar.activation(sq[:, m, :, :], outs[1 + m], ACT.Square).then_inc(sq_done, 1)
            act.wait_ge(var_ready, 2)
            nc.scalar.activation(root[:, :, :], stat[:, :, :], ACT.Abs_reciprocal_sqrt).then_inc(root3, 1)

        @block.vector
        def _(dve):
            chain = Chain(dve, own)

            def each_tile(ap):
                return ap.unsqueeze(1).to_broadcast([P, 4, S])

            dve.wait_ge(weights_in, 80)
            nc.vector.tensor_tensor(sgu_w[:, :, :], sgu_w[:, :, :], core.c("causal128").unsqueeze(1).to_broadcast([P, 4, P]),
                                    ALU.mult).then_inc(w_ready, 1)
            dve.wait_ge(gates_done, 8)
            for j in range(4):
                last = nc.vector.tensor_scalar(r_[:, j, :], r_[:, j, :], small["lru_c"][:, j:j + 1], None, ALU.mult)
            last.then_inc(log_ready, 1)
            chain.do(nc.vector.tensor_tensor(i_, i_, xc, ALU.mult))
            dve.wait_ge(mean_done, 1)
            chain.do(nc.vector.tensor_scalar(stat[:, 0, :], p_s[:, 0, :], 1.0 / 512, None, ALU.mult))
            nc.vector.tensor_tensor(gelu_v, gelu_v, each_tile(stat[:, 0, :]), ALU.subtract).then_inc(centred, 1)
            dve.wait_ge(exps_done, 2)
            dve.wait_ge(var_sq, 1)
            dve.wait_ge(var_done, 1)
            chain.do(nc.vector.tensor_tensor(t_, a_, a_, ALU.mult))
            chain.do(nc.vector.scalar_tensor_tensor(r_, t_, 1.0, r_, ALU.add, ALU.mult))
            nc.vector.tensor_scalar(r_, r_, -1.0, 1e-34, ALU.mult, ALU.max).then_inc(square_arg, 1)
            nc.vector.tensor_scalar(stat[:, 1, :], p_s[:, 1, :], 1.0 / 512, EPS, ALU.mult, ALU.add).then_inc(var_ready, 1)
            dve.wait_ge(var_root, 1)
            newton_rsqrt(nc, chain, root[:, 0, :], stat[:, 1, :], tmp[:, 0, :])
            for j in range(4):
                chain.add(nc.vector.scalar_tensor_tensor(gelu_v[:, j, :], gelu_v[:, j, :], core.v("ln_w", j), root[:, 0, :],
                                                         ALU.mult, ALU.mult))
            chain.settle()
            for j in range(4):
                last = nc.vector.tensor_scalar(gelu_v[:, j, :], gelu_v[:, j, :], core.v("ln_b", j), None, ALU.add)
            last.then_inc(v_ready, 1)
            dve.wait_ge(root_done, 1)
            chain.do(nc.vector.tensor_tensor(i_, i_, r_, ALU.mult))
            for j in range(4):
                chain.add(nc.vector.tensor_tensor_scan(t_[:, j, :], a_[:, j, :], i_[:, j, :], 0.0, ALU.mult, ALU.add))
            chain.settle()
            dve.wait_ge(gelu_done, 3)
            nc.vector.tensor_tensor(outs[1], t_, gelu_g, ALU.mult).then_inc(lru_done, 1)
            dve.wait_ge(sg_done, 1)
            chain.do(nc.vector.tensor_tensor(
                gelu_v.rearrange("p g (a c) -> p g a c", a=HALVES), p_sg.rearrange("p (g a) c -> p g a c", a=HALVES),
                bs.unsqueeze(2).to_broadcast([P, 4, HALVES, P]), ALU.add))
            nc.vector.tensor_tensor(outs[2], gelu_v, gelu_u, ALU.mult).then_inc(lru_done, 1)
            dve.wait_ge(sum_done, 3)
            nc.vector.tensor_scalar(stat[:, :, :], p_n[:, 0:3, :], 1.0 / 512, EPS, ALU.mult, ALU.add).then_inc(var_ready, 1)
            dve.wait_ge(root3, 1)
            newton_rsqrt(nc, chain, root[:, :, :], stat[:, :, :], tmp[:, :, :])
            for m in range(3):
                for j in range(4):
                    out = outs[1 + m][:, j, :]
                    nc.vector.scalar_tensor_tensor(out, out, core.v("grp", 4 * m + j), root[:, m, :],
                                                   ALU.mult, ALU.mult)



DQ, DK, FQ, FK, DV, FV, G_DIL, G_DIFF = 0, 12, 24, 32, 40, 52, 60, 76
MIX_TILES = 92
MIX_ORDER = [*range(0, 24), *range(36, 52), *range(24, 36), *range(52, 92)]
GROUPS = 3
ROPE = 32
ROPE_THETA = 500000.0
DILATIONS = ((128, 1), (512, 4), (2048, 16))
LAM_INIT = 0.8 - 0.6 * float(np.exp(-0.3 * 0))
MASKED = -1e30
TWO_PI = (6.28125, 0.0019350051879882812, 3.0199159819567e-07)
ROUND = 1.5 * 2.0 ** 23


def rotary_stage(core, trig, lam):
    nc = core.nc
    pos_in, own, angle, dot_done, dot_in, exp_done = (
        core.sem(f"rotary_{s}") for s in ("pos_in", "own", "angle", "dot_done", "dot_in", "exp_done"))
    with ExitStack() as ctx:
        pos_i = core.sb("pos_i", [ROPE, S], I32, ctx)
        ang = core.sb("rotary_angle", [ROPE, S], F32, ctx)
        turns = core.sb("rotary_turns", [ROPE, 2, S], F32, ctx)
        dots = core.sb("lam_dots", [P, 2], F32, ctx)
        exps = core.sb("lam_exps", [P, 2], F32, ctx)
        p_dot = core.ps("ps_dot", [P, 2], ctx)
        block = ctx.enter_context(nc.Block())

        @block.sync
        def _(sp):
            sp.dma_start(pos_i[:, :], core.d["positions"].partition_broadcast(ROPE)).then_inc(pos_in, 16)

        @block.vector
        def _(dve):
            chain = Chain(dve, own)
            lq = core.v("lam", 0, 4)
            nc.vector.tensor_tensor(dots[:, 0:1], lq[:, 0:1], lq[:, 1:2], ALU.mult).then_inc(dot_in, 1)
            nc.vector.tensor_tensor(dots[:, 1:2], lq[:, 2:3], lq[:, 3:4], ALU.mult).then_inc(dot_in, 1)
            dve.wait_ge(pos_in, 16)
            chain.do(nc.vector.tensor_copy(ang[:, :], pos_i[:, :]))
            chain.do(nc.vector.tensor_scalar(ang[:, :], ang[:, :], core.c("inv_freq")[0:ROPE, :], None, ALU.mult))
            for j, ahead in enumerate((0.25, 0.0)):
                chain.do(nc.vector.tensor_scalar(turns[:, j, :], ang[:, :], 0.5 / float(np.pi), ahead, ALU.mult, ALU.add))
            chain.do(nc.vector.tensor_scalar(turns[:, :, :], turns[:, :, :], ROUND, None, ALU.add))
            chain.do(nc.vector.tensor_scalar(turns[:, :, :], turns[:, :, :], -ROUND, None, ALU.add))
            for j in range(2):
                chain.do(nc.vector.scalar_tensor_tensor(trig[:, j, :], turns[:, j, :], -TWO_PI[0], ang[:, :],
                                                        ALU.mult, ALU.add))
            for part in TWO_PI[1:]:
                chain.do(nc.vector.scalar_tensor_tensor(trig[:, :, :], turns[:, :, :], -part, trig[:, :, :],
                                                        ALU.mult, ALU.add))
            chain.do(nc.vector.tensor_scalar(trig[:, 0, :], trig[:, 0, :], float(np.pi / 2), None, ALU.add))
            nc.vector.tensor_scalar(trig[:, :, :], trig[:, :, :], 3.1415925, -3.1415925, ALU.min, ALU.max).then_inc(angle, 1)
            dve.wait_ge(angle, 2)
            nc.vector.tensor_scalar(trig[:, 1, :], trig[:, 1, :], core.c("rope_sign")[0:ROPE, :], None, ALU.mult)
            dve.wait_ge(exp_done, 1)
            chain.do(nc.vector.tensor_tensor(lam[:, 0:1], exps[:, 0:1], exps[:, 1:2], ALU.subtract))
            chain.do(nc.vector.tensor_scalar(lam[:, 0:1], lam[:, 0:1], LAM_INIT, None, ALU.add))
            nc.vector.tensor_scalar(lam[:, 1:3], core.v("subln", 0, 2), 1.0 - LAM_INIT, None, ALU.mult)

        @block.tensor
        def _(pe):
            pe.wait_ge(dot_in, 2)
            nc.tensor.matmul(p_dot[:, :], core.c("ones"), dots[:, :], start=True, stop=True).then_inc(dot_done, 1)

        @block.scalar
        def _(act):
            act.wait_ge(angle, 1)
            nc.scalar.activation(trig[:, :, :], trig[:, :, :], ACT.Sin).then_inc(angle, 1)
            act.wait_ge(dot_done, 1)
            nc.scalar.activation(exps[:, :], p_dot[:, :], ACT.Exp).then_inc(exp_done, 1)


def mix_in_stage(core, prod, operand_of, proj, trig, following):
    nc = core.nc
    kept, squared, summed, var_ready, rooted, own, normed, pool_own, vt_done, vt_out, rotated, swapped, back = (
        core.sem(f"heads_{s}") for s in ("x_kept", "squared", "summed", "var_ready", "rooted", "own", "normed", "pool_own",
                                         "vt_done", "vt_out", "rotated", "swapped", "back"))
    QK_BODIES, V_BODIES = DV // 2, (G_DIL - DV) // 2
    with ExitStack() as ctx:
        acc = core.ps(f"acc_{core.chunk}", [P, 2, 2, S], ctx)
        p_sq = core.ps("ps_heads_sq", [P, 2, S], ctx)
        p_v = core.ps("ps_heads_v", [P, 4, P], ctx)
        y, var, tmp, swap, root = (core.x[:, 2 * j:2 * j + 2, :] for j in (0, 1, 2, 3, 5))
        swap = swap[0:ROPE, :, :]
        values = core.x[:, 8:10, :]
        operand = operand_of(ctx)
        scale = operand.scale
        block = ctx.enter_context(nc.Block())

        def pair(m):
            return proj[:, bass.ds(2 * m, 2), :]

        def body_scaled(eng, m):
            eng.wait_ge(core.z_free, m * 2 + (2 + core.scaled + 2))

        @block.sync
        def _(sp):
            sp.dma_start(core.d["x_kept"], core.x[:, :, :]).then_inc(kept, 16)
            stream(core, sp, prod, following)

        @block.scalar
        def _(act):
            def walk(lo, hi):
                return steps(core, act, prod, split_high, lo, hi, following=following if hi == prod.bodies else None)

            for i, t in walk(0, 1):
                take_cross(core, act, prod, acc, i, t)
                if t == 0:
                    scale.root(act)
            act.wait_ge(kept, 16)
            act.sem_inc(back, 1)

            def head_step(i, t):
                if t == 0:
                    body_scaled(act, i - 1)
                    act.wait_ge(normed, i)
                    core.carry_wait(act)
                    nc.scalar.activation(root, pair(i - 1), ACT.Square).then_inc(squared, 1)
                else:
                    act.wait_ge(var_ready, i)
                    nc.scalar.activation(root, var, ACT.Abs_reciprocal_sqrt).then_inc(rooted, 1)

            def put_back(i):
                act.wait_ge(rotated, i - 1)
                core.carry_wait(act)
                nc.scalar.activation(pair(i - 2), y, ACT.Copy).then_inc(back, 1)

            def value_step(i, t):
                if t == 1:
                    act.wait_ge(vt_done, i - (QK_BODIES - 1))
                    core.carry_wait(act)
                    nc.scalar.activation(pair(i - 1), p_v[:, :, :].rearrange("p (j b) c -> p j (b c)", b=2),
                                         ACT.Copy).then_inc(vt_out, 1)

            for i, t in walk(1, 2):
                head_step(i, t)
                take_cross(core, act, prod, acc, i, t)
            for i, t in walk(2, 1 + QK_BODIES):
                if t == 1:
                    put_back(i)
                head_step(i, t)
                take_cross(core, act, prod, acc, i, t)
            for i, t in walk(1 + QK_BODIES, 2 + QK_BODIES):
                if t == 1:
                    put_back(i)
                value_step(i, t)
                take_cross(core, act, prod, acc, i, t)
            for i, t in walk(2 + QK_BODIES, 1 + QK_BODIES + V_BODIES):
                value_step(i, t)
                take_cross(core, act, prod, acc, i, t)
            for i, t in walk(1 + QK_BODIES + V_BODIES, prod.bodies):
                take_cross(core, act, prod, acc, i, t)

        @block.vector
        def _(dve):
            def walk(lo, hi):
                return steps(core, dve, prod, split_low, lo, hi, following=following if hi == prod.bodies else None)

            dve.sem_inc(normed, 1)
            for i, t in walk(0, 1):
                take_for_scaling(core, dve, prod, acc, i, t)
                if t == 0:
                    scale.variance(dve)
                    scale.refine(dve)
            for i, t in walk(1, 1 + QK_BODIES):
                if t == 1:
                    dve.wait_ge(summed, i)
                    nc.vector.tensor_scalar(var, p_sq[:, :, :], 1.0 / HD, EPS, ALU.mult, ALU.add).then_inc(var_ready, 1)
                take_for_scaling(core, dve, prod, acc, i, t)
                if t == 1:
                    here = pair(i - 1)
                    dve.wait_ge(rooted, i)
                    nc.vector.tensor_tensor(tmp, root, root, ALU.mult).then_inc(own, 1)
                    dve.wait_ge(own, i * 3 - 2)
                    nc.vector.scalar_tensor_tensor(tmp, tmp, -0.5, var, ALU.mult, ALU.mult).then_inc(own, 1)
                    dve.wait_ge(own, i * 3 - 1)
                    nc.vector.scalar_tensor_tensor(root, tmp, 1.5, root, ALU.add, ALU.mult).then_inc(own, 1)
                    dve.wait_ge(own, i * 3)
                    dve.wait_ge(back, i)
                    nc.vector.scalar_tensor_tensor(y, here, core.v("head_gain", i - 1), root, ALU.mult,
                                                   ALU.mult).then_inc(normed, 1)
                    dve.wait_ge(normed, i + 1)
                    core.carry_wait(dve)
                    nc.vector.stream_shuffle(swap.rearrange("p j s -> p (j s)"), y[0:ROPE, :, :].rearrange("p j s -> p (j s)"),
                                             [(p + ROPE // 2) % ROPE for p in range(ROPE)]).then_inc(swapped, 1)
            for i, t in walk(1 + QK_BODIES, prod.bodies):
                take_for_scaling(core, dve, prod, acc, i, t)

        @block.gpsimd
        def _(pool):
            def each(ap):
                return ap.unsqueeze(1).to_broadcast([ROPE, 2, S])

            pool.sem_inc(vt_out, 1)
            pool.sem_inc(vt_done, 1)

            def scale_body(i):
                for t in range(2):
                    scale_tile(core, pool, prod, proj[:, 2 * i + t, :], i, t)

            def scale_values(i):
                pool.wait_ge(vt_done, i - (QK_BODIES - 1))
                for t in range(2):
                    scale_tile(core, pool, prod, values[:, t, :], i, t)

            def rotate(i):
                here = y[0:ROPE, :, :]
                pool.wait_ge(swapped, i)
                nc.gpsimd.tensor_tensor(swap, swap, each(trig[:, 1, :]), ALU.mult).then_inc(pool_own, 1)
                nc.gpsimd.tensor_tensor(here, here, each(trig[:, 0, :]), ALU.mult).then_inc(pool_own, 1)
                pool.wait_ge(pool_own, i * 2)
                nc.gpsimd.tensor_tensor(here, here, swap, ALU.add).then_inc(rotated, 1)

            scale.ready(pool)
            scale_body(0)
            with pool.Fori(1, QK_BODIES) as i:
                scale_body(i)
                rotate(i)
            scale_values(QK_BODIES)
            rotate(QK_BODIES)
            with pool.Fori(QK_BODIES + 1, QK_BODIES + V_BODIES) as i:
                scale_values(i)
            with pool.Fori(QK_BODIES + V_BODIES, prod.bodies) as i:
                scale_body(i)

        @block.tensor
        def _(pe):
            for i, t in pe_steps(core, pe, prod, acc, 0, 1, before=operand.on(pe)):
                if t == 0:
                    operand.after_first(pe)
            for i, t in pe_steps(core, pe, prod, acc, 1, 1 + QK_BODIES):
                if t == 0:
                    pe.wait_ge(squared, i)
                    nc.tensor.matmul(p_sq[:, :, :], core.c("ones"), root, start=True, stop=True).then_inc(summed, 1)
            for i, t in pe_steps(core, pe, prod, acc, 1 + QK_BODIES, 1 + QK_BODIES + V_BODIES):
                if t == 0:
                    body_scaled(pe, i - 1)
                    pe.wait_ge(vt_out, i - QK_BODIES)
                    for j in range(2):
                        for half in range(HALVES):
                            last = nc.tensor.transpose(p_v[:, 2 * j + half, :], values[:, j, half * P:(half + 1) * P],
                                                       core.c("ident"))
                    last.then_inc(vt_done, 1)
            for _ in pe_steps(core, pe, prod, acc, 1 + QK_BODIES + V_BODIES):
                pass
    operand.passed()
    passed(core, prod, scaled=True)


def attention_stage(core, proj, lam):
    nc = core.nc
    (masks_in, scores_done, logits, max_ready, exp_done, probs_ready, pt_done, pt_out, pv_done, out_done, own,
     sq_ready, sum_done, var_ready, rooted) = (
        core.sem(f"attn_{s}") for s in ("masks_in", "scores_done", "logits", "max_ready", "exp_done", "probs_ready",
                                        "pt_done", "pt_out", "pv_done", "out_done", "own", "sq_ready", "sum_done",
                                        "var_ready", "rooted"))
    SCALE = HD ** -0.5
    units = [(False, h, a) for h in range(HEADS) for a in range(HALVES)] + \
            [(True, h, a) for h in range(HEADS) for a in range(HALVES)]

    def parts_of(diff):
        return 2 if diff else GROUPS

    def exps_through(n):
        return sum(2 if units[m][0] else 1 for m in range(n + 1))

    with ExitStack() as ctx:
        spare = Region(core.x[:, :, :].rearrange("p k s -> p (k s)"))
        masks = spare.take(HALVES, 4, S)
        s_buf = spare.take(2, GROUPS, S)
        pT = Region(core.h_mem[:, :, :, :].rearrange("p k c s -> p (k c s)")).take(2, 2 * GROUPS, P)
        stats = core.sb("attn_stats", [P, 2, 8], F32, ctx)
        p_s = core.ps("ps_scores", [P, 2, 4, S], ctx)
        p_t = core.ps("ps_probs_T", [P, 8, P], ctx)
        p_o = core.ps("ps_out", [P, 2, 4, P], ctx)
        block = ctx.enter_context(nc.Block())

        @block.sync
        def _(sp):
            sp.dma_start(masks[:, :, :, :], core.d["masks"]).then_inc(masks_in, 16)

        def q_tile(diff, h, j):
            return FQ + 2 * h + j if diff else DQ + 4 * j + h

        def k_tile(diff, h, j):
            return FK + 2 * h + j if diff else DK + 4 * j + h

        def out_tile(diff, h, e):
            return FQ + 2 * h + e if diff else DQ + h

        @block.tensor
        def _(pe):
            def scores(n):
                diff, h, a = units[n]
                if n >= 2:
                    pe.wait_ge(logits, n - 1)
                for j in range(parts_of(diff)):
                    last = nc.tensor.matmul(p_s[:, n % 2, j, 0:(a + 1) * P], proj[:, q_tile(diff, h, j), a * P:(a + 1) * P],
                                            proj[:, k_tile(diff, h, j), 0:(a + 1) * P], start=True, stop=True)
                last.then_inc(scores_done, 1)

            scores(0)
            for n, (diff, h, a) in enumerate(units):
                if n + 1 < len(units):
                    scores(n + 1)
                pe.wait_ge(probs_ready, n + 1)
                if n:
                    pe.wait_ge(pt_out, n)
                n_mats = 1 if diff else GROUPS
                for j in range(n_mats):
                    for b in range(a + 1):
                        last = nc.tensor.transpose(p_t[:, j * 2 + b, :], s_buf[:, n % 2, j, b * P:(b + 1) * P], core.c("ident"))
                last.then_inc(pt_done, 1)
                pe.wait_ge(pt_out, n + 1)
                if n >= 2:
                    pe.wait_ge(out_done, n - 1)
                terms = [(j, b) for j in range(n_mats) for b in range(a + 1)]
                for e in range(2 if diff else 1):
                    for m, (j, b) in enumerate(terms):
                        v = FV + 2 * h + e if diff else DV + 4 * j + h
                        last = nc.tensor.matmul(p_o[:, n % 2, e, :], proj[:, v, b * P:(b + 1) * P], pT[:, n % 2, j * 2 + b, :],
                                                start=(m == 0), stop=(m == len(terms) - 1))
                last.then_inc(pv_done, 1)
            pe.wait_ge(sq_ready, 1)
            for h in range(HEADS):
                for e in range(2):
                    last = nc.tensor.matmul(p_s[:, 0, h, :], core.c("ones"), proj[:, FK + 2 * h + e, :],
                                            start=(e == 0), stop=(e == 1))
            last.then_inc(sum_done, 1)

        @block.scalar
        def _(act):
            def exps(n):
                diff, _, a = units[n]
                act.wait_ge(max_ready, n + 1)
                s, st = s_buf[:, n % 2, :, :], stats[:, n % 2, :]
                if diff:
                    for j in range(2):
                        nc.scalar.activation(s[:, j, 0:(a + 1) * P], s[:, j, 0:(a + 1) * P], ACT.Exp, bias=st[:, 2 + j:3 + j],
                                             scale=SCALE, accum_out=st[:, 4 + j:5 + j]).then_inc(exp_done, 1)
                else:
                    nc.scalar.activation(s[:, :, 0:(a + 1) * P], s[:, :, 0:(a + 1) * P], ACT.Exp, bias=st[:, 2:3],
                                         scale=SCALE, accum_out=st[:, 4:5]).then_inc(exp_done, 1)

            exps(0)
            for n, (diff, h, a) in enumerate(units):
                if n + 1 < len(units):
                    exps(n + 1)
                act.wait_ge(pt_done, n + 1)
                if n >= 2:
                    act.wait_ge(pv_done, n - 1)
                n_mats = 1 if diff else GROUPS
                nc.scalar.activation(pT[:, n % 2, :, :].rearrange("p (j b) c -> p j b c", b=2)[:, 0:n_mats, 0:a + 1, :],
                                     p_t[:, 0:2 * GROUPS, :].rearrange("p (j b) c -> p j b c", b=2)[:, 0:n_mats, 0:a + 1, :],
                                     ACT.Copy).then_inc(pt_out, 1)
                act.wait_ge(pv_done, n + 1)
                ne = 2 if diff else 1
                t = out_tile(diff, h, 0)
                nc.scalar.activation(proj[:, t:t + ne, a * P:(a + 1) * P], p_o[:, n % 2, 0:ne, :], ACT.Copy).then_inc(out_done, 1)
            act.wait_ge(out_done, len(units))
            nc.scalar.activation(proj[:, FK:FK + 8, :], proj[:, FQ:FQ + 8, :], ACT.Square).then_inc(sq_ready, 1)
            act.wait_ge(var_ready, 1)
            nc.scalar.activation(proj[:, FK:FK + 4, :], proj[:, FK + 4:FK + 8, :], ACT.Abs_reciprocal_sqrt).then_inc(rooted, 1)

        @block.vector
        def _(dve):
            chain = Chain(dve, own)
            dve.wait_ge(masks_in, 16)

            def logits_of(n):
                diff, _, a = units[n]
                keys = (a + 1) * P
                s, st = s_buf[:, n % 2, :, :], stats[:, n % 2, :]
                dve.wait_ge(scores_done, n + 1)
                if n >= 2:
                    dve.wait_ge(pt_done, n - 1)
                nj = parts_of(diff)
                mask = masks[:, a, 3:4, 0:keys].to_broadcast([P, 2, keys]) if diff else masks[:, a, 0:GROUPS, 0:keys]
                nc.vector.tensor_tensor(s[:, 0:nj, 0:keys], p_s[:, n % 2, 0:nj, 0:keys], mask, ALU.add).then_inc(logits, 1)
                dve.wait_ge(logits, n + 1)
                if diff:
                    chain.do(nc.vector.reduce_max(st[:, 0:2], s[:, 0:2, 0:keys], AX))
                    nc.vector.tensor_scalar(st[:, 2:4], st[:, 0:2], -SCALE, None, ALU.mult).then_inc(max_ready, 1)
                else:
                    chain.do(nc.vector.tensor_reduce(st[:, 0:1], s[:, 0:nj, 0:keys], mybir.AxisListType.XY, ALU.max))
                    nc.vector.tensor_scalar(st[:, 2:3], st[:, 0:1], -SCALE, None, ALU.mult).then_inc(max_ready, 1)

            logits_of(0)
            for n, (diff, h, a) in enumerate(units):
                if n + 1 < len(units):
                    logits_of(n + 1)
                keys = (a + 1) * P
                s, st = s_buf[:, n % 2, :, :], stats[:, n % 2, :]
                dve.wait_ge(exp_done, exps_through(n))
                if diff:
                    chain.do(nc.vector.reciprocal(st[:, 6:8], st[:, 4:6]))
                    chain.do(nc.vector.tensor_tensor(st[:, 7:8], st[:, 7:8], lam[:, 0:1], ALU.mult))
                    chain.do(nc.vector.tensor_scalar(s[:, 1, 0:keys], s[:, 1, 0:keys], st[:, 7:8], None, ALU.mult))
                    nc.vector.scalar_tensor_tensor(s[:, 0, 0:keys], s[:, 0, 0:keys], st[:, 6:7], s[:, 1, 0:keys],
                                                   ALU.mult, ALU.subtract).then_inc(probs_ready, 1)
                else:
                    chain.do(nc.vector.reciprocal(st[:, 6:7], st[:, 4:5]))
                    nc.vector.tensor_scalar(s[:, :, 0:keys], s[:, :, 0:keys], st[:, 6:7], None, ALU.mult).then_inc(probs_ready, 1)
            dve.wait_ge(sum_done, 1)
            var = proj[:, FK + 4:FK + 8, :]
            y = proj[:, FK:FK + 4, :]
            nc.vector.tensor_scalar(var, p_s[:, 0, :, :], 1.0 / (2 * HD), EPS, ALU.mult, ALU.add).then_inc(var_ready, 1)
            dve.wait_ge(rooted, 1)
            newton_rsqrt(nc, chain, y, var, proj[:, DK:DK + 4, :])
            for e in range(2):
                out = proj[:, FQ:FQ + 8, :].rearrange("p (h e) s -> p h e s", e=2)[:, :, e, :]
                nc.vector.scalar_tensor_tensor(out, out, lam[:, 1 + e:2 + e], y, ALU.mult, ALU.mult)


def branch_stage(core, prod, proj, y_parts, following):
    nc = core.nc
    gate_done, own, y_ready, y_high, x_back = (core.sem(f"branch_{s}") for s in ("gate_done", "own", "y_ready", "y_high", "x_back"))
    with ExitStack() as ctx:
        acc = core.ps(f"acc_{core.chunk}", [P, 2, 2, S], ctx)
        operand = Given(core, [proj[:, t, :] for t in (*range(DQ, DQ + 4), *range(FQ, FQ + 8))])
        free = core.h_mem[:, 12:16, :, :].rearrange("p k c s -> p (k c) s")
        z, gate = free[:, 0:4, :], free[:, 4:8, :]
        block = ctx.enter_context(nc.Block())

        @block.sync
        def _(sp):
            sp.dma_start(core.x[:, :, :], core.d["x_kept"]).then_inc(x_back, 16)
            stream(core, sp, prod, following)
            sp.wait_ge(x_back, 16)

        @block.scalar
        def _(act):
            def high(i, p):
                act.wait_ge(y_ready, 2 * i + (p + 1))
                nc.scalar.activation(y_parts[:, 2 * i + p, 0, :], proj[:, 2 * i + p, :], ACT.Copy).then_inc(y_high, 1)

            operand.act(act)
            nc.scalar.preload_act_table(ACT.Sigmoid)
            for i, t, previous in with_previous(core, act, prod, split_high, following):
                take_cross(core, act, prod, acc, i, t)
                g = proj[:, (G_DIFF if t % 2 else G_DIL) + t // 2 + 2 * i, :]
                nc.scalar.activation(gate[:, t, :], g, ACT.Sigmoid).then_inc(gate_done, 1)
                if previous and t % 2 == 0:
                    high(previous[0], previous[1] // 2)
            high(prod.bodies - 1, 1)

        @block.vector
        def _(dve):
            def low(i, p):
                dve.wait_ge(y_high, 2 * i + (p + 1))
                nc.vector.tensor_tensor(y_parts[:, 2 * i + p, 1, :], proj[:, 2 * i + p, :],
                                        y_parts[:, 2 * i + p, 0, :].bitcast(F32), ALU.subtract)

            operand.dve(dve)
            for i, t, previous in with_previous(core, dve, prod, split_low, following):
                take_tile(core, dve, prod, acc, z[:, t, :], i, t)
                taken(core, dve, prod, i, t)
                dve.wait_ge(gate_done, i * 4 + (t + 1))
                nc.vector.tensor_tensor(z[:, t, :], z[:, t, :], gate[:, t, :], ALU.mult).then_inc(own, 1)
                if t % 2:
                    dve.wait_ge(own, i * 4 + (t + 1))
                    nc.vector.tensor_tensor(proj[:, 2 * i + t // 2, :], z[:, t - 1, :], z[:, t, :],
                                            ALU.add).then_inc(y_ready, 1)
                elif previous:
                    low(previous[0], previous[1] // 2)
            low(prod.bodies - 1, 1)

        @block.tensor
        def _(pe):
            multiply_all(core, pe, prod, acc, operand.on(pe))
    passed(core, prod)



def weight_tiles(w):
    k, n = w.shape
    return np.ascontiguousarray(w.reshape(k // P, P, n // P, P).transpose(2, 1, 0, 3))


def by_partition(v):
    v = np.asarray(v)
    lead = int(np.prod(v.shape[:-1]))
    return v.reshape(lead, -1, P).transpose(2, 1, 0).reshape(P, -1)


def constants():
    t = np.arange(P)
    same = t[:, None] // CHUNK == t[None, :] // CHUNK
    parts = {
        "ident": np.eye(P), "ones": np.ones((P, P)),
        "causal64": same & (t[:, None] <= t[None, :]), "block64": same,
        "neg_strict64": -1.0 * (same & (t[:, None] < t[None, :])), "causal128": t[:, None] <= t[None, :],
        "inv_freq": (np.float32(ROPE_THETA) ** (-(2 * (t % (ROPE // 2))).astype(np.float32) / np.float32(ROPE)))[:, None],
        "rope_sign": np.where(t < ROPE // 2, -1.0, 1.0)[:, None],
    }
    return np.concatenate([np.asarray(parts[n], np.float32) for n in CONSTS], axis=1)


def attention_masks():
    q = (np.arange(HALVES)[None, :] * P + np.arange(P)[:, None])[:, :, None]
    dist = q - np.arange(S)[None, None, :]
    seen = [(dist >= 0) & (dist <= window) & (dist % dilation == 0) for window, dilation in DILATIONS] + [dist >= 0]
    return np.where(np.stack(seen, axis=2), 0.0, MASKED).astype(np.float32)



def whole(nc, d, out):
    def tiles_of(name, tile):
        def source(i, t, k0, nk):
            return d[name][tile(i, t)][:, k0:k0 + nk, :].rearrange("p a b -> p (a b)")
        return source

    def pair(i, t):
        return 2 * i + t

    with ExitStack() as ctx:
        core = Core(nc, ctx, d)
        stored = core.sem("stored")

        def proj_product(name, tiles, nk=KT, parts=None):
            return Product(tiles // 2, [nk, nk], tiles_of(name, pair), parts=parts)

        def up_product():
            return Product(FF_TILES, [KT, KT], tiles_of("ffn_up", lambda i, t: i + FF_TILES * t))

        def gate_up_product(n):
            def source(i, t, k0, nk):
                return d[f"ffn{n}_w_{('gate', 'up')[t]}_2"][i][:, k0:k0 + nk, :].rearrange("p a b -> p (a b)")
            return Product(FF_TILES, [KT, KT], source)

        def down_product(name, parts=None):
            return proj_product(name, KT, FF_TILES, parts)

        def branch_product():
            def source(i, t, k0, nk):
                name = ("w_dil_branch_2", "w_diff_branch_2")[t % 2]
                return d[name][2 * i + t // 2][:, k0:k0 + nk, :].rearrange("p a b -> p (a b)")
            return Product(KT // 2, [4, 8, 4, 8], source, first=[0, 4, 0, 4])

        def normed(*args, **kw):
            return lambda ctx: Normed(core, ctx, *args, **kw)

        g_parts = core.g_parts

        def swiglu(n, operand_of, following, next_gain=None):
            swiglu_up_stage(core, gate_up_product(n), operand_of, g_parts, down_product(f"ffn{n}_w_down_2"))
            product_add_stage(core, down_product(f"ffn{n}_w_down_2", g_parts), 0.5, following, next_gain)

        start_stage(core, proj_product("w_in", PROJ_TILES))

        with ExitStack() as c:
            arena = Region(core.arena[:, :, :].rearrange("p k s -> p (k s)"))
            proj = arena.take(PROJ_TILES, PAD + S)
            mix = {"conv": arena.take(16, S), "rows": arena.take(8 + 512),
                   "small": {n: core.sb(f"small_{n}", [P] + shape, F32, c)
                             for n, shape in (("g", [HEADS, HALVES]), ("beta", [HEADS, HALVES]), ("lru_c", [4]))}}
            mix["spare"] = arena.flat[:, arena.at:]
            normed_product_stage(core, proj_product("w_in", PROJ_TILES), "pre_mix",
                                 lambda i, t: proj[:, 2 * i + t, PAD:PAD + S], proj_product("w_out", KT),
                                 proj[:, :, 0:PAD])
            gdn_prepare_stage(core, proj, mix)
            gdn_stage(core, proj, mix)
            other_mixers_stage(core, proj, mix)
            plain_product_stage(core, proj_product("w_out", KT), [proj[:, at + j, PAD:PAD + S] for at in MIXED for j in range(4)],
                                lambda i, t: core.arena[:, 2 * i + t, :], up_product())

        conv_ffn_up_stage(core, up_product(), normed("pre_ffn", "residual", lambda k: core.arena[:, k, :], "post_mix"),
                          g_parts, down_product("ffn_down"))
        plain_product_stage(core, down_product("ffn_down", g_parts), [], lambda i, t: core.h_mem[:, 2 * i + t, 1, :],
                            gate_up_product(1))

        swiglu(1, normed("ffn1_norm", "residual", lambda k: core.h_mem[:, k, 1, :], "post_ffn"),
               proj_product("w_in_2", MIX_TILES), "mix_norm")
        with ExitStack() as c:
            proj = core.arena
            lam = core.sb("lam", [P, 3], F32, c)
            trig = core.sb("trig", [ROPE, 2, S], F32, c)
            rotary_stage(core, trig, lam)
            mix_in_stage(core, proj_product("w_in_2", MIX_TILES), normed("mix_norm", "prepared"), proj, trig, branch_product())
            attention_stage(core, proj, lam)
            y_parts = core.y_parts
            branch_stage(core, branch_product(), proj, y_parts, proj_product("w_out_2", KT))
            product_add_stage(core, proj_product("w_out_2", KT, parts=y_parts), 1.0, gate_up_product(2), "ffn2_norm")
        swiglu(2, normed("ffn2_norm", "prepared"), None)

        with nc.Block() as block:
            @block.sync
            def _(sp):
                sp.dma_start(out, core.x[:, :, :]).then_inc(stored, 16)
                sp.wait_ge(stored, 16)


def kernel(**inputs):
    import concourse.bacc as bacc
    from concourse.bass_utils import run_bass_kernel_spmd

    a = {k: np.asarray(v) for k, v in inputs.items()}
    gates = slice(4 * 512, 4 * 512 + 2 * HEADS)
    w_in = a["w_in"][0]
    arrays = {
        "x": a["x"][0].T.reshape(KT, P, S).transpose(1, 0, 2),
        "w_in": weight_tiles(np.delete(w_in, np.r_[gates], axis=1)),
        "w_ba": w_in[:, gates].reshape(KT, P, 2 * HEADS).transpose(1, 0, 2),
        "positions": a["positions_2"][0],
        "a_log": a["gdn_a_log"][0], "dt_bias": a["gdn_dt_bias"][0], "sgu_b": a["sgu_b"][0].reshape(-1),
        "lru_wa": a["lru_wa"][0], "lru_wx": a["lru_wx"][0], "sgu_ws": a["sgu_ws"][0].transpose(2, 0, 1),
        "consts": constants(), "masks": attention_masks(),
    }
    for name in ("w_out", "ffn_up", "ffn_down", "ffn1_w_gate_2", "ffn1_w_up_2", "ffn1_w_down_2", "w_in_2",
                 "w_dil_branch_2", "w_diff_branch_2", "w_out_2", "ffn2_w_gate_2", "ffn2_w_up_2", "ffn2_w_down_2"):
        arrays[name] = weight_tiles(a[name][0])
    arrays["w_in_2"] = arrays["w_in_2"][MIX_ORDER]
    vectors = {
        "pre_mix": a["pre_mix_norm"], "post_mix": a["post_mix_norm"], "pre_ffn": a["pre_ffn_norm"],
        "post_ffn": a["post_ffn_norm"], "ffn1_norm": a["ffn1_norm_2"], "mix_norm": a["mix_norm_2"],
        "ffn2_norm": a["ffn2_norm_2"], "gdn_conv": a["gdn_conv_w"][0], "gdn_norm": a["gdn_norm_w"],
        "lru_conv": a["lru_conv_w"][0], "lru_conv_b": a["lru_conv_b"], "lru_ba": a["lru_ba"].reshape(1, -1),
        "lru_bx": a["lru_bx"].reshape(1, -1), "lru_lambda": a["lru_lambda"], "ln_w": a["sgu_ln_w"], "ln_b": a["sgu_ln_b"],
        "sconv": a["sconv_w"][0], "grp": a["grp_norm_w"].reshape(1, -1), "ffn_conv": a["ffn_conv_w"][0],
        "ffn_conv_b": a["ffn_conv_b"], 
        "head_gain": np.concatenate([a[f"{n}_norm_2"] for n, pairs in (("dil_q", 6), ("dil_k", 6), ("diff_q", 4), ("diff_k", 4))
                                     for _ in range(pairs)]),
        "lam": np.concatenate([a["diff_lq1_2"], a["diff_lk1_2"], a["diff_lq2_2"], a["diff_lk2_2"]]),
        "subln": a["diff_subln_2"],
    }
    arrays["vectors"] = np.concatenate([by_partition(vectors[n]) for n in VECTORS], axis=1)

    nc = bacc.Bacc("TRN2", target_bir_lowering=False, num_devices=1)
    arrays = {f"in_{n}": np.ascontiguousarray(v) for n, v in arrays.items()}
    d = {n[3:]: nc.dram_tensor(n, v.shape, mybir.dt.from_np(v.dtype), kind="ExternalInput").ap()
         for n, v in arrays.items()}
    d["x_kept"] = nc.dram_tensor("x_kept", (P, KT, S), F32, kind="Internal").ap()
    out = nc.dram_tensor("out_x", (P, KT, S), F32, kind="ExternalOutput").ap()
    whole(nc, d, out)
    r = run_bass_kernel_spmd(nc, [arrays], core_ids=[0])
    got = r.results[0]["out_x"]
    return np.ascontiguousarray(got.transpose(2, 1, 0).reshape(1, S, DM))
```

```python
from contextlib import ExitStack

import numpy as np

import concourse.bass as bass
from concourse import mybir

F32 = mybir.dt.float32
F32R = mybir.dt.float32r
I32 = mybir.dt.int32
ALU = mybir.AluOpType
ACT = mybir.ActivationFunctionType
AX = mybir.AxisListType.X

P = 128
S = 256
DM = 2048
KT = DM // P
EPS = 1e-6
KG = 8
SLOTS = 4
HEADS = 4
FF_TILES = 5632 // P
PAD = 4
HALVES = S // P
ARENA_TILES = 92

VECTORS = {}
_at = 0
for _name, _n in (("pre_mix", 16), ("post_mix", 16), ("pre_ffn", 16), ("post_ffn", 16), ("ffn1_norm", 16),
                  ("mix_norm", 16), ("ffn2_norm", 16), ("gdn_conv", 48), ("gdn_norm", 1), ("lru_conv", 16),
                  ("lru_conv_b", 4), ("lru_ba", 4), ("lru_bx", 4), ("lru_lambda", 4), ("ln_w", 4), ("ln_b", 4),
                  ("sconv", 12), ("grp", 12), ("ffn_conv", 264), ("ffn_conv_b", 88), ("head_gain", 20),
                  ("lam", 4), ("subln", 2)):
    VECTORS[_name] = (_at, _n)
    _at += _n
N_VECTORS = _at

CONSTS = {}
_at = 0
for _name, _n in (("ident", 128), ("ones", 128), ("causal64", 128), ("block64", 128), ("neg_strict64", 128),
                  ("causal128", 128), ("inv_freq", 1), ("rope_sign", 1)):
    CONSTS[_name] = (_at, _n)
    _at += _n
N_CONSTS = _at


class Chain:

    def __init__(self, eng, sem):
        self.eng, self.sem, self.n = eng, sem, 0

    def add(self, ins):
        ins.then_inc(self.sem, 1)
        self.n += 1

    def settle(self):
        self.eng.wait_ge(self.sem, self.n)

    def do(self, ins):
        self.add(ins)
        self.settle()


class Product:

    def __init__(self, bodies, tiles, source, first=None, parts=None):
        self.bodies, self.tiles, self.source = bodies, tiles, source
        self.first, self.parts = first or [0] * len(tiles), parts
        self.chunks = [(t, k0, min(KG, nk - k0)) for t, nk in enumerate(tiles) for k0 in range(0, nk, KG)]
        self.per_body = len(self.chunks)
        assert self.per_body % SLOTS == 0 and len(tiles) % 2 == 0

    def of_tile(self, t):
        return [(u, c) for u, c in enumerate(self.chunks) if c[0] == t]


class Region:

    def __init__(self, flat):
        self.flat, self.at = flat, 0

    def take(self, *shape):
        n = int(np.prod(shape))
        assert self.at + n <= self.flat.shape[1]
        ap = self.flat[:, self.at:self.at + n]
        self.at += n
        if len(shape) == 1:
            return ap
        names = "abcd"[:len(shape)]
        return ap.rearrange(f"p ({' '.join(names)}) -> p {' '.join(names)}", **dict(zip(names, shape)))


class Core:

    def __init__(self, nc, ctx, d):
        self.nc, self.ctx, self.d = nc, ctx, d
        self.x = self.sb("x_T", [P, KT, S], F32)
        self.h_at = nc.sbuf_base
        self.h_mem = self.sb("halves_memory", [P, KT, 2, S], F32)
        self.h = self.over(self.h_at, "moving_halves", KT)
        self.arena_at = nc.sbuf_base
        self.arena = self.sb("arena", [P, ARENA_TILES, S], F32)
        self.g_parts = self.over(self.arena_at, "gated_halves", FF_TILES)
        self.y_parts = self.over(self.arena_at + KT * S * 4, "branch_halves", KT)
        self.raw = self.sb("weights_raw", [P, SLOTS, KG * P], F32)
        self.high = self.sb("weights_high", [P, SLOTS, KG, P], F32R)
        self.low = self.sb("weights_low", [P, SLOTS, KG, P], F32R)
        self.cross = self.sb("cross_products", [P, 2, S], F32)
        self.z = self.sb("unscaled", [P, 2, S], F32)
        self.sq = self.sb("squares", [P, 2, S], F32)
        self.total = self.sb("squares_total", [P, S], F32)
        self.rs = self.sb("token_scale", [P, S], F32)
        self.trig = self.sb("trig", [ROPE, 2, S], F32)
        self.lam = self.sb("lam", [P, 3], F32)
        self.vec = self.sb("vectors", [P, N_VECTORS], F32)
        self.const = self.sb("constants", [P, N_CONSTS], F32)
        self.loaded = [self.sem(f"weights_loaded{s}") for s in range(SLOTS)]
        self.x_loaded = [self.sem(f"x_loaded{g}") for g in range(KT // 4)]
        self.high_ready = self.sem("high_ready")
        self.low_ready = self.sem("low_ready")
        self.slots_free = self.sem("slots_free")
        self.acc_free = self.sem("acc_free")
        self.cross_ready = self.sem("cross_ready")
        self.z_free = self.sem("z_free")
        self.y_scaled = self.sem("y_scaled")
        self.x_ready = self.sem("x_ready")
        self.part_high = self.sem("part_high")
        self.part_low = self.sem("part_low")
        self.squared = self.sem("squared")
        self.squares_used = self.sem("squares_used")
        self.summed = self.sem("summed")
        self.carried = self.sem("carried")
        self.var_ready = self.sem("var_ready")
        self.rooted = self.sem("rooted")
        self.newton = self.sem("newton")
        self.rs_ready = self.sem("rs_ready")
        self.hidden_free = [self.sem(f"hidden{t}_free") for t in range(2)]
        self.activated = self.sem("activated")
        self.product_ready = self.sem("product_ready")
        self.g_high = self.sem("g_high")
        self.swiglus = 0
        self.pairs = 0
        self.parts = 0
        self.squares = 0
        self.totals = 0
        self.norms = 0
        self.xs = 0
        self.ys = 0
        self.scaled = 0
        self.chunk = 0
        self.tile = 0
        self.stage = 0

    def sb(self, name, shape, dt, ctx=None):
        return (ctx or self.ctx).enter_context(self.nc.sbuf_tensor(name, shape, dt))

    def over(self, at, name, n):
        assert at % 32 == 0
        return self.nc.alloc_sbuf_tensor_at(name, [P, n, 2, S], F32R, offset=at)

    def carry_wait(self, eng):
        eng.sem_inc(self.carried, 1)

    def ps(self, name, shape, ctx, dt=F32):
        return ctx.enter_context(self.nc.psum_tensor(name, shape, dt))

    def sem(self, name):
        return self.ctx.enter_context(self.nc.semaphore(name))

    def v(self, name, j=0, n=1):
        c = VECTORS[name][0] + j
        return self.vec[:, c:c + n] if isinstance(c, int) else self.vec[:, bass.ds(c, n)]

    def c(self, name):
        c, n = CONSTS[name]
        return self.const[:, c:c + n]



def load_chunk(core, sp, prod, base, i, u):
    t, k0, nk = prod.chunks[u]
    n = i * prod.per_body + (base + u)
    if not (isinstance(n, int) and n < SLOTS):
        sp.wait_ge(core.low_ready, n - (SLOTS - 1))
    sp.dma_start(core.raw[:, u % SLOTS, 0:nk * P], prod.source(i, t, k0, nk)).then_inc(core.loaded[u % SLOTS], 16)


def prefetch(core, sp, prod, base):
    for u in range(SLOTS):
        load_chunk(core, sp, prod, base, 0, u)


def stream(core, sp, prod, following):
    base, per = core.chunk, prod.per_body

    ahead = -(-2 * SLOTS // per)
    with sp.Fori(0, prod.bodies - ahead) as i:
        for u in range(2 * SLOTS, per + 2 * SLOTS):
            load_chunk(core, sp, prod, base, i + u // per, u % per)
    for u in range((prod.bodies - ahead) * per + 2 * SLOTS, prod.bodies * per + 2 * SLOTS):
        if u < prod.bodies * per:
            load_chunk(core, sp, prod, base, u // per, u % per)
        elif following is not None:
            v = u - prod.bodies * per
            load_chunk(core, sp, following, base + prod.bodies * per, v // following.per_body, v % following.per_body)


def split_high(core, act, n, slot, nk):
    act.wait_ge(core.loaded[slot], n[0])
    act.wait_ge(core.slots_free, n[1] + 1)
    core.nc.scalar.activation(core.high[:, slot, 0:nk, :].rearrange("p a b -> p (a b)"),
                              core.raw[:, slot, 0:nk * P], ACT.Copy).then_inc(core.high_ready, 1)


def split_low(core, dve, n, slot, nk):
    dve.wait_ge(core.high_ready, n[1] + 1)
    core.nc.vector.tensor_tensor(core.low[:, slot, 0:nk, :].rearrange("p a b -> p (a b)"),
                                 core.raw[:, slot, 0:nk * P],
                                 core.high[:, slot, 0:nk, :].rearrange("p a b -> p (a b)").bitcast(F32),
                                 ALU.subtract).then_inc(core.low_ready, 1)


def steps(core, eng, prod, split, lo=0, hi=None, following=None):
    hi = prod.bodies if hi is None else hi
    per = prod.per_body

    def body(i, final):
        for t in range(len(prod.tiles)):
            own = prod.of_tile(t)
            for j, (u, _) in enumerate(own):
                if j == len(own) - 1:
                    yield i, t
                v = u + SLOTS
                source = following if v >= per and final else prod
                if source is not None:
                    nk = source.chunks[v % per if source is prod else v - per][2]
                    n = (i * (16 * per // SLOTS) + 16 * ((core.chunk + v) // SLOTS + 1), i * per + (core.chunk + v))
                    split(core, eng, n, v % SLOTS, nk)

    ends = hi == prod.bodies
    last = hi - 1 if ends else hi
    if last - lo > 1:
        with eng.Fori(lo, last) as i:
            yield from body(i, False)
    elif last > lo:
        yield from body(lo, False)
    if ends:
        yield from body(prod.bodies - 1, True)


def multiply(core, pe, prod, acc, i, t, before=None):
    bank = t % 2
    pe.wait_ge(core.acc_free, i * len(prod.tiles) + (core.tile + t + 1))
    nk_all = prod.tiles[t]
    parts = core.h if prod.parts is None else prod.parts
    for u, (_, k0, nk) in prod.of_tile(t):
        pe.wait_ge(core.low_ready, i * prod.per_body + (core.chunk + u + 1))
        for k in range(nk):
            if before is not None:
                before(t, prod.first[t] + k0 + k)
            x = parts[:, prod.first[t] + k0 + k, :, :]
            core.nc.tensor.matmul(acc[:, bank, :, :], core.high[:, u % SLOTS, k, :], x,
                                  start=(k0 + k == 0), stop=False)
            last = core.nc.tensor.matmul(acc[:, bank, 0, :], core.low[:, u % SLOTS, k, :], x[:, 0, :],
                                         start=False, stop=(k0 + k == nk_all - 1))
        last.then_inc(core.slots_free, 1)


def pe_steps(core, pe, prod, acc, lo=0, hi=None, before=None):
    hi = prod.bodies if hi is None else hi
    if lo == 0 and before is not None:
        for t in range(len(prod.tiles)):
            multiply(core, pe, prod, acc, 0, t, before)
            yield 0, t
        lo = 1
    if hi - lo > 1:
        with pe.Fori(lo, hi) as i:
            for t in range(len(prod.tiles)):
                multiply(core, pe, prod, acc, i, t)
                yield i, t
    elif hi > lo:
        for t in range(len(prod.tiles)):
            multiply(core, pe, prod, acc, lo, t)
            yield lo, t


def multiply_all(core, pe, prod, acc, before=None):
    for _ in pe_steps(core, pe, prod, acc, before=before):
        pass


def take_cross(core, act, prod, acc, i, t):
    last = prod.of_tile(t)[-1][0]
    act.wait_ge(core.slots_free, i * prod.per_body + (SLOTS + core.chunk + last + 1))
    core.nc.scalar.activation(core.cross[:, t % 2, :], acc[:, t % 2, 1, :], ACT.Copy).then_inc(core.cross_ready, 1)


def take_tile(core, dve, prod, acc, out, i, t):
    dve.wait_ge(core.cross_ready, i * len(prod.tiles) + (core.tile + t + 1))
    core.nc.vector.tensor_tensor(out, acc[:, t % 2, 0, :], core.cross[:, t % 2, :], ALU.add).then_inc(core.acc_free, 1)


def taken(core, eng, prod, i, t):
    eng.wait_ge(core.acc_free, i * len(prod.tiles) + (2 + core.tile + t + 1))


def take_for_scaling(core, dve, prod, acc, i, t):
    dve.wait_ge(core.z_free, i * len(prod.tiles) + (core.scaled + t + 1))
    take_tile(core, dve, prod, acc, core.z[:, t % 2, :], i, t)


def scale_tile(core, pool, prod, out, i, t):
    taken(core, pool, prod, i, t)
    core.nc.gpsimd.tensor_tensor(out, core.z[:, t % 2, :], core.rs[:, :], ALU.mult).then_inc(core.z_free, 1)


def tile_scaled(core, eng, prod, i, t):
    eng.wait_ge(core.z_free, i * len(prod.tiles) + (2 + core.scaled + t + 1))


def with_previous(core, eng, prod, split, following):
    for i, t in steps(core, eng, prod, split, 0, 1):
        yield i, t, (i, t - 1) if t else None
    for i, t in steps(core, eng, prod, split, 1, following=following):
        yield i, t, (i, t - 1) if t else (i - 1, len(prod.tiles) - 1)


def passed(core, prod, scaled=False):
    core.chunk += prod.bodies * prod.per_body
    core.tile += prod.bodies * len(prod.tiles)
    if scaled:
        core.scaled += prod.bodies * len(prod.tiles)



def square_tile(core, act, src, base, i, n, t):
    act.wait_ge(core.squares_used, i * n + (base + t + 1))
    core.carry_wait(act)
    core.nc.scalar.activation(core.sq[:, t % 2, :], src, ACT.Square).then_inc(core.squared, 1)


def add_squares(core, pool, prod, base):
    n = len(prod.tiles)

    def add(i, t):
        pool.wait_ge(core.squared, i * n + (base + t + 1))
        if isinstance(i, int) and i * n + t == 0:
            core.nc.gpsimd.tensor_copy(core.total[:, :], core.sq[:, 0, :]).then_inc(core.squares_used, 1)
        else:
            pool.wait_ge(core.squares_used, i * n + (base + t + 2))
            core.nc.gpsimd.tensor_tensor(core.total[:, :], core.total[:, :], core.sq[:, t % 2, :],
                                         ALU.add).then_inc(core.squares_used, 1)
    for t in range(n):
        add(0, t)
    with pool.Fori(1, prod.bodies) as i:
        for t in range(n):
            add(i, t)


class TokenScale:

    def __init__(self, core, sum_):
        self.core, self.sum, self.norm = core, sum_, core.norms
        self.var, self.tmp = core.sq[:, 0, :], core.sq[:, 1, :]
        core.norms += 1

    def of_total(self):
        self.total_at = self.core.totals
        self.core.totals += 1
        self.sum_done = (self.core.summed, self.total_at + 1)
        return self

    def of_tiles(self, base):
        self.base = base
        self.sum_done = (self.core.squares_used, base + KT + 2)
        return self

    def sum_total(self, pe):
        core = self.core
        pe.wait_ge(core.squares_used, core.squares + 2)
        core.nc.tensor.matmul(self.sum, core.c("ones"), core.total[:, :], start=True, stop=True).then_inc(core.summed, 1)

    def sum_tile(self, pe, k):
        core = self.core
        pe.wait_ge(core.squared, self.base + k + 1)
        core.nc.tensor.matmul(self.sum, core.c("ones"), core.sq[:, k % 2, :], start=(k == 0),
                              stop=(k == KT - 1)).then_inc(core.squares_used, 1)

    def variance(self, dve):
        dve.wait_ge(*self.sum_done)
        self.core.nc.vector.tensor_scalar(self.var, self.sum, 1.0 / DM, EPS, ALU.mult,
                                          ALU.add).then_inc(self.core.var_ready, 1)

    def root(self, act):
        core = self.core
        act.wait_ge(core.var_ready, self.norm + 1)
        core.nc.scalar.activation(core.rs[:, :], self.var, ACT.Abs_reciprocal_sqrt).then_inc(core.rooted, 1)

    def refine(self, dve):
        core = self.core
        dve.wait_ge(core.rooted, self.norm + 1)
        chain = Chain(dve, core.newton)
        chain.n = 2 * self.norm
        chain.do(core.nc.vector.tensor_tensor(self.tmp, core.rs[:, :], core.rs[:, :], ALU.mult))
        chain.do(core.nc.vector.scalar_tensor_tensor(self.tmp, self.tmp, -0.5, self.var, ALU.mult, ALU.mult))
        core.nc.vector.scalar_tensor_tensor(core.rs[:, :], self.tmp, 1.5, core.rs[:, :],
                                            ALU.add, ALU.mult).then_inc(core.rs_ready, 1)

    def ready(self, eng):
        eng.wait_ge(self.core.rs_ready, self.norm + 1)



def high_part(core, act, k, src, gain):
    core.nc.scalar.activation(core.h[:, k, 0, :], src, ACT.Copy,
                              scale=1.0 if gain is None else gain).then_inc(core.part_high, 1)


def low_part(core, dve, k, src, gain, base):
    dve.wait_ge(core.part_high, k + (base + 1))
    high = core.h[:, k, 0, :].bitcast(F32)
    if gain is None:
        ins = core.nc.vector.tensor_tensor(core.h[:, k, 1, :], src, high, ALU.subtract)
    else:
        ins = core.nc.vector.scalar_tensor_tensor(core.h[:, k, 1, :], src, gain, high, ALU.mult, ALU.subtract)
    ins.then_inc(core.part_low, 1)


class Given:

    def __init__(self, core, sources):
        self.core, self.sources, self.base = core, sources, core.parts
        core.parts += len(sources)

    def act(self, act):
        for k, src in enumerate(self.sources):
            high_part(self.core, act, k, src, None)

    def dve(self, dve):
        for k, src in enumerate(self.sources):
            low_part(self.core, dve, k, src, None, self.base)

    def on(self, pe):
        return None if not self.sources else lambda t, k: pe.wait_ge(self.core.part_low, self.base + k + 1)


class Normed:

    def __init__(self, core, ctx, gain, how, y=None, y_gain=None):
        self.core, self.gain, self.how, self.y, self.y_gain = core, gain, how, y, y_gain
        core.stage += 1
        self.bank = ps = core.ps(f"ps_scale{core.stage}", [P, 2, S], ctx)
        self.y_scale = TokenScale(core, ps[:, 0, :]).of_total() if how == "residual" else None
        self.scale = TokenScale(core, ps[:, 1, :])
        if how == "prepared":
            self.scale.of_total()
        else:
            self.scale.of_tiles(core.squares)
        self.base, self.xs, self.ys = core.parts, core.xs, core.ys

    def passed(self):
        core = self.core
        if self.how != "prepared":
            core.parts += KT
            core.squares += KT
        if self.how == "residual":
            core.xs += KT
            core.ys += KT

    def g(self, k):
        return self.core.v(self.gain, k)

    def act(self, act):
        core = self.core
        if self.how == "residual":
            self.y_scale.root(act)
        if self.how != "prepared":
            for k in range(KT):
                if self.how == "loaded":
                    act.wait_ge(core.x_loaded[k // 4], 16)
                if self.how == "residual":
                    act.wait_ge(core.x_ready, self.xs + k + 1)
                high_part(core, act, k, core.x[:, k, :], self.g(k))
                if self.how == "residual":
                    square_tile(core, act, core.x[:, k, :], self.scale.base, 0, 0, k)

    def dve(self, dve):
        core = self.core
        if self.how == "loaded":
            for k in range(KT):
                dve.wait_ge(core.x_loaded[k // 4], 16)
                dve.wait_ge(core.squares_used, self.scale.base + k + 1)
                core.nc.vector.tensor_tensor(core.sq[:, k % 2, :], core.x[:, k, :], core.x[:, k, :],
                                             ALU.mult).then_inc(core.squared, 1)
                low_part(core, dve, k, core.x[:, k, :], self.g(k), self.base)
        elif self.how == "residual":
            self.y_scale.variance(dve)
            self.y_scale.refine(dve)
            self.y_scale.ready(dve)
            AHEAD = 3
            for k in range(KT + AHEAD):
                if k < KT:
                    core.nc.vector.scalar_tensor_tensor(self.y(k), self.y(k), core.v(self.y_gain, k), core.rs[:, :],
                                                        ALU.mult, ALU.mult).then_inc(core.y_scaled, 1)
                if k >= AHEAD:
                    low_part(core, dve, k - AHEAD, core.x[:, k - AHEAD, :], self.g(k - AHEAD), self.base)

    def pool(self, pool):
        core = self.core
        if self.how == "residual":
            for k in range(KT):
                pool.wait_ge(core.y_scaled, self.ys + k + 1)
                core.nc.gpsimd.tensor_tensor(core.x[:, k, :], core.x[:, k, :], self.y(k), ALU.add).then_inc(core.x_ready, 1)

    def start(self, pe):
        if self.how == "residual":
            self.y_scale.sum_total(pe)

    def on(self, pe):
        if self.how == "prepared":
            return lambda t, k: None

        def before(t, k):
            if t == 0:
                self.scale.sum_tile(pe, k)
                pe.wait_ge(self.core.part_low, self.base + k + 1)
        return before

    def after_first(self, pe):
        if self.how == "prepared":
            self.scale.sum_total(pe)



def plain_product_stage(core, prod, sources, out, following):
    nc = core.nc
    n = len(prod.tiles)
    base = core.squares
    final = (prod.bodies - 1, n - 1)
    with ExitStack() as ctx:
        acc = core.ps(f"acc_{core.chunk}", [P, 2, 2, S], ctx)
        operand = Given(core, sources)
        block = ctx.enter_context(nc.Block())

        @block.sync
        def _(sp):
            stream(core, sp, prod, following)

        @block.scalar
        def _(act):
            def square(i, t):
                taken(core, act, prod, i, t)
                square_tile(core, act, out(i, t), base, i, n, t)

            operand.act(act)
            for i, t, previous in with_previous(core, act, prod, split_high, following):
                take_cross(core, act, prod, acc, i, t)
                if previous:
                    square(*previous)
            square(*final)

        @block.vector
        def _(dve):
            operand.dve(dve)
            for i, t in steps(core, dve, prod, split_low, following=following):
                take_tile(core, dve, prod, acc, out(i, t), i, t)

        @block.tensor
        def _(pe):
            multiply_all(core, pe, prod, acc, operand.on(pe))

        @block.gpsimd
        def _(pool):
            add_squares(core, pool, prod, base)
    core.squares += prod.bodies * n
    passed(core, prod)


def normed_product_stage(core, prod, gain, out, following, zeros):
    nc = core.nc
    with ExitStack() as ctx:
        acc = core.ps(f"acc_{core.chunk}", [P, 2, 2, S], ctx)
        operand = Normed(core, ctx, gain, "loaded")
        rotary = Rotary(core, ctx)
        block = ctx.enter_context(nc.Block())

        @block.sync
        def _(sp):
            rotary.load(sp)
            stream(core, sp, prod, following)

        @block.scalar
        def _(act):
            operand.act(act)
            for i, t in steps(core, act, prod, split_high, 0, 1):
                take_cross(core, act, prod, acc, i, t)
                if t == 0:
                    operand.scale.root(act)
            for i, t in steps(core, act, prod, split_high, 1, 2):
                take_cross(core, act, prod, acc, i, t)
                if t == 1:
                    rotary.sines(act)
            for i, t in steps(core, act, prod, split_high, 2, following=following):
                take_cross(core, act, prod, acc, i, t)

        @block.vector
        def _(dve):
            operand.dve(dve)
            for i, t in steps(core, dve, prod, split_low, 0, 1):
                take_for_scaling(core, dve, prod, acc, i, t)
                if t == 0:
                    operand.scale.variance(dve)
                    operand.scale.refine(dve)
            for i, t in steps(core, dve, prod, split_low, 1, 2):
                take_for_scaling(core, dve, prod, acc, i, t)
                if t == 0:
                    chain = rotary.angles(dve)
            for i, t in steps(core, dve, prod, split_low, 2, 3):
                take_for_scaling(core, dve, prod, acc, i, t)
                if t == 0:
                    rotary.finish(dve, chain)
            for i, t in steps(core, dve, prod, split_low, 3, following=following):
                take_for_scaling(core, dve, prod, acc, i, t)

        @block.tensor
        def _(pe):
            for i, t in pe_steps(core, pe, prod, acc, 0, 1, before=operand.on(pe)):
                pass
            for i, t in pe_steps(core, pe, prod, acc, 1, 2):
                if t == 1:
                    rotary.dot(pe)
            for i, t in pe_steps(core, pe, prod, acc, 2):
                pass

        @block.gpsimd
        def _(pool):
            nc.gpsimd.memset(zeros, 0.0)
            operand.scale.ready(pool)
            with pool.Fori(0, prod.bodies) as i:
                for t in range(len(prod.tiles)):
                    scale_tile(core, pool, prod, out(i, t), i, t)
    operand.passed()
    passed(core, prod, scaled=True)


def product_add_stage(core, prod, factor, following, next_gain=None):
    nc = core.nc
    core.stage += 1
    n = len(prod.tiles)
    squares, xs, parts = core.squares, core.xs, core.parts
    final = (prod.bodies - 1, n - 1)
    with ExitStack() as ctx:
        acc = core.ps(f"acc_{core.chunk}", [P, 2, 2, S], ctx)
        y = core.sb(f"branch{core.stage}", [P, 2, S], F32, ctx)
        block = ctx.enter_context(nc.Block())

        @block.sync
        def _(sp):
            stream(core, sp, prod, following)

        @block.scalar
        def _(act):
            def prepare(i, t):
                k = i * n + t
                act.wait_ge(core.x_ready, k + (xs + 1))
                high_part(core, act, k, core.x[:, k, :], core.v(next_gain, k))
                square_tile(core, act, core.x[:, k, :], squares, i, n, t)

            for i, t, previous in with_previous(core, act, prod, split_high, following):
                take_cross(core, act, prod, acc, i, t)
                if previous and next_gain:
                    prepare(*previous)
            if next_gain:
                prepare(*final)

        @block.vector
        def _(dve):
            def prepare(i, t):
                k = i * n + t
                low_part(core, dve, k, core.x[:, k, :], core.v(next_gain, k), parts)

            for i, t, previous in with_previous(core, dve, prod, split_low, following):
                take_tile(core, dve, prod, acc, y[:, t, :], i, t)
                taken(core, dve, prod, i, t)
                x = core.x[:, n * i + t, :]
                nc.vector.scalar_tensor_tensor(x, y[:, t, :], factor, x, ALU.mult, ALU.add).then_inc(core.x_ready, 1)
                if previous and next_gain:
                    prepare(*previous)
            if next_gain:
                prepare(*final)

        @block.tensor
        def _(pe):
            multiply_all(core, pe, prod, acc)

        @block.gpsimd
        def _(pool):
            if next_gain:
                add_squares(core, pool, prod, squares)
    core.xs += KT
    if next_gain:
        core.parts += KT
        core.squares += KT
    passed(core, prod)


def conv_ffn_up_stage(core, prod, operand_of, g_parts, following):
    nc = core.nc
    biased_ready, conv_ready, own = core.sem("ffn_biased_ready"), core.sem("ffn_conv_ready"), core.sem("ffn_own")
    with ExitStack() as ctx:
        acc = core.ps(f"acc_{core.chunk}", [P, 2, 2, S], ctx)
        hidden = core.sb("ffn_hidden", [P, 2, PAD + S], F32, ctx)
        tail = core.arena[:, 2 * FF_TILES:2 * FF_TILES + 4, :]
        conv, gelu, g = tail[:, 0:2, :], tail[:, 2, :], tail[:, 3, :]
        operand = operand_of(ctx)
        scale = operand.scale
        base = core.pairs
        block = ctx.enter_context(nc.Block())

        def tap(i, t, j):
            return core.v("ffn_conv", i * 3 + (t * FF_TILES * 3 + j))

        @block.sync
        def _(sp):
            stream(core, sp, prod, following)

        @block.gpsimd
        def _(pool):
            nc.gpsimd.memset(hidden[:, :, 0:PAD], 0.0)
            operand.pool(pool)
            scale.ready(pool)
            with pool.Fori(0, prod.bodies) as i:
                for t in range(2):
                    pool.wait_ge(conv_ready, i * 2 + (t + 1))
                    scale_tile(core, pool, prod, hidden[:, t, PAD:PAD + S], i, t)

        @block.scalar
        def _(act):
            def bias_tile(i, t):
                tile_scaled(core, act, prod, i, t)
                nc.scalar.activation(conv[:, t, :], hidden[:, t, PAD:PAD + S], ACT.Identity, scale=tap(i, t, 2),
                                     bias=core.v("ffn_conv_b", i + t * FF_TILES)).then_inc(biased_ready, 1)

            def activate(i):
                act.wait_ge(conv_ready, i * 2 + 3)
                nc.scalar.activation(gelu, conv[:, 0, :], ACT.Gelu_apprx_tanh).then_inc(core.activated, 1)

            def high(i):
                act.wait_ge(core.product_ready, i + (base + 1))
                nc.scalar.activation(g_parts[:, i, 0, :], g, ACT.Copy).then_inc(core.g_high, 1)

            operand.act(act)
            for i, t in steps(core, act, prod, split_high, 0, 1):
                take_cross(core, act, prod, acc, i, t)
                if t == 0:
                    scale.root(act)
                    nc.scalar.preload_act_table(ACT.Gelu_apprx_tanh)
            bias_tile(0, 0)
            for i, t in steps(core, act, prod, split_high, 1, following=following):
                take_cross(core, act, prod, acc, i, t)
                if t == 0:
                    activate(i - 1)
                    bias_tile(i - 1, 1)
                else:
                    high(i - 1)
                    bias_tile(i, 0)
            activate(prod.bodies - 1)
            bias_tile(prod.bodies - 1, 1)
            high(prod.bodies - 1)

        @block.vector
        def _(dve):
            def convolve(i, t):
                dve.wait_ge(biased_ready, i * 2 + (t + 1))
                nc.vector.scalar_tensor_tensor(conv[:, t, :], hidden[:, t, PAD - 1:PAD - 1 + S], tap(i, t, 1),
                                               conv[:, t, :], ALU.mult, ALU.add).then_inc(own, 1)
                dve.wait_ge(own, i * 2 + (t + 1))
                nc.vector.scalar_tensor_tensor(conv[:, t, :], hidden[:, t, PAD - 2:PAD - 2 + S], tap(i, t, 0),
                                               conv[:, t, :], ALU.mult, ALU.add).then_inc(conv_ready, 1)

            def gated(i):
                dve.wait_ge(core.activated, i + (base + 1))
                dve.wait_ge(conv_ready, i * 2 + 4)
                nc.vector.tensor_tensor(g, gelu, conv[:, 1, :], ALU.mult).then_inc(core.product_ready, 1)

            def low(i):
                dve.wait_ge(core.g_high, i + (base + 1))
                nc.vector.tensor_tensor(g_parts[:, i, 1, :], g, g_parts[:, i, 0, :].bitcast(F32), ALU.subtract)

            dve.sem_inc(conv_ready, 2)
            operand.dve(dve)
            for i, t in steps(core, dve, prod, split_low, 0, 1):
                take_for_scaling(core, dve, prod, acc, i, t)
                if t == 0:
                    scale.variance(dve)
                    scale.refine(dve)
            convolve(0, 0)
            for i, t in steps(core, dve, prod, split_low, 1, following=following):
                take_for_scaling(core, dve, prod, acc, i, t)
                if t == 0:
                    convolve(i - 1, 1)
                    gated(i - 1)
                else:
                    low(i - 1)
                    convolve(i, 0)
            convolve(prod.bodies - 1, 1)
            gated(prod.bodies - 1)
            low(prod.bodies - 1)

        @block.tensor
        def _(pe):
            operand.start(pe)
            for i, t in pe_steps(core, pe, prod, acc, before=operand.on(pe)):
                if isinstance(i, int) and i + t == 0:
                    operand.after_first(pe)
    operand.passed()
    core.pairs += prod.bodies
    passed(core, prod, scaled=True)


def swiglu_up_stage(core, prod, operand_of, g_parts, following):
    nc = core.nc
    core.stage += 1
    with ExitStack() as ctx:
        acc = core.ps(f"acc_{core.chunk}", [P, 2, 2, S], ctx)
        hidden = core.sb(f"ffn_hidden{core.stage}", [P, 2, S], F32, ctx)
        silu = core.sb(f"ffn_silu{core.stage}", [P, S], F32, ctx)
        g = core.sb(f"ffn_g{core.stage}", [P, S], F32, ctx)
        operand = operand_of(ctx)
        scale = operand.scale
        base = core.pairs
        used = core.swiglus * prod.bodies
        core.swiglus += 1
        block = ctx.enter_context(nc.Block())

        @block.sync
        def _(sp):
            stream(core, sp, prod, following)

        @block.gpsimd
        def _(pool):
            operand.pool(pool)
            scale.ready(pool)
            with pool.Fori(0, prod.bodies) as i:
                for t in range(2):
                    pool.wait_ge(core.hidden_free[t], i + (used + 1))
                    scale_tile(core, pool, prod, hidden[:, t, :], i, t)

        @block.scalar
        def _(act):
            def activate(i):
                tile_scaled(core, act, prod, i, 0)
                act.wait_ge(core.product_ready, i + base)
                nc.scalar.activation(silu[:, :], hidden[:, 0, :], ACT.Silu).then_inc(core.hidden_free[0], 1)

            def high(i):
                act.wait_ge(core.product_ready, i + (base + 1))
                nc.scalar.activation(g_parts[:, i, 0, :], g[:, :], ACT.Copy).then_inc(core.g_high, 1)

            operand.act(act)
            for i, t in steps(core, act, prod, split_high, 0, 1):
                take_cross(core, act, prod, acc, i, t)
                if t == 0:
                    scale.root(act)
                    nc.scalar.preload_act_table(ACT.Silu)
            activate(0)
            for i, t in steps(core, act, prod, split_high, 1, following=following):
                take_cross(core, act, prod, acc, i, t)
                if t == 0:
                    high(i - 1)
                else:
                    activate(i)
            high(prod.bodies - 1)

        @block.vector
        def _(dve):
            def gated(i):
                dve.wait_ge(core.hidden_free[0], i + (used + 2))
                tile_scaled(core, dve, prod, i, 1)
                nc.vector.tensor_tensor(g[:, :], silu[:, :], hidden[:, 1, :], ALU.mult).then_inc(core.product_ready, 1)

            def low(i):
                dve.wait_ge(core.g_high, i + (base + 1))
                nc.vector.tensor_tensor(g_parts[:, i, 1, :], g[:, :], g_parts[:, i, 0, :].bitcast(F32),
                                        ALU.subtract).then_inc(core.hidden_free[1], 1)

            operand.dve(dve)
            for i, t in steps(core, dve, prod, split_low, 0, 1):
                take_for_scaling(core, dve, prod, acc, i, t)
                if t == 0:
                    scale.variance(dve)
                    scale.refine(dve)
            for i, t in steps(core, dve, prod, split_low, 1, following=following):
                take_for_scaling(core, dve, prod, acc, i, t)
                if t == 0:
                    gated(i - 1)
                else:
                    low(i - 1)
            gated(prod.bodies - 1)
            low(prod.bodies - 1)

        @block.tensor
        def _(pe):
            operand.start(pe)
            for i, t in pe_steps(core, pe, prod, acc, before=operand.on(pe)):
                if isinstance(i, int) and i + t == 0:
                    operand.after_first(pe)
    operand.passed()
    core.pairs += prod.bodies
    passed(core, prod, scaled=True)


def start_stage(core, first):
    nc = core.nc
    inputs_loaded = core.sem("inputs_loaded")
    with nc.Block() as block:
        @block.sync
        def _(sp):
            sp.dma_start(core.vec[:, :], core.d["vectors"]).then_inc(inputs_loaded, 16)
            sp.dma_start(core.const[:, :], core.d["consts"]).then_inc(inputs_loaded, 16)
            prefetch(core, sp, first, 0)
            for g in range(KT // 4):
                sp.dma_start(core.x[:, 4 * g:4 * g + 4, :], core.d["x"][:, 4 * g:4 * g + 4, :]).then_inc(core.x_loaded[g], 16)
            for u in range(SLOTS, 2 * SLOTS):
                load_chunk(core, sp, first, 0, u // first.per_body, u % first.per_body)
            sp.wait_ge(inputs_loaded, 32)

        @block.tensor
        def _(pe):
            pe.sem_inc(core.slots_free, SLOTS)

        @block.scalar
        def _(act):
            for u in range(SLOTS):
                split_high(core, act, (16, u), u, first.chunks[u][2])

        @block.vector
        def _(dve):
            dve.sem_inc(core.acc_free, 2)
            for u in range(SLOTS):
                split_low(core, dve, (16, u), u, first.chunks[u][2])

        @block.gpsimd
        def _(pool):
            pool.sem_inc(core.z_free, 2)
            pool.sem_inc(core.squares_used, 2)
            pool.sem_inc(core.hidden_free[0], 1)
            pool.sem_inc(core.hidden_free[1], 1)



Q, K_, V, Z, LRU_X, LRU_G, SGU_U, SGU_V, SC_B, SC_C, SC_H = (4 * j for j in range(11))
PROJ_TILES = 44
MIXED = (Z, LRU_X, SGU_U, SC_C)
UNITS = HEADS * HALVES
HD = 128
CHUNK = 64
LRU_C = 8.0


def newton_rsqrt(nc, chain, y, v, t):
    chain.do(nc.vector.tensor_tensor(t, y, y, ALU.mult))
    chain.do(nc.vector.scalar_tensor_tensor(t, t, -0.5, v, ALU.mult, ALU.mult))
    chain.do(nc.vector.scalar_tensor_tensor(y, t, 1.5, y, ALU.add, ALU.mult))


def gdn_prepare_stage(core, proj, mix):
    nc = core.nc
    w_ba_loaded, conv_steps, silu_done, squared, ba_done, summed, rooted, own, gate_in, gate_exp, var_ready = (
        core.sem(f"gdn_{s}") for s in ("w_ba_loaded", "conv_steps", "silu_done", "squared", "ba_done", "summed",
                                       "rooted", "own", "gate_in", "gate_exp", "var_ready"))
    conv, small, rows = mix["conv"], mix["small"], mix["rows"]
    with ExitStack() as ctx:
        w_ba = core.sb("w_ba", [P, KT, 2 * HEADS], F32, ctx)
        spare = Region(mix["spare"])
        sq, var, tmp = spare.take(8, S), spare.take(4, S), spare.take(4, S)
        sp_in, sp_abs, sp_e, sp_z, sp_w, sp_p = (core.sb(f"softplus_{n}", [P, 12], F32, ctx)
                                                 for n in ("in", "abs", "e", "z", "w", "p"))
        beta_e = core.sb("beta_e", [P, HALVES, HEADS], F32, ctx)
        exp_a = core.sb("exp_a", [P, HEADS], F32, ctx)
        scales = core.sb("ba_scales", [P, HALVES], F32, ctx)
        ba = core.sb("ba", [P, HALVES, 2 * HEADS], F32, ctx)
        p_ba = core.ps("ps_ba", [P, HALVES, 2 * HEADS], ctx)
        p_rs = core.ps("ps_rs", [P, HALVES, P], ctx)
        ssq = core.ps("ps_ssq", [P, 8, S], ctx)
        block = ctx.enter_context(nc.Block())
        GROUP_AT = (Q, K_, V, LRU_X)

        @block.sync
        def _(sp):
            sp.dma_start(w_ba[:, :, :], core.d["w_ba"]).then_inc(w_ba_loaded, 16)
            sp.dma_start(rows[:, 0:HEADS], core.d["a_log"].partition_broadcast(P)).then_inc(w_ba_loaded, 16)
            sp.dma_start(rows[:, HEADS:2 * HEADS], core.d["dt_bias"].partition_broadcast(P)).then_inc(w_ba_loaded, 16)
            sp.dma_start(rows[:, 8:8 + 512], core.d["sgu_b"].partition_broadcast(P)).then_inc(w_ba_loaded, 16)

        @block.tensor
        def _(pe):
            pe.wait_ge(w_ba_loaded, 64)
            for half in range(HALVES):
                at = slice(half * P, (half + 1) * P)
                for k in range(KT):
                    for part in range(2):
                        last = nc.tensor.matmul(p_ba[:, half, :], core.h[:, k, part, at].bitcast(F32), w_ba[:, k, :],
                                                start=(k == 0 and part == 0), stop=(k == KT - 1 and part == 1))
            last.then_inc(ba_done, 1)
            for half in range(HALVES):
                last = nc.tensor.transpose(p_rs[:, half, :], core.rs[:, half * P:(half + 1) * P], core.c("ident"))
            last.then_inc(ba_done, 1)
            for g in range(2):
                pe.wait_ge(squared, g + 1)
                for j in range(2):
                    at = slice(4 * g + 2 * j, 4 * g + 2 * j + 2)
                    last = nc.tensor.matmul(ssq[:, at, :], core.c("ones"), sq[:, at, :], start=True, stop=True)
                last.then_inc(summed, 1)

        @block.scalar
        def _(act):
            for g in range(3):
                act.wait_ge(conv_steps, 16 * (g + 1))
                at = slice(4 * g, 4 * g + 4)
                nc.scalar.activation(conv[:, at, :], conv[:, at, :], ACT.Silu).then_inc(silu_done, 1)
                if g < 2:
                    act.wait_ge(silu_done, g + 1)
                    nc.scalar.activation(sq[:, at, :], conv[:, at, :], ACT.Square).then_inc(squared, 1)
            act.wait_ge(gate_in, 1)
            nc.scalar.activation(sp_e[:, :], sp_abs[:, :], ACT.Exp, scale=-1.0).then_inc(gate_exp, 1)
            nc.scalar.activation(beta_e[:, :, :], ba[:, :, 0:HEADS], ACT.Exp, scale=-1.0).then_inc(gate_exp, 1)
            nc.scalar.activation(exp_a[:, :], rows[:, 0:HEADS], ACT.Exp).then_inc(gate_exp, 1)
            for g in range(2):
                act.wait_ge(var_ready, g + 1)
                nc.scalar.activation(sq[:, 4 * g:4 * g + 4, :], var[:, :, :], ACT.Abs_reciprocal_sqrt).then_inc(rooted, 1)

        @block.vector
        def _(dve):
            steps = Chain(dve, conv_steps)
            for g in range(4):
                for o in range(4):
                    for j in range(4):
                        src = proj[:, GROUP_AT[g] + j, PAD - o:PAD - o + S]
                        dst = conv[:, 4 * g + j, :]
                        w = core.v("gdn_conv", 4 * (4 * g + j) + 3 - o) if g < 3 else core.v("lru_conv", 4 * j + 3 - o)
                        if o:
                            steps.add(nc.vector.scalar_tensor_tensor(dst, src, w, dst, ALU.mult, ALU.add))
                        elif g < 3:
                            steps.add(nc.vector.tensor_scalar(dst, src, w, None, ALU.mult))
                        else:
                            steps.add(nc.vector.tensor_scalar(dst, src, w, core.v("lru_conv_b", j), ALU.mult, ALU.add))
                    steps.settle()
            chain = Chain(dve, own)
            dve.wait_ge(ba_done, 2)
            chain.do(nc.vector.tensor_copy(scales[:, :], p_rs[:, :, 0]))
            for half in range(HALVES):
                chain.add(nc.vector.tensor_scalar(ba[:, half, :], p_ba[:, half, :], scales[:, half:half + 1], None, ALU.mult))
            chain.settle()
            chain.add(nc.vector.tensor_tensor(
                sp_in[:, 0:8].rearrange("p (a h) -> p a h", a=HALVES), ba[:, :, HEADS:2 * HEADS],
                rows[:, HEADS:2 * HEADS].unsqueeze(1).to_broadcast([P, HALVES, HEADS]), ALU.add))
            chain.do(nc.vector.tensor_scalar(sp_in[:, 8:12], core.v("lru_lambda", 0, 4), -1.0, None, ALU.mult))
            chain.do(nc.vector.tensor_scalar(sp_z[:, :], sp_in[:, :], -1.0, None, ALU.mult))
            nc.vector.tensor_tensor(sp_abs[:, :], sp_in[:, :], sp_z[:, :], ALU.max).then_inc(gate_in, 1)
            dve.wait_ge(gate_exp, 3)
            chain.do(nc.vector.tensor_scalar(sp_w[:, :], sp_e[:, :], 2.0, None, ALU.add))
            chain.do(nc.vector.reciprocal(sp_w[:, :], sp_w[:, :]))
            chain.do(nc.vector.tensor_tensor(sp_z[:, :], sp_e[:, :], sp_w[:, :], ALU.mult))
            chain.do(nc.vector.tensor_tensor(sp_w[:, :], sp_z[:, :], sp_z[:, :], ALU.mult))
            chain.do(nc.vector.tensor_scalar(sp_p[:, :], sp_w[:, :], 1.0 / 17, None, ALU.mult))
            for d in (15, 13, 11, 9, 7, 5, 3):
                chain.do(nc.vector.scalar_tensor_tensor(sp_p[:, :], sp_p[:, :], 1.0 / d, sp_w[:, :], ALU.add, ALU.mult))
            chain.do(nc.vector.scalar_tensor_tensor(sp_p[:, :], sp_p[:, :], 1.0, sp_z[:, :], ALU.add, ALU.mult))
            chain.do(nc.vector.tensor_scalar(sp_in[:, :], sp_in[:, :], 0.0, None, ALU.max))
            chain.do(nc.vector.scalar_tensor_tensor(sp_in[:, :], sp_p[:, :], 2.0, sp_in[:, :], ALU.mult, ALU.add))
            chain.add(nc.vector.scalar_tensor_tensor(
                small["g"][:, :, :].rearrange("p h a -> p a h"), sp_in[:, 0:8].rearrange("p (a h) -> p a h", a=HALVES),
                -1.0, exp_a[:, :].unsqueeze(1).to_broadcast([P, HALVES, HEADS]), ALU.mult, ALU.mult))
            chain.add(nc.vector.tensor_scalar(small["lru_c"][:, :], sp_in[:, 8:12], -LRU_C, None, ALU.mult))
            chain.do(nc.vector.tensor_scalar(beta_e[:, :, :], beta_e[:, :, :], 1.0, None, ALU.add))
            chain.do(nc.vector.reciprocal(beta_e[:, :, :], beta_e[:, :, :]))
            chain.do(nc.vector.tensor_copy(small["beta"][:, :, :].rearrange("p h a -> p a h"), beta_e[:, :, :]))
            for g in range(2):
                at = slice(4 * g, 4 * g + 4)
                dve.wait_ge(summed, g + 1)
                nc.vector.tensor_scalar(var[:, :, :], ssq[:, at, :], EPS, None, ALU.add).then_inc(var_ready, 1)
                dve.wait_ge(rooted, g + 1)
                newton_rsqrt(nc, chain, sq[:, at, :], var[:, :, :], tmp[:, :, :])
                chain.do(nc.vector.scalar_tensor_tensor(conv[:, at, :], conv[:, at, :], HD ** -0.5 if g == 0 else 1.0,
                                                        sq[:, at, :], ALU.mult, ALU.mult))


def gdn_stage(core, proj, mix):
    nc = core.nc
    (diag, cols_done, cols_out, ecols, rows_done, diff_done, decay_done, masked, kk_done, qk_done, n_ready, nt_back,
     p_ready, pp_done, ppt_done, pt_ready, tt_done, tt_ready, kt_done, vt_done, k_out, v_out, w_done, w_out, u_out,
     ws_done, vn_ready, o_done, st_done, o_out, state_ready, o_sq, o_sum, o_root, z_done, own, kg_out, q_ready, o_var) = (
        core.sem(f"delta_{s}") for s in (
            "diag", "cols_done", "cols_out", "ecols", "rows_done", "diff_done", "decay_done", "masked", "kk_done",
            "qk_done", "n_ready", "nt_back", "p_ready", "pp_done", "ppt_done", "pt_ready", "tt_done", "tt_ready",
            "kt_done", "vt_done", "k_out", "v_out", "w_done", "w_out", "u_out", "ws_done", "vn_ready", "o_done",
            "st_done", "o_out", "state_ready", "o_sq", "o_sum", "o_root", "z_done", "own", "kg_out", "q_ready", "o_var"))
    conv, small = mix["conv"], mix["small"]
    ITER = 5
    G4 = UNITS // 2
    qT = conv[:, 0:4, :].rearrange("p h (a c) -> p (h a) c", a=HALVES)
    kT = conv[:, 4:8, :].rearrange("p h (a c) -> p (h a) c", a=HALVES)
    vT = conv[:, 8:12, :].rearrange("p h (a c) -> p (h a) c", a=HALVES)

    def over_units(ap):
        return ap.unsqueeze(1).to_broadcast([P, UNITS, P])

    with ExitStack() as ctx:
        halves, spare = Region(core.h_mem[:, :, :, :].rearrange("p k c s -> p (k c s)")), Region(mix["spare"])
        g_diag, b_diag, egrow, decay, attnT, TT = (halves.take(UNITS, P) for _ in range(6))
        pw = [halves.take(UNITS, P) for _ in range(2)]
        pt = [spare.take(UNITS, P) for _ in range(2)]
        kbg, kg, vb = (spare.take(UNITS, P) for _ in range(3))
        cols = core.sb("delta_cols", [P, 6, UNITS], F32, ctx)
        state = core.sb("delta_state", [P, HEADS, HD], F32, ctx)
        gcol, tot, ecol, kgs, bec, left = (cols[:, j, :] for j in range(6))
        pa, pb, pc, pd = (core.ps(f"delta_ps{n}", [P, UNITS, P], ctx) for n in "abcd")
        wT, u_sb = g_diag, b_diag
        v_new, oT = kbg, decay
        block = ctx.enter_context(nc.Block())
        g8 = small["g"][:, :, :].rearrange("p h a -> p (h a)")
        beta8 = small["beta"][:, :, :].rearrange("p h a -> p (h a)")

        @block.tensor
        def _(pe):
            nc.tensor.matmul(pa[:, 0, 0:UNITS], core.c("causal64"), g8, start=True, stop=True)
            nc.tensor.matmul(pa[:, 0, UNITS:2 * UNITS], core.c("block64"), g8, start=True, stop=True).then_inc(cols_done, 1)
            for n, (out, rhs) in enumerate(((pb, g_diag), (pc, b_diag))):
                pe.wait_ge(diag, n + 1)
                for g in range(2):
                    at = slice(G4 * g, G4 * g + G4)
                    last = nc.tensor.matmul(out[:, at, :], core.c("ones"), rhs[:, at, :], start=True, stop=True)
                last.then_inc(rows_done, 1)
            for u in range(UNITS):
                last = nc.tensor.matmul(pd[:, u, :], kT[:, u, :], kT[:, u, :], start=True, stop=True)
            last.then_inc(kk_done, 1)
            pe.wait_ge(cols_out, 1)
            for u in range(UNITS):
                last = nc.tensor.matmul(pa[:, u, :], kT[:, u, :], qT[:, u, :], start=True, stop=True)
            last.then_inc(qk_done, 1)
            pe.wait_ge(n_ready, 1)
            pe.wait_ge(ecols, 3)
            pe.wait_ge(diff_done, 1)
            for u in range(UNITS):
                last = nc.tensor.transpose(pb[:, u, :], pt[0][:, u, :], core.c("ident"))
            last.then_inc(nt_back, 1)
            pe.wait_ge(p_ready, 2)
            for u in range(UNITS):
                last = nc.tensor.transpose(pb[:, u, :], kT[:, u, :], core.c("ident"))
            last.then_inc(kt_done, 1)
            pe.wait_ge(n_ready, 2)
            for it in range(ITER):
                old = it % 2
                for g in range(2):
                    pe.wait_ge(p_ready, 2 * it + g + 1)
                    if it:
                        pe.wait_ge(pt_ready, 2 * (it - 1) + g + 1)
                    for u in range(G4 * g, G4 * g + G4):
                        last = nc.tensor.matmul(pa[:, u, :], pt[old][:, u, :], pw[old][:, u, :], start=True, stop=True)
                    last.then_inc(pp_done, 1)
                    if it < ITER - 1:
                        for u in range(G4 * g, G4 * g + G4):
                            last = nc.tensor.matmul(pc[:, u, :], pw[old][:, u, :], pt[old][:, u, :], start=True, stop=True)
                        last.then_inc(ppt_done, 1)
                for g in range(2):
                    pe.wait_ge(p_ready, 2 * (it + 1) + g + 1)
                    pe.wait_ge(tt_ready, 2 * it + g + 1)
                    for u in range(G4 * g, G4 * g + G4):
                        last = nc.tensor.matmul(pd[:, u, :], pw[1 - old][:, u, :], TT[:, u, :], start=True, stop=True)
                    last.then_inc(tt_done, 1)
            pe.wait_ge(k_out, 1)
            pe.wait_ge(kg_out, 1)
            for u in range(UNITS):
                last = nc.tensor.transpose(pb[:, u, :], vT[:, u, :], core.c("ident"))
            last.then_inc(vt_done, 1)
            pe.wait_ge(tt_ready, 2 * ITER + 2)
            for u in range(UNITS):
                last = nc.tensor.matmul(pa[:, u, :], kbg[:, u, :], TT[:, u, :], start=True, stop=True)
            last.then_inc(w_done, 1)
            pe.wait_ge(v_out, 1)
            for u in range(UNITS):
                last = nc.tensor.matmul(pc[:, u, :], TT[:, u, :], vb[:, u, :], start=True, stop=True)
            last.then_inc(w_done, 1)
            pe.wait_ge(w_out, 1)
            pe.wait_ge(u_out, 1)
            pe.wait_ge(q_ready, 1)
            for n in range(S // CHUNK):
                half, r = n // 2, n % 2
                rows = slice(CHUNK * r, CHUNK * r + CHUNK)
                pe.wait_ge(state_ready, n + 1)
                for h in range(HEADS):
                    last = nc.tensor.matmul(pd[rows, h, :], wT[:, 2 * h + half, rows], state[:, h, :],
                                            start=True, stop=True)
                last.then_inc(ws_done, 1)
                pe.wait_ge(vn_ready, n + 1)
                if n:
                    pe.wait_ge(o_out, n)
                for h in range(HEADS):
                    nc.tensor.matmul(pb[:, h, 0:CHUNK], state[:, h, :], qT[:, 2 * h + half, rows],
                                     start=True, stop=False)
                    last = nc.tensor.matmul(pb[:, h, 0:CHUNK], v_new[rows, h, :], attnT[rows, 2 * h + half, rows],
                                            start=False, stop=True)
                last.then_inc(o_done, 1)
                if n < S // CHUNK - 1:
                    for h in range(HEADS):
                        last = nc.tensor.matmul(pc[:, h, :], kg[rows, 2 * h + half, :], v_new[rows, h, :],
                                                start=True, stop=True)
                    last.then_inc(st_done, 1)
            pe.wait_ge(o_sq, 1)
            for g in range(2):
                at = slice(G4 * g, G4 * g + G4)
                last = nc.tensor.matmul(pa[:, at, :], core.c("ones"), pw[0][:, at, :], start=True, stop=True)
            last.then_inc(o_sum, 1)

        @block.scalar
        def _(act):
            act.wait_ge(cols_out, 2)
            nc.scalar.activation(ecol, gcol, ACT.Exp).then_inc(ecols, 1)
            nc.scalar.activation(kgs, left, ACT.Exp).then_inc(ecols, 1)
            act.wait_ge(diff_done, 1)
            nc.scalar.activation(egrow[:, :, :], pb[:, :, :], ACT.Exp).then_inc(ecols, 1)
            nc.scalar.activation(decay[:, :, :], decay[:, :, :], ACT.Exp).then_inc(decay_done, 1)
            act.wait_ge(nt_back, 1)
            for g in range(2):
                at = slice(G4 * g, G4 * g + G4)
                nc.scalar.activation(pw[0][:, at, :], pb[:, at, :], ACT.Copy).then_inc(p_ready, 1)
            act.wait_ge(kt_done, 1)
            act.wait_ge(masked, 2)
            for u in range(UNITS):
                last = nc.scalar.activation(kbg[:, u, :], pb[:, u, :], ACT.Copy, scale=bec[:, u:u + 1])
            last.then_inc(k_out, 1)
            for it in range(ITER):
                for g in range(2):
                    act.wait_ge(pp_done, 2 * it + g + 1)
                    at = slice(G4 * g, G4 * g + G4)
                    nc.scalar.activation(pw[1 - it % 2][:, at, :], pa[:, at, :], ACT.Copy).then_inc(p_ready, 1)
            act.wait_ge(vt_done, 1)
            for u in range(UNITS):
                last = nc.scalar.activation(vb[:, u, :], pb[:, u, :], ACT.Copy, scale=beta8[:, u:u + 1])
            last.then_inc(v_out, 1)
            act.wait_ge(w_done, 1)
            nc.scalar.activation(wT[:, :, :], pa[:, :, :], ACT.Copy).then_inc(w_out, 1)
            for n in range(S // CHUNK):
                act.wait_ge(o_done, n + 1)
                nc.scalar.activation(oT[:, :, :].rearrange("p (h a) c -> p h (a c)", a=HALVES)[:, :, n * CHUNK:(n + 1) * CHUNK],
                                     pb[:, 0:HEADS, 0:CHUNK], ACT.Copy).then_inc(o_out, 1)
            act.wait_ge(o_out, S // CHUNK)
            nc.scalar.activation(pw[0][:, :, :], oT[:, :, :], ACT.Square).then_inc(o_sq, 1)
            nc.scalar.activation(attnT[:, :, :].rearrange("p (h a) c -> p h (a c)", a=HALVES),
                                 proj[:, Z:Z + 4, PAD:PAD + S], ACT.Silu).then_inc(z_done, 1)
            act.wait_ge(o_var, 1)
            nc.scalar.activation(pw[1][:, :, :], TT[:, :, :], ACT.Abs_reciprocal_sqrt).then_inc(o_root, 1)

        @block.vector
        def _(dve):
            chain = Chain(dve, own)
            nc.vector.tensor_tensor(g_diag[:, :, :], over_units(core.c("causal64")),
                                    g8.unsqueeze(2).to_broadcast([P, UNITS, P]), ALU.mult).then_inc(diag, 1)
            nc.vector.tensor_tensor(b_diag[:, :, :], over_units(core.c("ident")),
                                    beta8.unsqueeze(2).to_broadcast([P, UNITS, P]), ALU.mult).then_inc(diag, 1)
            nc.vector.memset(state[:, :, :], 0.0).then_inc(state_ready, 1)
            dve.wait_ge(cols_done, 1)
            nc.vector.tensor_copy(cols[:, 0:2, :].rearrange("p a b -> p (a b)"), pa[:, 0, 0:2 * UNITS]).then_inc(cols_out, 1)
            dve.wait_ge(cols_out, 1)
            nc.vector.tensor_tensor(left, tot, gcol, ALU.subtract).then_inc(cols_out, 1)
            dve.wait_ge(rows_done, 1)
            for u in range(UNITS):
                last = nc.vector.tensor_scalar(decay[:, u, :], pb[:, u, :], gcol[:, u:u + 1], 0.0, ALU.subtract, ALU.min)
            last.then_inc(diff_done, 1)
            dve.wait_ge(decay_done, 1)
            nc.vector.tensor_tensor(decay[:, :, :], decay[:, :, :], over_units(core.c("causal64")), ALU.mult).then_inc(masked, 1)
            dve.wait_ge(ecols, 3)
            nc.vector.tensor_tensor(bec, beta8, ecol, ALU.mult).then_inc(masked, 1)
            dve.wait_ge(masked, 2)
            dve.wait_ge(kk_done, 1)
            chain.do(nc.vector.tensor_tensor(pt[0][:, :, :], pd[:, :, :], decay[:, :, :], ALU.mult))
            dve.wait_ge(rows_done, 2)
            chain.do(nc.vector.tensor_tensor(pt[0][:, :, :], pc[:, :, :], pt[0][:, :, :], ALU.mult))
            nc.vector.tensor_tensor(pt[0][:, :, :], pt[0][:, :, :], over_units(core.c("neg_strict64")), ALU.mult).then_inc(n_ready, 1)
            dve.wait_ge(qk_done, 1)
            nc.vector.tensor_tensor(attnT[:, :, :], pa[:, :, :], decay[:, :, :], ALU.mult).then_inc(n_ready, 1)
            dve.wait_ge(n_ready, 1)
            for g in range(2):
                at = slice(G4 * g, G4 * g + G4)
                nc.vector.tensor_tensor(TT[:, at, :], pt[0][:, at, :],
                                        core.c("ident").unsqueeze(1).to_broadcast([P, G4, P]), ALU.add).then_inc(tt_ready, 1)
            dve.wait_ge(k_out, 1)
            for u in range(UNITS):
                last = nc.vector.tensor_scalar(kg[:, u, :], pb[:, u, :], kgs[:, u:u + 1], None, ALU.mult)
            last.then_inc(kg_out, 1)
            nc.vector.tensor_tensor(qT, qT, egrow[:, :, :], ALU.mult).then_inc(q_ready, 1)
            for it in range(ITER):
                if it < ITER - 1:
                    for g in range(2):
                        at = slice(G4 * g, G4 * g + G4)
                        dve.wait_ge(ppt_done, 2 * it + g + 1)
                        nc.vector.tensor_copy(pt[1 - it % 2][:, at, :], pc[:, at, :]).then_inc(pt_ready, 1)
                for g in range(2):
                    at = slice(G4 * g, G4 * g + G4)
                    dve.wait_ge(tt_done, 2 * it + g + 1)
                    dve.wait_ge(tt_ready, 2 * it + g + 1)
                    nc.vector.tensor_tensor(TT[:, at, :], pd[:, at, :], TT[:, at, :], ALU.add).then_inc(tt_ready, 1)
            dve.wait_ge(w_done, 2)
            nc.vector.tensor_copy(u_sb[:, :, :], pc[:, :, :]).then_inc(u_out, 1)
            u_by = u_sb[:, :, :].rearrange("p (h a) d -> p h a d", a=HALVES)
            for n in range(S // CHUNK):
                half, r = n // 2, n % 2
                rows = slice(CHUNK * r, CHUNK * r + CHUNK)
                dve.wait_ge(ws_done, n + 1)
                if n == 0:
                    dve.wait_ge(u_out, 1)
                nc.vector.tensor_tensor(v_new[rows, 0:HEADS, :], u_by[rows, :, half, :], pd[rows, 0:HEADS, :],
                                        ALU.subtract).then_inc(vn_ready, 1)
                if n < S // CHUNK - 1:
                    dve.wait_ge(st_done, n + 1)
                    for h in range(HEADS):
                        end = egrow[:, 2 * h + half, CHUNK * r + CHUNK - 1:CHUNK * r + CHUNK]
                        last = nc.vector.scalar_tensor_tensor(state[:, h, :], state[:, h, :], end, pc[:, h, :],
                                                              ALU.mult, ALU.add)
                    last.then_inc(state_ready, 1)
                    dve.wait_ge(state_ready, n + 2)
            dve.wait_ge(o_sum, 1)
            nc.vector.tensor_scalar(TT[:, :, :], pa[:, :, :], 1.0 / HD, EPS, ALU.mult, ALU.add).then_inc(o_var, 1)
            dve.wait_ge(o_root, 1)
            newton_rsqrt(nc, chain, pw[1][:, :, :], TT[:, :, :], pt[0][:, :, :])
            chain.do(nc.vector.tensor_tensor(pw[1][:, :, :], pw[1][:, :, :], oT[:, :, :], ALU.mult))
            dve.wait_ge(z_done, 1)
            chain.do(nc.vector.scalar_tensor_tensor(
                proj[:, Z:Z + 4, PAD:PAD + S], pw[1][:, :, :].rearrange("p (h a) c -> p h (a c)", a=HALVES), core.v("gdn_norm"),
                attnT[:, :, :].rearrange("p (h a) c -> p h (a c)", a=HALVES), ALU.mult, ALU.mult))


def other_mixers_stage(core, proj, mix):
    nc = core.nc
    (weights_in, w_ready, w_zero, rx_done, gates_done, log_ready, exps_done, square_arg, root_done, lru_done, gelu_done,
     mean_done, centred, var_sq, var_done, var_root, v_ready, vt_done, vt_out, sg_done, own, sc_own, sc_done, sq_done,
     sum_done, root3, var_ready) = (
        core.sem(f"mix_{s}") for s in (
            "weights_in", "w_ready", "w_zero", "rx_done", "gates_done", "log_ready", "exps_done", "square_arg",
            "root_done", "lru_done", "gelu_done", "mean_done", "centred", "var_sq", "var_done", "var_root", "v_ready",
            "vt_done", "vt_out", "sg_done", "own", "sc_own", "sc_done", "sq_done", "sum_done", "root3", "var_ready"))
    conv, small, rows = mix["conv"], mix["small"], mix["rows"]
    xc = conv[:, 12:16, :]
    with ExitStack() as ctx:
        halves, spare = Region(core.h_mem[:, :, :, :].rearrange("p k c s -> p (k c s)")), Region(mix["spare"])
        lru_w = spare.take(2, 4, P)
        sgu_w = spare.take(4, P)
        bufs = halves.take(4, 4, S)
        a_, r_, i_, t_ = (bufs[:, j, :, :] for j in range(4))
        gelu_u, gelu_v = (proj[:, at:at + 4, PAD:] for at in (SGU_U, SGU_V))
        outs = [proj[:, at:at + 4, PAD:] for at in MIXED]
        padded = halves.take(4, PAD + S)
        stat, tmp, root = (spare.take(3, S) for _ in range(3))
        gelu_g = conv[:, 0:4, :]
        vtok = conv[:, 4:8, :]
        sq = bufs
        p_r = core.ps("ps_r", [P, 4, S], ctx)
        p_x = core.ps("ps_x", [P, 4, S], ctx)
        p_s = core.ps("ps_stat", [P, 2, S], ctx)
        p_n = core.ps("ps_norms", [P, 4, S], ctx)
        block = ctx.enter_context(nc.Block())
        bs = rows[:, 8:8 + 512].rearrange("p (g t) -> p g t", g=4)

        def quarter(ap):
            return ap.rearrange("p j s -> p (j s)").rearrange("p (u c) -> p u c", c=P)

        vt, p_vt, p_sg = quarter(vtok), quarter(p_r[:, :, :]), quarter(p_x[:, :, :])

        @block.sync
        def _(sp):
            sp.wait_ge(w_zero, 1)
            for m, name in enumerate(("lru_wa", "lru_wx")):
                src = core.d[name].rearrange("(j b) i o -> b i j o", b=2)
                for b in range(2):
                    at = slice(64 * b, 64 * b + 64)
                    sp.dma_start(lru_w[at, m, :, at], src[b]).then_inc(weights_in, 16)
            sp.dma_start(sgu_w[:, :, :], core.d["sgu_ws"]).then_inc(weights_in, 16)

        @block.gpsimd
        def _(pool):
            nc.gpsimd.memset(lru_w[:, :, :, :], 0.0).then_inc(w_zero, 1)
            steps = Chain(pool, sc_own)
            steps.add(nc.gpsimd.memset(padded[:, :, 0:PAD], 0.0))
            steps.do(nc.gpsimd.tensor_tensor(padded[:, :, PAD:], proj[:, SC_C:SC_C + 4, PAD:], proj[:, SC_H:SC_H + 4, PAD:],
                                             ALU.mult))
            out = outs[3]
            tap = conv[:, 8:12, :]
            for o in range(3):
                for j in range(4):
                    steps.add(nc.gpsimd.tensor_scalar((tap if o else out)[:, j, :], padded[:, j, PAD - o:PAD - o + S],
                                                      core.v("sconv", 3 * j + 2 - o), None, ALU.mult))
                steps.settle()
                if o:
                    steps.do(nc.gpsimd.tensor_tensor(out, out, tap, ALU.add))
            nc.gpsimd.tensor_tensor(out, out, proj[:, SC_B:SC_B + 4, PAD:], ALU.mult).then_inc(sc_done, 1)

        @block.tensor
        def _(pe):
            pe.wait_ge(weights_in, 80)
            for m, out in enumerate((p_r, p_x)):
                for j in range(4):
                    last = nc.tensor.matmul(out[:, j, :], lru_w[:, m, j, :], xc[:, j, :], start=True, stop=True)
                last.then_inc(rx_done, 1)
            pe.wait_ge(gelu_done, 2)
            for j in range(4):
                last = nc.tensor.matmul(p_s[:, 0, :], core.c("ones"), gelu_v[:, j, :], start=(j == 0), stop=(j == 3))
            last.then_inc(mean_done, 1)
            pe.wait_ge(var_sq, 1)
            for j in range(4):
                last = nc.tensor.matmul(p_s[:, 1, :], core.c("ones"), t_[:, j, :], start=(j == 0), stop=(j == 3))
            last.then_inc(var_done, 1)
            pe.wait_ge(v_ready, 1)
            pe.wait_ge(gates_done, 8)
            for g in range(4):
                for half in range(HALVES):
                    last = nc.tensor.transpose(p_vt[:, 2 * g + half, :], gelu_v[:, g, half * P:(half + 1) * P],
                                               core.c("ident"))
            last.then_inc(vt_done, 1)
            pe.wait_ge(vt_out, 1)
            pe.wait_ge(w_ready, 1)
            for g in range(4):
                for half in range(HALVES):
                    last = nc.tensor.matmul(p_sg[:, 2 * g + half, :], vt[:, 2 * g + half, :], sgu_w[:, g, :],
                                            start=True, stop=True)
            last.then_inc(sg_done, 1)
            for m in range(3):
                pe.wait_ge(sq_done, m + 1)
                for j in range(4):
                    last = nc.tensor.matmul(p_n[:, m, :], core.c("ones"), sq[:, m, j, :], start=(j == 0), stop=(j == 3))
                last.then_inc(sum_done, 1)

        @block.scalar
        def _(act):
            nc.scalar.activation(gelu_v, proj[:, SGU_V:SGU_V + 4, PAD:], ACT.Gelu_apprx_tanh).then_inc(gelu_done, 1)
            nc.scalar.activation(gelu_u, proj[:, SGU_U:SGU_U + 4, PAD:], ACT.Gelu_apprx_tanh).then_inc(gelu_done, 1)
            nc.scalar.activation(gelu_g, proj[:, LRU_G:LRU_G + 4, PAD:], ACT.Gelu_apprx_tanh).then_inc(gelu_done, 1)
            for m, (src, dst, bias) in enumerate(((p_r, r_, "lru_ba"), (p_x, i_, "lru_bx"))):
                act.wait_ge(rx_done, m + 1)
                for j in range(4):
                    nc.scalar.activation(dst[:, j, :], src[:, j, :], ACT.Sigmoid, bias=core.v(bias, j)).then_inc(gates_done, 1)
            act.wait_ge(log_ready, 1)
            nc.scalar.activation(a_, r_, ACT.Exp).then_inc(exps_done, 1)
            nc.scalar.activation(r_, r_, ACT.Tanh).then_inc(exps_done, 1)
            act.wait_ge(centred, 1)
            nc.scalar.activation(t_, gelu_v, ACT.Square).then_inc(var_sq, 1)
            act.wait_ge(square_arg, 1)
            nc.scalar.activation(r_, r_, ACT.Sqrt).then_inc(root_done, 1)
            act.wait_ge(var_ready, 1)
            nc.scalar.activation(root[:, 0, :], stat[:, 1, :], ACT.Abs_reciprocal_sqrt).then_inc(var_root, 1)
            act.wait_ge(vt_done, 1)
            nc.scalar.activation(vt, p_vt, ACT.Copy).then_inc(vt_out, 1)
            for m, ready in enumerate((lru_done, lru_done, sc_done)):
                act.wait_ge(ready, (1, 2, 1)[m])
                nc.scalar.activation(sq[:, m, :, :], outs[1 + m], ACT.Square).then_inc(sq_done, 1)
            act.wait_ge(var_ready, 2)
            nc.scalar.activation(root[:, :, :], stat[:, :, :], ACT.Abs_reciprocal_sqrt).then_inc(root3, 1)

        @block.vector
        def _(dve):
            chain = Chain(dve, own)

            def each_tile(ap):
                return ap.unsqueeze(1).to_broadcast([P, 4, S])

            dve.wait_ge(weights_in, 80)
            nc.vector.tensor_tensor(sgu_w[:, :, :], sgu_w[:, :, :], core.c("causal128").unsqueeze(1).to_broadcast([P, 4, P]),
                                    ALU.mult).then_inc(w_ready, 1)
            dve.wait_ge(gates_done, 8)
            for j in range(4):
                last = nc.vector.tensor_scalar(r_[:, j, :], r_[:, j, :], small["lru_c"][:, j:j + 1], None, ALU.mult)
            last.then_inc(log_ready, 1)
            chain.do(nc.vector.tensor_tensor(i_, i_, xc, ALU.mult))
            dve.wait_ge(mean_done, 1)
            chain.do(nc.vector.tensor_scalar(stat[:, 0, :], p_s[:, 0, :], 1.0 / 512, None, ALU.mult))
            nc.vector.tensor_tensor(gelu_v, gelu_v, each_tile(stat[:, 0, :]), ALU.subtract).then_inc(centred, 1)
            dve.wait_ge(exps_done, 2)
            dve.wait_ge(var_sq, 1)
            dve.wait_ge(var_done, 1)
            chain.do(nc.vector.tensor_tensor(t_, a_, a_, ALU.mult))
            chain.do(nc.vector.scalar_tensor_tensor(r_, t_, 1.0, r_, ALU.add, ALU.mult))
            nc.vector.tensor_scalar(r_, r_, -1.0, 1e-34, ALU.mult, ALU.max).then_inc(square_arg, 1)
            nc.vector.tensor_scalar(stat[:, 1, :], p_s[:, 1, :], 1.0 / 512, EPS, ALU.mult, ALU.add).then_inc(var_ready, 1)
            dve.wait_ge(var_root, 1)
            newton_rsqrt(nc, chain, root[:, 0, :], stat[:, 1, :], tmp[:, 0, :])
            for j in range(4):
                chain.add(nc.vector.scalar_tensor_tensor(gelu_v[:, j, :], gelu_v[:, j, :], core.v("ln_w", j), root[:, 0, :],
                                                         ALU.mult, ALU.mult))
            chain.settle()
            for j in range(4):
                last = nc.vector.tensor_scalar(gelu_v[:, j, :], gelu_v[:, j, :], core.v("ln_b", j), None, ALU.add)
            last.then_inc(v_ready, 1)
            dve.wait_ge(root_done, 1)
            chain.do(nc.vector.tensor_tensor(i_, i_, r_, ALU.mult))
            for j in range(4):
                chain.add(nc.vector.tensor_tensor_scan(t_[:, j, :], a_[:, j, :], i_[:, j, :], 0.0, ALU.mult, ALU.add))
            chain.settle()
            dve.wait_ge(gelu_done, 3)
            nc.vector.tensor_tensor(outs[1], t_, gelu_g, ALU.mult).then_inc(lru_done, 1)
            dve.wait_ge(sg_done, 1)
            chain.do(nc.vector.tensor_tensor(
                gelu_v.rearrange("p g (a c) -> p g a c", a=HALVES), p_sg.rearrange("p (g a) c -> p g a c", a=HALVES),
                bs.unsqueeze(2).to_broadcast([P, 4, HALVES, P]), ALU.add))
            nc.vector.tensor_tensor(outs[2], gelu_v, gelu_u, ALU.mult).then_inc(lru_done, 1)
            dve.wait_ge(sum_done, 3)
            nc.vector.tensor_scalar(stat[:, :, :], p_n[:, 0:3, :], 1.0 / 512, EPS, ALU.mult, ALU.add).then_inc(var_ready, 1)
            dve.wait_ge(root3, 1)
            newton_rsqrt(nc, chain, root[:, :, :], stat[:, :, :], tmp[:, :, :])
            for m in range(3):
                for j in range(4):
                    out = outs[1 + m][:, j, :]
                    nc.vector.scalar_tensor_tensor(out, out, core.v("grp", 4 * m + j), root[:, m, :],
                                                   ALU.mult, ALU.mult)



DQ, DK, FQ, FK, DV, FV, G_DIL, G_DIFF = 0, 12, 24, 32, 40, 52, 60, 76
MIX_TILES = 92
MIX_ORDER = [*range(0, 24), *range(36, 52), *range(24, 36), *range(52, 92)]
GROUPS = 3
ROPE = 32
ROPE_THETA = 500000.0
DILATIONS = ((128, 1), (512, 4), (2048, 16))
LAM_INIT = 0.8 - 0.6 * float(np.exp(-0.3 * 0))
MASKED = -1e30
TWO_PI = (6.28125, 0.0019350051879882812, 3.0199159819567e-07)
ROUND = 1.5 * 2.0 ** 23


class Rotary:

    def __init__(self, core, ctx):
        self.core, self.nc = core, core.nc
        self.pos_in, self.own, self.angle, self.dot_done, self.dot_in, self.exp_done = (
            core.sem(f"rotary_{s}") for s in ("pos_in", "own", "angle", "dot_done", "dot_in", "exp_done"))
        self.pos_i = core.sb("pos_i", [ROPE, S], I32, ctx)
        self.dots = core.sb("lam_dots", [P, 2], F32, ctx)
        self.exps = core.sb("lam_exps", [P, 2], F32, ctx)
        self.ang = core.arena[0:ROPE, ARENA_TILES - 1, :]
        self.turns = core.arena[0:ROPE, ARENA_TILES - 3:ARENA_TILES - 1, :]
        self.p_dot = core.ps("ps_dot", [P, 2], ctx)

    def load(self, sp):
        sp.dma_start(self.pos_i[:, :], self.core.d["positions"].partition_broadcast(ROPE)).then_inc(self.pos_in, 16)

    def angles(self, dve):
        nc, core, ang, turns, trig = self.nc, self.core, self.ang, self.turns, self.core.trig
        chain = Chain(dve, self.own)
        lq = core.v("lam", 0, 4)
        nc.vector.tensor_tensor(self.dots[:, 0:1], lq[:, 0:1], lq[:, 1:2], ALU.mult).then_inc(self.dot_in, 1)
        nc.vector.tensor_tensor(self.dots[:, 1:2], lq[:, 2:3], lq[:, 3:4], ALU.mult).then_inc(self.dot_in, 1)
        dve.wait_ge(self.pos_in, 16)
        chain.do(nc.vector.tensor_copy(ang, self.pos_i[:, :]))
        chain.do(nc.vector.tensor_scalar(ang, ang, core.c("inv_freq")[0:ROPE, :], None, ALU.mult))
        for j, ahead in enumerate((0.25, 0.0)):
            chain.do(nc.vector.tensor_scalar(turns[:, j, :], ang, 0.5 / float(np.pi), ahead, ALU.mult, ALU.add))
        chain.do(nc.vector.tensor_scalar(turns, turns, ROUND, None, ALU.add))
        chain.do(nc.vector.tensor_scalar(turns, turns, -ROUND, None, ALU.add))
        for j in range(2):
            chain.do(nc.vector.scalar_tensor_tensor(trig[:, j, :], turns[:, j, :], -TWO_PI[0], ang, ALU.mult, ALU.add))
        for part in TWO_PI[1:]:
            chain.do(nc.vector.scalar_tensor_tensor(trig[:, :, :], turns, -part, trig[:, :, :], ALU.mult, ALU.add))
        chain.do(nc.vector.tensor_scalar(trig[:, 0, :], trig[:, 0, :], float(np.pi / 2), None, ALU.add))
        nc.vector.tensor_scalar(trig[:, :, :], trig[:, :, :], 3.1415925, -3.1415925, ALU.min, ALU.max).then_inc(self.angle, 1)
        return chain

    def dot(self, pe):
        pe.wait_ge(self.dot_in, 2)
        self.nc.tensor.matmul(self.p_dot[:, :], self.core.c("ones"), self.dots[:, :], start=True, stop=True).then_inc(self.dot_done, 1)

    def sines(self, act):
        act.wait_ge(self.angle, 1)
        self.nc.scalar.activation(self.core.trig[:, :, :], self.core.trig[:, :, :], ACT.Sin).then_inc(self.angle, 1)
        act.wait_ge(self.dot_done, 1)
        self.nc.scalar.activation(self.exps[:, :], self.p_dot[:, :], ACT.Exp).then_inc(self.exp_done, 1)

    def finish(self, dve, chain):
        nc, core, trig, lam, exps = self.nc, self.core, self.core.trig, self.core.lam, self.exps
        dve.wait_ge(self.angle, 2)
        nc.vector.tensor_scalar(trig[:, 1, :], trig[:, 1, :], core.c("rope_sign")[0:ROPE, :], None, ALU.mult)
        dve.wait_ge(self.exp_done, 1)
        chain.do(nc.vector.tensor_tensor(lam[:, 0:1], exps[:, 0:1], exps[:, 1:2], ALU.subtract))
        chain.do(nc.vector.tensor_scalar(lam[:, 0:1], lam[:, 0:1], LAM_INIT, None, ALU.add))
        nc.vector.tensor_scalar(lam[:, 1:3], core.v("subln", 0, 2), 1.0 - LAM_INIT, None, ALU.mult)


class Attention:

    SCALE = HD ** -0.5
    UNITS = [(False, h, a) for h in range(HEADS) for a in range(HALVES)] + \
            [(True, h, a) for h in range(HEADS) for a in range(HALVES)]

    def __init__(self, core, ctx, proj, lam, memory):
        self.core, self.nc, self.proj, self.lam = core, core.nc, proj, lam
        (self.masks_in, self.scores_done, self.logits, self.max_ready, self.exp_done, self.probs_ready, self.pt_done,
         self.pt_out, self.pv_done, self.out_done, self.own, self.sq_ready, self.sum_done, self.var_ready,
         self.rooted) = (
            core.sem(f"attn_{s}") for s in ("masks_in", "scores_done", "logits", "max_ready", "exp_done", "probs_ready",
                                            "pt_done", "pt_out", "pv_done", "out_done", "own", "sq_ready", "sum_done",
                                            "var_ready", "rooted"))
        self.masks = memory[:, 0:8, :].rearrange("p (a m) s -> p a m s", a=HALVES)
        self.s_buf = memory[:, 10:16, :].rearrange("p (b j) s -> p b j s", b=2)
        self.pT = core.sb("probs_T", [P, 2 * GROUPS, P], F32, ctx)
        self.stats = core.sb("attn_stats", [P, 2, 8], F32, ctx)
        self.p_s = core.ps("ps_scores", [P, 4, S], ctx)
        self.p_t = core.ps("ps_probs_T", [P, 8, P], ctx)
        self.p_o = core.ps("ps_out", [P, 4, P], ctx)

    @staticmethod
    def q_tile(diff, h, j):
        return FQ + 2 * h + j if diff else DQ + 4 * j + h

    @staticmethod
    def k_tile(diff, h, j):
        return FK + 2 * h + j if diff else DK + 4 * j + h

    @staticmethod
    def mats(diff):
        return 1 if diff else GROUPS

    @staticmethod
    def parts_of(diff):
        return 2 if diff else GROUPS

    def exps_through(self, n):
        return sum(2 if self.UNITS[m][0] else 1 for m in range(n + 1))

    def scores(self, pe, n):
        diff, h, a = self.UNITS[n]
        if n:
            pe.wait_ge(self.logits, n)
        for j in range(self.parts_of(diff)):
            last = self.nc.tensor.matmul(self.p_s[:, j, 0:(a + 1) * P], self.proj[:, self.q_tile(diff, h, j), a * P:(a + 1) * P],
                                         self.proj[:, self.k_tile(diff, h, j), 0:(a + 1) * P], start=True, stop=True)
        last.then_inc(self.scores_done, 1)

    def transpose_probs(self, pe, n):
        diff, h, a = self.UNITS[n]
        pe.wait_ge(self.probs_ready, n + 1)
        if n:
            pe.wait_ge(self.pt_out, n)
        for j in range(self.mats(diff)):
            for b in range(a + 1):
                last = self.nc.tensor.transpose(self.p_t[:, j * 2 + b, :], self.s_buf[:, n % 2, j, b * P:(b + 1) * P],
                                                self.core.c("ident"))
        last.then_inc(self.pt_done, 1)

    def weigh_values(self, pe, n):
        diff, h, a = self.UNITS[n]
        pe.wait_ge(self.pt_out, n + 1)
        if n:
            pe.wait_ge(self.out_done, n)
        terms = [(j, b) for j in range(self.mats(diff)) for b in range(a + 1)]
        for e in range(2 if diff else 1):
            for m, (j, b) in enumerate(terms):
                v = FV + 2 * h + e if diff else DV + 4 * j + h
                last = self.nc.tensor.matmul(self.p_o[:, e, :], self.proj[:, v, b * P:(b + 1) * P], self.pT[:, j * 2 + b, :],
                                             start=(m == 0), stop=(m == len(terms) - 1))
        last.then_inc(self.pv_done, 1)

    def sum_squares(self, pe):
        pe.wait_ge(self.sq_ready, 1)
        for h in range(HEADS):
            for e in range(2):
                last = self.nc.tensor.matmul(self.p_s[:, h, :], self.core.c("ones"), self.proj[:, FK + 2 * h + e, :],
                                             start=(e == 0), stop=(e == 1))
        last.then_inc(self.sum_done, 1)

    def load_masks(self, act):
        act.dma_start(self.masks, self.core.d["masks"]).then_inc(self.masks_in, 16)

    def exps(self, act, n):
        diff, _, a = self.UNITS[n]
        act.wait_ge(self.max_ready, n + 1)
        s, st = self.s_buf[:, n % 2, :, :], self.stats[:, n % 2, :]
        if diff:
            for j in range(2):
                self.nc.scalar.activation(s[:, j, 0:(a + 1) * P], s[:, j, 0:(a + 1) * P], ACT.Exp, bias=st[:, 2 + j:3 + j],
                                          scale=self.SCALE, accum_out=st[:, 4 + j:5 + j]).then_inc(self.exp_done, 1)
        else:
            self.nc.scalar.activation(s[:, :, 0:(a + 1) * P], s[:, :, 0:(a + 1) * P], ACT.Exp, bias=st[:, 2:3],
                                      scale=self.SCALE, accum_out=st[:, 4:5]).then_inc(self.exp_done, 1)

    def take_probs(self, act, n):
        diff, _, a = self.UNITS[n]
        act.wait_ge(self.pt_done, n + 1)
        if n:
            act.wait_ge(self.pv_done, n)
        at = (slice(None), slice(0, self.mats(diff)), slice(0, a + 1), slice(None))
        self.nc.scalar.activation(self.pT[:, :, :].rearrange("p (j b) c -> p j b c", b=2)[at],
                                  self.p_t[:, 0:2 * GROUPS, :].rearrange("p (j b) c -> p j b c", b=2)[at],
                                  ACT.Copy).then_inc(self.pt_out, 1)

    def take_out(self, act, n):
        diff, h, a = self.UNITS[n]
        act.wait_ge(self.pv_done, n + 1)
        ne = 2 if diff else 1
        t = self.q_tile(diff, h, 0)
        self.nc.scalar.activation(self.proj[:, t:t + ne, a * P:(a + 1) * P], self.p_o[:, 0:ne, :],
                                  ACT.Copy).then_inc(self.out_done, 1)

    def finish_act(self, act):
        proj = self.proj
        act.wait_ge(self.out_done, len(self.UNITS))
        self.nc.scalar.activation(proj[:, FK:FK + 8, :], proj[:, FQ:FQ + 8, :], ACT.Square).then_inc(self.sq_ready, 1)
        act.wait_ge(self.var_ready, 1)
        self.nc.scalar.activation(proj[:, FK:FK + 4, :], proj[:, FK + 4:FK + 8, :],
                                  ACT.Abs_reciprocal_sqrt).then_inc(self.rooted, 1)

    def take_scores(self, dve, chain, n):
        diff, _, a = self.UNITS[n]
        nc, keys, nj = self.nc, (a + 1) * P, self.parts_of(diff)
        s, st = self.s_buf[:, n % 2, :, :], self.stats[:, n % 2, :]
        dve.wait_ge(self.scores_done, n + 1)
        if n >= 2:
            dve.wait_ge(self.pt_done, n - 1)
        mask = self.masks[:, a, 3:4, 0:keys].to_broadcast([P, 2, keys]) if diff else self.masks[:, a, 0:GROUPS, 0:keys]
        nc.vector.tensor_tensor(s[:, 0:nj, 0:keys], self.p_s[:, 0:nj, 0:keys], mask, ALU.add).then_inc(self.logits, 1)
        dve.wait_ge(self.logits, n + 1)
        if diff:
            chain.do(nc.vector.reduce_max(st[:, 0:2], s[:, 0:2, 0:keys], AX))
            nc.vector.tensor_scalar(st[:, 2:4], st[:, 0:2], -self.SCALE, None, ALU.mult).then_inc(self.max_ready, 1)
        else:
            chain.do(nc.vector.tensor_reduce(st[:, 0:1], s[:, 0:nj, 0:keys], mybir.AxisListType.XY, ALU.max))
            nc.vector.tensor_scalar(st[:, 2:3], st[:, 0:1], -self.SCALE, None, ALU.mult).then_inc(self.max_ready, 1)

    def normalize(self, dve, chain, n):
        diff, _, a = self.UNITS[n]
        nc, keys = self.nc, (a + 1) * P
        s, st = self.s_buf[:, n % 2, :, :], self.stats[:, n % 2, :]
        dve.wait_ge(self.exp_done, self.exps_through(n))
        if diff:
            chain.do(nc.vector.reciprocal(st[:, 6:8], st[:, 4:6]))
            chain.do(nc.vector.tensor_tensor(st[:, 7:8], st[:, 7:8], self.lam[:, 0:1], ALU.mult))
            chain.do(nc.vector.tensor_scalar(s[:, 1, 0:keys], s[:, 1, 0:keys], st[:, 7:8], None, ALU.mult))
            nc.vector.scalar_tensor_tensor(s[:, 0, 0:keys], s[:, 0, 0:keys], st[:, 6:7], s[:, 1, 0:keys],
                                           ALU.mult, ALU.subtract).then_inc(self.probs_ready, 1)
        else:
            chain.do(nc.vector.reciprocal(st[:, 6:7], st[:, 4:5]))
            nc.vector.tensor_scalar(s[:, :, 0:keys], s[:, :, 0:keys], st[:, 6:7], None, ALU.mult).then_inc(self.probs_ready, 1)

    def finish_dve(self, dve, chain):
        nc, proj = self.nc, self.proj
        dve.wait_ge(self.sum_done, 1)
        var, y = proj[:, FK + 4:FK + 8, :], proj[:, FK:FK + 4, :]
        nc.vector.tensor_scalar(var, self.p_s[:, :, :], 1.0 / (2 * HD), EPS, ALU.mult, ALU.add).then_inc(self.var_ready, 1)
        dve.wait_ge(self.rooted, 1)
        newton_rsqrt(nc, chain, y, var, proj[:, DK:DK + 4, :])
        for e in range(2):
            out = proj[:, FQ:FQ + 8, :].rearrange("p (h e) s -> p h e s", e=2)[:, :, e, :]
            nc.vector.scalar_tensor_tensor(out, out, self.lam[:, 1 + e:2 + e], y, ALU.mult, ALU.mult)


def mix_in_stage(core, prod, operand_of, proj, trig, lam, following):
    nc = core.nc
    kept, squared, summed, var_ready, rooted, own, normed, pool_own, vt_done, vt_out, rotated, swapped, back = (
        core.sem(f"heads_{s}") for s in ("x_kept", "squared", "summed", "var_ready", "rooted", "own", "normed", "pool_own",
                                         "vt_done", "vt_out", "rotated", "swapped", "back"))
    QK_BODIES, V_BODIES = DV // 2, (G_DIL - DV) // 2
    with ExitStack() as ctx:
        acc = core.ps(f"acc_{core.chunk}", [P, 2, 2, S], ctx)
        y, var, tmp, swap, root = (core.x[:, 2 * j:2 * j + 2, :] for j in (0, 1, 2, 3, 5))
        swap = swap[0:ROPE, :, :]
        values = core.x[:, 8:10, :]
        operand = operand_of(ctx)
        scale = operand.scale
        p_sq, p_v = operand.bank, operand.bank[:, :, :].rearrange("p j (b c) -> p (j b) c", b=2)
        attention = Attention(core, ctx, proj, lam, core.x)
        FIRST = QK_BODIES + V_BODIES
        assert prod.bodies - FIRST == len(attention.UNITS)
        block = ctx.enter_context(nc.Block())

        def pair(m):
            return proj[:, bass.ds(2 * m, 2), :]

        def body_scaled(eng, m):
            eng.wait_ge(core.z_free, m * 2 + (2 + core.scaled + 2))

        @block.sync
        def _(sp):
            sp.dma_start(core.d["x_kept"], core.x[:, :, :]).then_inc(kept, 16)
            stream(core, sp, prod, following)

        @block.scalar
        def _(act):
            def walk(lo, hi):
                return steps(core, act, prod, split_high, lo, hi, following=following if hi == prod.bodies else None)

            for i, t in walk(0, 1):
                take_cross(core, act, prod, acc, i, t)
                if t == 0:
                    scale.root(act)
            act.wait_ge(kept, 16)
            act.sem_inc(back, 1)

            def head_step(i, t):
                if t == 0:
                    body_scaled(act, i - 1)
                    act.wait_ge(normed, i)
                    core.carry_wait(act)
                    nc.scalar.activation(root, pair(i - 1), ACT.Square).then_inc(squared, 1)
                else:
                    act.wait_ge(var_ready, i)
                    nc.scalar.activation(root, var, ACT.Abs_reciprocal_sqrt).then_inc(rooted, 1)

            def put_back(i):
                act.wait_ge(rotated, i - 1)
                core.carry_wait(act)
                nc.scalar.activation(pair(i - 2), y, ACT.Copy).then_inc(back, 1)

            def value_step(i, t):
                if t == 1:
                    act.wait_ge(vt_done, i - (QK_BODIES - 1))
                    core.carry_wait(act)
                    nc.scalar.activation(pair(i - 1), operand.bank[:, :, :],
                                         ACT.Copy).then_inc(vt_out, 1)

            for i, t in walk(1, 2):
                head_step(i, t)
                take_cross(core, act, prod, acc, i, t)
            for i, t in walk(2, 1 + QK_BODIES):
                if t == 1:
                    put_back(i)
                head_step(i, t)
                take_cross(core, act, prod, acc, i, t)
            for i, t in walk(1 + QK_BODIES, 2 + QK_BODIES):
                if t == 1:
                    put_back(i)
                    act.wait_ge(back, QK_BODIES + 1)
                    attention.load_masks(act)
                value_step(i, t)
                take_cross(core, act, prod, acc, i, t)
            for i, t in walk(2 + QK_BODIES, FIRST):
                value_step(i, t)
                take_cross(core, act, prod, acc, i, t)
            for n in range(prod.bodies - FIRST):
                for i, t in walk(FIRST + n, FIRST + n + 1):
                    if n == 0:
                        value_step(i, t)
                    if t == 1:
                        attention.exps(act, n)
                    take_cross(core, act, prod, acc, i, t)
                    if n and t == 0:
                        attention.take_probs(act, n - 1)
                    if n and t == 1:
                        attention.take_out(act, n - 1)
            attention.take_probs(act, n)
            attention.take_out(act, n)
            attention.finish_act(act)

        @block.vector
        def _(dve):
            def walk(lo, hi):
                return steps(core, dve, prod, split_low, lo, hi, following=following if hi == prod.bodies else None)

            dve.sem_inc(normed, 1)
            for i, t in walk(0, 1):
                take_for_scaling(core, dve, prod, acc, i, t)
                if t == 0:
                    scale.variance(dve)
                    scale.refine(dve)
            for i, t in walk(1, 1 + QK_BODIES):
                if t == 1:
                    dve.wait_ge(summed, i)
                    nc.vector.tensor_scalar(var, p_sq[:, :, :], 1.0 / HD, EPS, ALU.mult, ALU.add).then_inc(var_ready, 1)
                take_for_scaling(core, dve, prod, acc, i, t)
                if t == 1:
                    here = pair(i - 1)
                    dve.wait_ge(rooted, i)
                    nc.vector.tensor_tensor(tmp, root, root, ALU.mult).then_inc(own, 1)
                    dve.wait_ge(own, i * 3 - 2)
                    nc.vector.scalar_tensor_tensor(tmp, tmp, -0.5, var, ALU.mult, ALU.mult).then_inc(own, 1)
                    dve.wait_ge(own, i * 3 - 1)
                    nc.vector.scalar_tensor_tensor(root, tmp, 1.5, root, ALU.add, ALU.mult).then_inc(own, 1)
                    dve.wait_ge(own, i * 3)
                    dve.wait_ge(back, i)
                    nc.vector.scalar_tensor_tensor(y, here, core.v("head_gain", i - 1), root, ALU.mult,
                                                   ALU.mult).then_inc(normed, 1)
                    dve.wait_ge(normed, i + 1)
                    core.carry_wait(dve)
                    nc.vector.stream_shuffle(swap.rearrange("p j s -> p (j s)"), y[0:ROPE, :, :].rearrange("p j s -> p (j s)"),
                                             [(p + ROPE // 2) % ROPE for p in range(ROPE)]).then_inc(swapped, 1)
            for i, t in walk(1 + QK_BODIES, FIRST):
                take_for_scaling(core, dve, prod, acc, i, t)
            chain = Chain(dve, attention.own)
            dve.wait_ge(attention.masks_in, 16)
            for n in range(prod.bodies - FIRST):
                for i, t in walk(FIRST + n, FIRST + n + 1):
                    take_for_scaling(core, dve, prod, acc, i, t)
                    if t == 0:
                        attention.take_scores(dve, chain, n)
                    else:
                        attention.normalize(dve, chain, n)
            attention.finish_dve(dve, chain)

        @block.gpsimd
        def _(pool):
            def each(ap):
                return ap.unsqueeze(1).to_broadcast([ROPE, 2, S])

            pool.sem_inc(vt_out, 1)
            pool.sem_inc(vt_done, 1)

            def scale_body(i):
                for t in range(2):
                    scale_tile(core, pool, prod, proj[:, 2 * i + t, :], i, t)

            def scale_values(i):
                pool.wait_ge(vt_done, i - (QK_BODIES - 1))
                for t in range(2):
                    scale_tile(core, pool, prod, values[:, t, :], i, t)

            def rotate(i):
                here = y[0:ROPE, :, :]
                pool.wait_ge(swapped, i)
                nc.gpsimd.tensor_tensor(swap, swap, each(trig[:, 1, :]), ALU.mult).then_inc(pool_own, 1)
                nc.gpsimd.tensor_tensor(here, here, each(trig[:, 0, :]), ALU.mult).then_inc(pool_own, 1)
                pool.wait_ge(pool_own, i * 2)
                nc.gpsimd.tensor_tensor(here, here, swap, ALU.add).then_inc(rotated, 1)

            scale.ready(pool)
            scale_body(0)
            with pool.Fori(1, QK_BODIES) as i:
                scale_body(i)
                rotate(i)
            scale_values(QK_BODIES)
            rotate(QK_BODIES)
            with pool.Fori(QK_BODIES + 1, QK_BODIES + V_BODIES) as i:
                scale_values(i)
            with pool.Fori(QK_BODIES + V_BODIES, prod.bodies) as i:
                scale_body(i)

        @block.tensor
        def _(pe):
            for i, t in pe_steps(core, pe, prod, acc, 0, 1, before=operand.on(pe)):
                if t == 0:
                    operand.after_first(pe)
            pe.wait_ge(core.var_ready, scale.norm + 1)
            for i, t in pe_steps(core, pe, prod, acc, 1, 1 + QK_BODIES):
                if t == 0:
                    pe.wait_ge(squared, i)
                    nc.tensor.matmul(p_sq[:, :, :], core.c("ones"), root, start=True, stop=True).then_inc(summed, 1)
            def transpose_values(i):
                body_scaled(pe, i - 1)
                pe.wait_ge(vt_out, i - QK_BODIES)
                for j in range(2):
                    for half in range(HALVES):
                        last = nc.tensor.transpose(p_v[:, 2 * j + half, :], values[:, j, half * P:(half + 1) * P],
                                                   core.c("ident"))
                last.then_inc(vt_done, 1)

            pe.wait_ge(var_ready, QK_BODIES)
            for i, t in pe_steps(core, pe, prod, acc, 1 + QK_BODIES, FIRST):
                if t == 0:
                    transpose_values(i)
            pe.wait_ge(back, QK_BODIES + 1)
            for n in range(prod.bodies - FIRST):
                for i, t in pe_steps(core, pe, prod, acc, FIRST + n, FIRST + n + 1):
                    if n == 0 and t == 0:
                        transpose_values(i)
                    if t == 0:
                        if n:
                            attention.transpose_probs(pe, n - 1)
                        attention.scores(pe, n)
                    elif n:
                        if n == 1:
                            pe.wait_ge(vt_out, V_BODIES + 1)
                        attention.weigh_values(pe, n - 1)
            attention.transpose_probs(pe, n)
            attention.weigh_values(pe, n)
            attention.sum_squares(pe)
    operand.passed()
    passed(core, prod, scaled=True)


def branch_stage(core, prod, proj, y_parts, following):
    nc = core.nc
    gate_done, own, y_ready, y_high, x_back = (core.sem(f"branch_{s}") for s in ("gate_done", "own", "y_ready", "y_high", "x_back"))
    with ExitStack() as ctx:
        acc = core.ps(f"acc_{core.chunk}", [P, 2, 2, S], ctx)
        operand = Given(core, [proj[:, t, :] for t in (*range(DQ, DQ + 4), *range(FQ, FQ + 8))])
        free = core.h_mem[:, 12:16, :, :].rearrange("p k c s -> p (k c) s")
        z, gate = free[:, 0:4, :], free[:, 4:8, :]
        block = ctx.enter_context(nc.Block())

        @block.sync
        def _(sp):
            sp.dma_start(core.x[:, :, :], core.d["x_kept"]).then_inc(x_back, 16)
            stream(core, sp, prod, following)
            sp.wait_ge(x_back, 16)

        @block.scalar
        def _(act):
            def high(i, p):
                act.wait_ge(y_ready, 2 * i + (p + 1))
                nc.scalar.activation(y_parts[:, 2 * i + p, 0, :], proj[:, 2 * i + p, :], ACT.Copy).then_inc(y_high, 1)

            operand.act(act)
            nc.scalar.preload_act_table(ACT.Sigmoid)
            for i, t, previous in with_previous(core, act, prod, split_high, following):
                take_cross(core, act, prod, acc, i, t)
                g = proj[:, (G_DIFF if t % 2 else G_DIL) + t // 2 + 2 * i, :]
                nc.scalar.activation(gate[:, t, :], g, ACT.Sigmoid).then_inc(gate_done, 1)
                if previous and t % 2 == 0:
                    high(previous[0], previous[1] // 2)
            high(prod.bodies - 1, 1)

        @block.vector
        def _(dve):
            def low(i, p):
                dve.wait_ge(y_high, 2 * i + (p + 1))
                nc.vector.tensor_tensor(y_parts[:, 2 * i + p, 1, :], proj[:, 2 * i + p, :],
                                        y_parts[:, 2 * i + p, 0, :].bitcast(F32), ALU.subtract)

            operand.dve(dve)
            for i, t, previous in with_previous(core, dve, prod, split_low, following):
                take_tile(core, dve, prod, acc, z[:, t, :], i, t)
                taken(core, dve, prod, i, t)
                dve.wait_ge(gate_done, i * 4 + (t + 1))
                nc.vector.tensor_tensor(z[:, t, :], z[:, t, :], gate[:, t, :], ALU.mult).then_inc(own, 1)
                if t % 2:
                    dve.wait_ge(own, i * 4 + (t + 1))
                    nc.vector.tensor_tensor(proj[:, 2 * i + t // 2, :], z[:, t - 1, :], z[:, t, :],
                                            ALU.add).then_inc(y_ready, 1)
                elif previous:
                    low(previous[0], previous[1] // 2)
            low(prod.bodies - 1, 1)

        @block.tensor
        def _(pe):
            multiply_all(core, pe, prod, acc, operand.on(pe))
    passed(core, prod)



def weight_tiles(w):
    k, n = w.shape
    return np.ascontiguousarray(w.reshape(k // P, P, n // P, P).transpose(2, 1, 0, 3))


def by_partition(v):
    v = np.asarray(v)
    lead = int(np.prod(v.shape[:-1]))
    return v.reshape(lead, -1, P).transpose(2, 1, 0).reshape(P, -1)


def constants():
    t = np.arange(P)
    same = t[:, None] // CHUNK == t[None, :] // CHUNK
    parts = {
        "ident": np.eye(P), "ones": np.ones((P, P)),
        "causal64": same & (t[:, None] <= t[None, :]), "block64": same,
        "neg_strict64": -1.0 * (same & (t[:, None] < t[None, :])), "causal128": t[:, None] <= t[None, :],
        "inv_freq": (np.float32(ROPE_THETA) ** (-(2 * (t % (ROPE // 2))).astype(np.float32) / np.float32(ROPE)))[:, None],
        "rope_sign": np.where(t < ROPE // 2, -1.0, 1.0)[:, None],
    }
    return np.concatenate([np.asarray(parts[n], np.float32) for n in CONSTS], axis=1)


def attention_masks():
    q = (np.arange(HALVES)[None, :] * P + np.arange(P)[:, None])[:, :, None]
    dist = q - np.arange(S)[None, None, :]
    seen = [(dist >= 0) & (dist <= window) & (dist % dilation == 0) for window, dilation in DILATIONS] + [dist >= 0]
    return np.where(np.stack(seen, axis=2), 0.0, MASKED).astype(np.float32)



def whole(nc, d, out):
    def tiles_of(name, tile):
        def source(i, t, k0, nk):
            return d[name][tile(i, t)][:, k0:k0 + nk, :].rearrange("p a b -> p (a b)")
        return source

    def pair(i, t):
        return 2 * i + t

    with ExitStack() as ctx:
        core = Core(nc, ctx, d)
        stored = core.sem("stored")

        def proj_product(name, tiles, nk=KT, parts=None):
            return Product(tiles // 2, [nk, nk], tiles_of(name, pair), parts=parts)

        def up_product():
            return Product(FF_TILES, [KT, KT], tiles_of("ffn_up", lambda i, t: i + FF_TILES * t))

        def gate_up_product(n):
            def source(i, t, k0, nk):
                return d[f"ffn{n}_w_{('gate', 'up')[t]}_2"][i][:, k0:k0 + nk, :].rearrange("p a b -> p (a b)")
            return Product(FF_TILES, [KT, KT], source)

        def down_product(name, parts=None):
            return proj_product(name, KT, FF_TILES, parts)

        def branch_product():
            def source(i, t, k0, nk):
                name = ("w_dil_branch_2", "w_diff_branch_2")[t % 2]
                return d[name][2 * i + t // 2][:, k0:k0 + nk, :].rearrange("p a b -> p (a b)")
            return Product(KT // 2, [4, 8, 4, 8], source, first=[0, 4, 0, 4])

        def normed(*args, **kw):
            return lambda ctx: Normed(core, ctx, *args, **kw)

        g_parts = core.g_parts

        def swiglu(n, operand_of, following, next_gain=None):
            swiglu_up_stage(core, gate_up_product(n), operand_of, g_parts, down_product(f"ffn{n}_w_down_2"))
            product_add_stage(core, down_product(f"ffn{n}_w_down_2", g_parts), 0.5, following, next_gain)

        start_stage(core, proj_product("w_in", PROJ_TILES))

        with ExitStack() as c:
            arena = Region(core.arena[:, :, :].rearrange("p k s -> p (k s)"))
            proj = arena.take(PROJ_TILES, PAD + S)
            mix = {"conv": arena.take(16, S), "rows": arena.take(8 + 512),
                   "small": {n: core.sb(f"small_{n}", [P] + shape, F32, c)
                             for n, shape in (("g", [HEADS, HALVES]), ("beta", [HEADS, HALVES]), ("lru_c", [4]))}}
            mix["spare"] = arena.flat[:, arena.at:]
            normed_product_stage(core, proj_product("w_in", PROJ_TILES), "pre_mix",
                                 lambda i, t: proj[:, 2 * i + t, PAD:PAD + S], proj_product("w_out", KT),
                                 proj[:, :, 0:PAD])
            gdn_prepare_stage(core, proj, mix)
            gdn_stage(core, proj, mix)
            other_mixers_stage(core, proj, mix)
            plain_product_stage(core, proj_product("w_out", KT), [proj[:, at + j, PAD:PAD + S] for at in MIXED for j in range(4)],
                                lambda i, t: core.arena[:, 2 * i + t, :], up_product())

        conv_ffn_up_stage(core, up_product(), normed("pre_ffn", "residual", lambda k: core.arena[:, k, :], "post_mix"),
                          g_parts, down_product("ffn_down"))
        plain_product_stage(core, down_product("ffn_down", g_parts), [], lambda i, t: core.h_mem[:, 2 * i + t, 1, :],
                            gate_up_product(1))

        swiglu(1, normed("ffn1_norm", "residual", lambda k: core.h_mem[:, k, 1, :], "post_ffn"),
               proj_product("w_in_2", MIX_TILES), "mix_norm")
        with ExitStack() as c:
            proj = core.arena
            mix_in_stage(core, proj_product("w_in_2", MIX_TILES), normed("mix_norm", "prepared"), proj, core.trig, core.lam,
                         branch_product())
            y_parts = core.y_parts
            branch_stage(core, branch_product(), proj, y_parts, proj_product("w_out_2", KT))
            product_add_stage(core, proj_product("w_out_2", KT, parts=y_parts), 1.0, gate_up_product(2), "ffn2_norm")
        swiglu(2, normed("ffn2_norm", "prepared"), None)

        with nc.Block() as block:
            @block.sync
            def _(sp):
                sp.dma_start(out, core.x[:, :, :]).then_inc(stored, 16)
                sp.wait_ge(stored, 16)


def kernel(**inputs):
    import concourse.bacc as bacc
    from concourse.bass_utils import run_bass_kernel_spmd

    a = {k: np.asarray(v) for k, v in inputs.items()}
    gates = slice(4 * 512, 4 * 512 + 2 * HEADS)
    w_in = a["w_in"][0]
    arrays = {
        "x": a["x"][0].T.reshape(KT, P, S).transpose(1, 0, 2),
        "w_in": weight_tiles(np.delete(w_in, np.r_[gates], axis=1)),
        "w_ba": w_in[:, gates].reshape(KT, P, 2 * HEADS).transpose(1, 0, 2),
        "positions": a["positions_2"][0],
        "a_log": a["gdn_a_log"][0], "dt_bias": a["gdn_dt_bias"][0], "sgu_b": a["sgu_b"][0].reshape(-1),
        "lru_wa": a["lru_wa"][0], "lru_wx": a["lru_wx"][0], "sgu_ws": a["sgu_ws"][0].transpose(2, 0, 1),
        "consts": constants(), "masks": attention_masks(),
    }
    for name in ("w_out", "ffn_up", "ffn_down", "ffn1_w_gate_2", "ffn1_w_up_2", "ffn1_w_down_2", "w_in_2",
                 "w_dil_branch_2", "w_diff_branch_2", "w_out_2", "ffn2_w_gate_2", "ffn2_w_up_2", "ffn2_w_down_2"):
        arrays[name] = weight_tiles(a[name][0])
    arrays["w_in_2"] = arrays["w_in_2"][MIX_ORDER]
    vectors = {
        "pre_mix": a["pre_mix_norm"], "post_mix": a["post_mix_norm"], "pre_ffn": a["pre_ffn_norm"],
        "post_ffn": a["post_ffn_norm"], "ffn1_norm": a["ffn1_norm_2"], "mix_norm": a["mix_norm_2"],
        "ffn2_norm": a["ffn2_norm_2"], "gdn_conv": a["gdn_conv_w"][0], "gdn_norm": a["gdn_norm_w"],
        "lru_conv": a["lru_conv_w"][0], "lru_conv_b": a["lru_conv_b"], "lru_ba": a["lru_ba"].reshape(1, -1),
        "lru_bx": a["lru_bx"].reshape(1, -1), "lru_lambda": a["lru_lambda"], "ln_w": a["sgu_ln_w"], "ln_b": a["sgu_ln_b"],
        "sconv": a["sconv_w"][0], "grp": a["grp_norm_w"].reshape(1, -1), "ffn_conv": a["ffn_conv_w"][0],
        "ffn_conv_b": a["ffn_conv_b"], 
        "head_gain": np.concatenate([a[f"{n}_norm_2"] for n, pairs in (("dil_q", 6), ("dil_k", 6), ("diff_q", 4), ("diff_k", 4))
                                     for _ in range(pairs)]),
        "lam": np.concatenate([a["diff_lq1_2"], a["diff_lk1_2"], a["diff_lq2_2"], a["diff_lk2_2"]]),
        "subln": a["diff_subln_2"],
    }
    arrays["vectors"] = np.concatenate([by_partition(vectors[n]) for n in VECTORS], axis=1)

    nc = bacc.Bacc("TRN2", target_bir_lowering=False, num_devices=1)
    arrays = {f"in_{n}": np.ascontiguousarray(v) for n, v in arrays.items()}
    d = {n[3:]: nc.dram_tensor(n, v.shape, mybir.dt.from_np(v.dtype), kind="ExternalInput").ap()
         for n, v in arrays.items()}
    d["x_kept"] = nc.dram_tensor("x_kept", (P, KT, S), F32, kind="Internal").ap()
    out = nc.dram_tensor("out_x", (P, KT, S), F32, kind="ExternalOutput").ap()
    whole(nc, d, out)
    r = run_bass_kernel_spmd(nc, [arrays], core_ids=[0])
    got = r.results[0]["out_x"]
    return np.ascontiguousarray(got.transpose(2, 1, 0).reshape(1, S, DM))
```
